# Optimizing a Trainium2 kernel written in Bass

```python
import math
import jax, jax.numpy as jnp
from jax import lax
import numpy as np

D_MODEL = 1024
BATCH = 1
SEQ = 256
DEPTH = 2
DEC_BATCH = 1
DEC_SEQ = 32
PAST_LEN = 256

CHUNK = 64
Q_BLOCK = 128
A_HEADS = 8
A_KV_HEADS = 2
A_HEAD_DIM = 64
IDX_HEADS = 8
IDX_DIM = 64
TOPK_MAX = 256
B_HEADS = 4
B_KEY_DIM = 128
B_VAL_DIM = 128
CONV_WIDTH = 4
D_FF = 2816
N_EXPERTS = 8
TOP_K = 2
D_FF_EXPERT = 3584
LN_EPS = 1e-5
RMS_EPS = 1e-6
DEEPNORM_ALPHA = (2 * DEPTH) ** 0.25
DEEPNORM_BETA = (8 * DEPTH) ** -0.25

A_Q = A_HEADS * A_HEAD_DIM
A_KV = A_KV_HEADS * A_HEAD_DIM
B_QK = B_HEADS * B_KEY_DIM
B_V = B_HEADS * B_VAL_DIM
B_CONV_CH = 2 * B_QK + B_V
SPLIT_WIDTHS = (A_Q, A_KV, A_KV, IDX_HEADS * IDX_DIM, IDX_DIM, IDX_HEADS,
                B_CONV_CH, B_HEADS, B_HEADS, B_V, 2 * D_MODEL)
SPLIT_POINTS = tuple(int(s) for s in np.cumsum(SPLIT_WIDTHS)[:-1])
D_IN = int(sum(SPLIT_WIDTHS))
N_DENSE = (DEPTH + 1) // 2
N_MOE = DEPTH // 2
ALIBI_SLOPES = tuple(2.0 ** (-8.0 * (h + 1) / A_HEADS) for h in range(A_HEADS))

kernel_name = 'hybrid_dsa_gdn_streaming_step'

def layer_norm(x, g, b):
    xf = x.astype(jnp.float32)
    mu = jnp.mean(xf, axis=-1, keepdims=True)
    var = jnp.mean(jnp.square(xf - mu), axis=-1, keepdims=True)
    return ((xf - mu) * lax.rsqrt(var + LN_EPS) * g + b).astype(x.dtype)

def l2norm(x):
    xf = x.astype(jnp.float32)
    return xf * lax.rsqrt(jnp.sum(xf * xf, axis=-1, keepdims=True) + RMS_EPS)

def causal_conv(u, buf, w):
    T = u.shape[1]
    up = jnp.concatenate([buf.astype(u.dtype), u], axis=1)
    y = up[:, 0:T] * w[0]
    for j in range(1, CONV_WIDTH):
        y = y + up[:, j:j + T] * w[j]
    return jax.nn.silu(y), up[:, up.shape[1] - (CONV_WIDTH - 1):]

def dsa_attention(q, qi, wi, k, v, ik, q_start):
    bsz, T = q.shape[0], q.shape[1]
    S = k.shape[1]
    n_sel = min(TOPK_MAX, S // 4)
    qb_len = Q_BLOCK if T % Q_BLOCK == 0 else T
    nb = T // qb_len
    grp = A_HEADS // A_KV_HEADS
    slopes = jnp.asarray(ALIBI_SLOPES, jnp.float32).reshape(A_KV_HEADS, grp)
    k_pos = jnp.arange(S)
    q_pos = q_start + jnp.arange(T)

    def blocks(a):
        return jnp.moveaxis(a.reshape((bsz, nb, qb_len) + a.shape[2:]), 1, 0)

    def attend_block(xs):
        q_b, qi_b, wi_b, t_pos = xs
        idx = jnp.einsum('bqhd,bsd->bqhs', qi_b, ik).astype(jnp.float32)
        score = jnp.einsum('bqhs,bqh->bqs', jax.nn.relu(idx), wi_b.astype(jnp.float32)) * IDX_DIM ** -0.5
        admissible = (k_pos[None, :] // CHUNK) <= (t_pos[:, None] // CHUNK)
        score = jnp.where(admissible[None], score, -jnp.inf)
        top_val, top_idx = lax.top_k(score, n_sel)
        valid = jnp.isfinite(top_val)
        k_g = jax.vmap(lambda kk, ii: kk[ii])(k, top_idx)
        v_g = jax.vmap(lambda vv, ii: vv[ii])(v, top_idx)
        q_g = q_b.reshape(bsz, qb_len, A_KV_HEADS, grp, A_HEAD_DIM)
        logits = jnp.einsum('bqgrd,bqkgd->bqgrk', q_g, k_g).astype(jnp.float32) * A_HEAD_DIM ** -0.5
        dist = jnp.abs(t_pos[None, :, None] - top_idx).astype(jnp.float32)
        logits = logits - slopes[None, None, :, :, None] * dist[:, :, None, None, :]
        logits = jnp.where(valid[:, :, None, None, :], logits, -jnp.inf)
        p = jax.nn.softmax(logits, axis=-1).astype(v.dtype)
        o = jnp.einsum('bqgrk,bqkgd->bqgrd', p, v_g)
        return o.reshape(bsz, qb_len, A_Q)

    out = lax.map(attend_block, (blocks(q), blocks(qi), blocks(wi), q_pos.reshape(nb, qb_len)))
    return jnp.moveaxis(out, 0, 1).reshape(bsz, T, A_Q)

def gated_delta_rule(q, k, v, g, beta, s0):
    bsz, T, H, dk = q.shape
    dv = v.shape[-1]
    c = CHUNK if T % CHUNK == 0 else T
    n = T // c

    def to_chunks(a):
        a = a.reshape((bsz, n, c, H) + a.shape[3:])
        return a.transpose((1, 0, 3, 2) + tuple(range(4, a.ndim)))

    q = to_chunks(q * dk ** -0.5)
    k = to_chunks(k)
    v = to_chunks(v)
    g = to_chunks(g)
    beta = to_chunks(beta)
    G = jnp.cumsum(g, axis=-1)
    incl = jnp.tril(jnp.ones((c, c), dtype=bool))
    strict = jnp.tril(jnp.ones((c, c), dtype=bool), -1)
    diff = G[..., :, None] - G[..., None, :]
    decay = jnp.where(incl, jnp.exp(jnp.where(incl, diff, 0.0)), 0.0)
    k_beta = k * beta[..., None]
    m = jnp.where(strict, jnp.einsum('nbhik,nbhjk->nbhij', k_beta, k) * decay, 0.0)
    tri = m + jnp.eye(c, dtype=jnp.float32)
    rhs = jnp.concatenate([v * beta[..., None], k_beta * jnp.exp(G)[..., None]], axis=-1)
    sol = lax.linalg.triangular_solve(tri, rhs, left_side=True, lower=True, unit_diagonal=True)
    u, w = sol[..., :dv], sol[..., dv:]
    qk = jnp.where(incl, jnp.einsum('nbhik,nbhjk->nbhij', q, k) * decay, 0.0)
    q_dec = q * jnp.exp(G)[..., None]
    k_tail = k * jnp.exp(G[..., -1:] - G)[..., None]

    def step(s, xs):
        u_c, w_c, qk_c, qd_c, kt_c, gl_c = xs
        v_new = u_c - jnp.einsum('bhck,bhkv->bhcv', w_c, s)
        o = jnp.einsum('bhck,bhkv->bhcv', qd_c, s) + jnp.einsum('bhij,bhjv->bhiv', qk_c, v_new)
        s = s * jnp.exp(gl_c)[..., None, None] + jnp.einsum('bhck,bhcv->bhkv', kt_c, v_new)
        return s, o

    s_fin, o = lax.scan(step, s0, (u, w, qk, q_dec, k_tail, G[..., -1]))
    o = o.transpose(1, 0, 3, 2, 4).reshape(bsz, T, H, dv)
    return o, s_fin

def token_mixer(h, past_k, past_v, past_ik, conv_buf, s0, w_in, conv_w, a_log, dt_bias,
                gnorm_g, w_oa, w_ob, w_out):
    bsz, T, _ = h.shape
    P = past_k.shape[1]
    qa, ka, va, qi, ki, wi, qkv_b, a_b, b_b, z_b, gates = jnp.split(h @ w_in, SPLIT_POINTS, axis=-1)
    qa = qa.reshape(bsz, T, A_HEADS, A_HEAD_DIM)
    ka = ka.reshape(bsz, T, A_KV_HEADS, A_HEAD_DIM)
    va = va.reshape(bsz, T, A_KV_HEADS, A_HEAD_DIM)
    qi = qi.reshape(bsz, T, IDX_HEADS, IDX_DIM)
    k_all = jnp.concatenate([past_k.astype(ka.dtype), ka], axis=1)
    v_all = jnp.concatenate([past_v.astype(va.dtype), va], axis=1)
    ik_all = jnp.concatenate([past_ik.astype(ki.dtype), ki], axis=1)
    o_a = dsa_attention(qa, qi, wi, k_all, v_all, ik_all, P)
    c, conv_new = causal_conv(qkv_b, conv_buf, conv_w)
    qb, kb, vb = jnp.split(c, (B_QK, 2 * B_QK), axis=-1)
    qb = l2norm(qb.reshape(bsz, T, B_HEADS, B_KEY_DIM))
    kb = l2norm(kb.reshape(bsz, T, B_HEADS, B_KEY_DIM))
    vb = vb.reshape(bsz, T, B_HEADS, B_VAL_DIM).astype(jnp.float32)
    g = -jnp.exp(a_log.astype(jnp.float32)) * jax.nn.softplus(a_b.astype(jnp.float32) + dt_bias.astype(jnp.float32))
    beta = jax.nn.sigmoid(b_b.astype(jnp.float32))
    o_b, s_new = gated_delta_rule(qb, kb, vb, g, beta, s0.astype(jnp.float32))
    o_b = o_b * lax.rsqrt(jnp.mean(o_b * o_b, axis=-1, keepdims=True) + RMS_EPS) * gnorm_g.astype(jnp.float32)
    o_b = o_b * jax.nn.silu(z_b.astype(jnp.float32).reshape(bsz, T, B_HEADS, B_VAL_DIM))
    o_b = o_b.reshape(bsz, T, B_V).astype(h.dtype)
    g_a, g_b = jnp.split(jax.nn.sigmoid(gates), 2, axis=-1)
    y = (g_a * (o_a @ w_oa) + g_b * (o_b @ w_ob)) @ w_out
    return y, ka, va, ki, conv_new, s_new

def swiglu(h, w1, w3, w2):
    return (jax.nn.silu(h @ w1) * (h @ w3)) @ w2

def moe_ffn(h, router, w1, w3, w2):
    logits = (h @ router).astype(jnp.float32)
    top_val, top_idx = lax.top_k(logits, TOP_K)
    top_w = jax.nn.softmax(top_val, axis=-1)
    gate = jnp.sum(jax.nn.one_hot(top_idx, N_EXPERTS, dtype=jnp.float32) * top_w[..., None], axis=-2)
    out = gate[..., 0:1].astype(h.dtype) * swiglu(h, w1[0], w3[0], w2[0])
    for e in range(1, N_EXPERTS):
        out = out + gate[..., e:e + 1].astype(h.dtype) * swiglu(h, w1[e], w3[e], w2[e])
    return out

def trunk(x, past_k, past_v, past_ik, conv0, s0, weights):
    (ln_in_g, ln_in_b, w_in, conv_w, a_log, dt_bias, gnorm_g, w_oa, w_ob, w_out,
     ln1_g, ln1_b, ln2_g, ln2_b, ffn_w1, ffn_w3, ffn_w2, moe_router, moe_w1, moe_w3, moe_w2) = weights
    h = layer_norm(x, ln_in_g, ln_in_b)
    ks, vs, iks, convs, ss = [], [], [], [], []
    for l in range(DEPTH):
        y, k_new, v_new, ik_new, conv_new, s_new = token_mixer(
            h, past_k[l], past_v[l], past_ik[l], conv0[l], s0[l], w_in[l], conv_w[l], a_log[l],
            dt_bias[l], gnorm_g[l], w_oa[l], w_ob[l], w_out[l])
        h = layer_norm(DEEPNORM_ALPHA * h + y, ln1_g[l], ln1_b[l])
        if l % 2 == 0:
            f = swiglu(h, ffn_w1[l // 2], ffn_w3[l // 2], ffn_w2[l // 2])
        else:
            f = moe_ffn(h, moe_router[l // 2], moe_w1[l // 2], moe_w3[l // 2], moe_w2[l // 2])
        h = layer_norm(DEEPNORM_ALPHA * h + f, ln2_g[l], ln2_b[l])
        ks.append(k_new)
        vs.append(v_new)
        iks.append(ik_new)
        convs.append(conv_new)
        ss.append(s_new)
    return h, jnp.stack(ks), jnp.stack(vs), jnp.stack(iks), jnp.stack(convs), jnp.stack(ss)

def setup_inputs(seed: int = 0) -> dict:
    key = jax.random.key(seed)
    ks = jax.random.split(key, 32)
    f32 = jnp.float32
    nrm = lambda k, shape, s: jax.random.normal(k, shape, f32) * s
    dt = jnp.exp(jax.random.uniform(ks[10], (DEPTH, B_HEADS), f32) * (math.log(0.1) - math.log(0.001)) + math.log(0.001))
    return {
        'x_prompt': nrm(ks[0], (BATCH, SEQ, D_MODEL), 1.0),
        'x_sample': nrm(ks[1], (DEC_BATCH, DEC_SEQ, D_MODEL), 1.0),
        'cache_k': nrm(ks[2], (DEPTH, DEC_BATCH, PAST_LEN, A_KV_HEADS, A_HEAD_DIM), 1.0),
        'cache_v': nrm(ks[3], (DEPTH, DEC_BATCH, PAST_LEN, A_KV_HEADS, A_HEAD_DIM), 1.0),
        'cache_idx_k': nrm(ks[4], (DEPTH, DEC_BATCH, PAST_LEN, IDX_DIM), 1.0),
        'state_conv': nrm(ks[5], (DEPTH, DEC_BATCH, CONV_WIDTH - 1, B_CONV_CH), 1.0),
        'state_gdn': nrm(ks[6], (DEPTH, DEC_BATCH, B_HEADS, B_KEY_DIM, B_VAL_DIM), 0.1),
        'ln_in_g': 1.0 + nrm(ks[7], (D_MODEL,), 0.02),
        'ln_in_b': nrm(ks[8], (D_MODEL,), 0.02),
        'w_in': nrm(ks[9], (DEPTH, D_MODEL, D_IN), D_MODEL ** -0.5),
        'conv_w': nrm(ks[11], (DEPTH, CONV_WIDTH, B_CONV_CH), CONV_WIDTH ** -0.5),
        'a_log': jnp.log(jax.random.uniform(ks[12], (DEPTH, B_HEADS), f32, 1.0, 16.0)),
        'dt_bias': dt + jnp.log(-jnp.expm1(-dt)),
        'gnorm_g': 1.0 + nrm(ks[13], (DEPTH, B_VAL_DIM), 0.02),
        'w_oa': nrm(ks[14], (DEPTH, A_Q, D_MODEL), A_Q ** -0.5 * DEEPNORM_BETA),
        'w_ob': nrm(ks[15], (DEPTH, B_V, D_MODEL), B_V ** -0.5 * DEEPNORM_BETA),
        'w_out': nrm(ks[16], (DEPTH, D_MODEL, D_MODEL), D_MODEL ** -0.5 * DEEPNORM_BETA),
        'ln1_g': 1.0 + nrm(ks[17], (DEPTH, D_MODEL), 0.02),
        'ln1_b': nrm(ks[18], (DEPTH, D_MODEL), 0.02),
        'ln2_g': 1.0 + nrm(ks[19], (DEPTH, D_MODEL), 0.02),
        'ln2_b': nrm(ks[20], (DEPTH, D_MODEL), 0.02),
        'ffn_w1': nrm(ks[21], (N_DENSE, D_MODEL, D_FF), D_MODEL ** -0.5),
        'ffn_w3': nrm(ks[22], (N_DENSE, D_MODEL, D_FF), D_MODEL ** -0.5),
        'ffn_w2': nrm(ks[23], (N_DENSE, D_FF, D_MODEL), D_FF ** -0.5 * DEEPNORM_BETA),
        'moe_router': nrm(ks[24], (N_MOE, D_MODEL, N_EXPERTS), D_MODEL ** -0.5),
        'moe_w1': nrm(ks[25], (N_MOE, N_EXPERTS, D_MODEL, D_FF_EXPERT), D_MODEL ** -0.5),
        'moe_w3': nrm(ks[26], (N_MOE, N_EXPERTS, D_MODEL, D_FF_EXPERT), D_MODEL ** -0.5),
        'moe_w2': nrm(ks[27], (N_MOE, N_EXPERTS, D_FF_EXPERT, D_MODEL), D_FF_EXPERT ** -0.5 * DEEPNORM_BETA),
    }

def reference(x_prompt, x_sample, cache_k, cache_v, cache_idx_k, state_conv, state_gdn,
              ln_in_g, ln_in_b, w_in, conv_w, a_log, dt_bias, gnorm_g, w_oa, w_ob, w_out,
              ln1_g, ln1_b, ln2_g, ln2_b, ffn_w1, ffn_w3, ffn_w2,
              moe_router, moe_w1, moe_w3, moe_w2):
    weights = (ln_in_g, ln_in_b, w_in, conv_w, a_log, dt_bias, gnorm_g, w_oa, w_ob, w_out,
               ln1_g, ln1_b, ln2_g, ln2_b, ffn_w1, ffn_w3, ffn_w2, moe_router, moe_w1, moe_w3, moe_w2)
    bp = x_prompt.shape[0]
    empty_kv = jnp.zeros((DEPTH, bp, 0, A_KV_HEADS, A_HEAD_DIM), x_prompt.dtype)
    empty_ik = jnp.zeros((DEPTH, bp, 0, IDX_DIM), x_prompt.dtype)
    conv0 = jnp.zeros((DEPTH, bp, CONV_WIDTH - 1, B_CONV_CH), x_prompt.dtype)
    s0 = jnp.zeros((DEPTH, bp, B_HEADS, B_KEY_DIM, B_VAL_DIM), jnp.float32)
    y_prompt, pk, pv, pik, pconv, ps = trunk(x_prompt, empty_kv, empty_kv, empty_ik, conv0, s0, weights)
    y_sample, sk, sv, sik, sconv, ss = trunk(x_sample, cache_k, cache_v, cache_idx_k, state_conv, state_gdn, weights)
    return (y_prompt, y_sample, pk, pv, pik, pconv, ps, sk, sv, sik, sconv, ss)


_drawn_inputs = setup_inputs


def setup_inputs(seed=0):
    import zlib

    import numpy as np

    out = dict(_drawn_inputs(seed))
    spreads = {}
    factors = {'gnorm_g': 22.721, 'cache_k': 4.257, 'cache_idx_k': 2.914}
    for name, (base, spread) in spreads.items():
        noise = np.random.default_rng([zlib.crc32(name.encode()), seed]).standard_normal(out[name].shape)
        drawn = base * np.exp(spread * noise) if base else spread * noise
        out[name] = __import__('jax').numpy.asarray(drawn.astype(out[name].dtype))
    for name, factor in factors.items():
        out[name] = (out[name] * factor).astype(out[name].dtype)
    return out
```

```python
from contextlib import ExitStack

import concourse.bass as bass
from concourse import mybir

F32 = mybir.dt.float32
I32 = mybir.dt.int32
U32 = mybir.dt.uint32
ALU = mybir.AluOpType
ACT = mybir.ActivationFunctionType
AX = mybir.AxisListType

P = 128
D = 1024
KD = D // P
SEQ, DEC, PAST = 256, 32, 256
T = SEQ + DEC
TILES = [(0, 128), (128, 128), (256, DEC)]
NT = len(TILES)
DEPTH = 2
CHUNK = 64
A_HEADS, A_KV, HD = 8, 2, 64
IH = 8
B_HEADS, BD = 4, 128
CW = 4
CCH = 3 * B_HEADS * BD
CT = CCH // P
D_FF, D_FFE, NE = 2816, 3584, 8
ALPHA = (2 * DEPTH) ** 0.25
LN_EPS, RMS_EPS = 1e-5, 1e-6

O_QA = 0
O_KA = O_QA + A_HEADS * HD
O_VA = O_KA + A_KV * HD
O_QI = O_VA + A_KV * HD
O_KI = O_QI + IH * HD
O_WI = O_KI + HD
O_CV = O_WI + IH
O_AB = O_CV + CCH
O_Z = O_AB + 2 * B_HEADS
O_GA = O_Z + B_HEADS * BD
O_GB = O_GA + D

K_CACHE = SEQ
K_SMP = SEQ + PAST
NK = SEQ + PAST + DEC
KEYS = [(0, SEQ), (0, SEQ), (K_CACHE, PAST + DEC)]
NSEL = [min(256, s // 4) for _, s in KEYS]
VT = [[0, 1], [0, 1], [2, 3, 4]]
CI = (CW - 1) + SEQ + (CW - 1) + DEC
CO = CI - (CW - 1)
C_SMP = SEQ + CW - 1
CCOL = [0, 128, C_SMP]
NEG = -3.0e38
TAKEN = -3.4e38

RING, SLOT = 7, 2048
CAP = 128
ROUNDS = -(-T // CAP)


def program(nc, A, OUT, upto=99):
    ctx = ExitStack()
    with ctx:
        def sb(name, shape, dt=F32):
            return ctx.enter_context(nc.sbuf_tensor(name, shape, dt))

        def sem(name):
            return ctx.enter_context(nc.semaphore(name))

        ps = [ctx.enter_context(nc.psum_tensor(f"ps{b}", [P, 512], F32)) for b in range(8)]

        ring = sb("ring", [P, RING * SLOT])
        resid = sb("resid", [P, NT, D])
        hT = sb("hT", [P, KD, T])
        lnp = sb("lnp", [P, 10, KD])
        stats = sb("stats", [P, NT, 2, 6])
        mv = sb("mv", [P, NT, 2])
        std = sb("std", [P, NT])
        rstd = sb("rstd", [P, NT])
        ident = sb("ident", [P, P])
        ones = sb("ones", [P, P])
        cumU = sb("cumU", [P, P])
        blk = sb("blk", [P, P])
        d16 = sb("d16", [P, P])
        off16 = sb("off16", [P, P])
        negL = sb("negL", [P, P])
        negU = sb("negU", [P, P])
        before = sb("before", [P, P])
        iota = sb("iota", [P, CAP])
        itmp = sb("itmp", [P, 320], I32)
        adm = sb("adm", [P, 2, SEQ])
        ndist = sb("ndist", [P, NT, PAST + DEC])
        cT = sb("cT", [P, CT, CO])
        zT = sb("zT", [P, B_HEADS, T])
        oaT = sb("oaT", [P, 4, T])
        obT = sb("obT", [P, 4, T])
        wsm = sb("wsm", [P, NT, 16])
        gates = sb("gates", [P, 4, 2, B_HEADS])
        ARENA = (nc.sbuf_usable_end - nc.sbuf_base) // 4 - 64
        ARENA = min(ARENA, 20000)
        arena = sb("arena", [P, ARENA])

        class Area:
            def __init__(self):
                self.at = 0

            def __call__(self, *dims):
                n = 1
                for d in dims:
                    n *= d
                v = arena[:, self.at:self.at + n]
                self.at += n
                assert self.at <= ARENA, (self.at, ARENA)
                if len(dims) == 2:
                    v = v.rearrange("p (a b) -> p a b", a=dims[0])
                if len(dims) == 3:
                    v = v.rearrange("p (a b c) -> p a b c", a=dims[0], b=dims[1])
                return v

        ar = Area()
        qaT = ar(4, T)
        kT = ar(NK)
        kiT = ar(NK)
        qiT = ar(4, T)
        vtok = ar(5, A_KV * HD)
        ATT0 = ar.at
        cin = ar(CT, CI)
        vT = ar(T)
        ktok = ar(2, A_KV * HD)
        kitok = ar(2, 2 * HD)
        crow = ar(CCH)
        cw = ar(CT, 8)
        last = ar(CT, 6)
        lrow = ar(CCH)
        knew = ar(NT, A_KV * HD)
        inew = ar(NT, HD)

        units = []

        def slot(n, dims):
            s = (n % RING) * SLOT
            size = 1
            for d in dims:
                size *= d
            v = ring[:, s:s + size]
            return v.rearrange("p (a b) -> p a b", a=dims[0])

        def unit(*loads):
            n = len(units)
            units.append(loads)
            return n

        def rows(w):
            return w.rearrange("(k p) n -> p k n", p=P)

        def project_units(l):
            w = rows(A["w_in"][l])
            n0 = len(units)
            for k in (0, 4):
                v = slot(len(units), (4, 512)).rearrange("p k (c a x) -> p k c a x", a=2, x=HD)
                unit(*[(v[:, q, :, a, :], w[:, k + q, O_QA + 256 * a:O_QA + 256 * a + 256]
                        .rearrange("p (c x) -> p c x", x=HD)) for q in range(4) for a in range(2)])
            n = len(units)
            unit((slot(n, (8, 256)), w[:, :, O_KA:O_KA + 256]))
            for k in (0, 4):
                n = len(units)
                unit((slot(n, (4, 512)), w[:, k:k + 4, O_QI:O_QI + 512]))
            n = len(units)
            v = slot(n, (8, 80))
            unit((v[:, :, 0:72], w[:, :, O_KI:O_KI + 72]), (v[:, :, 72:80], w[:, :, O_AB:O_AB + 8]))
            for j in range(6):
                n = len(units)
                unit((slot(n, (8, 256)), w[:, :, O_CV + 256 * j:O_CV + 256 * j + 256]))
            for j in range(2):
                n = len(units)
                unit((slot(n, (8, 256)), w[:, :, O_Z + 256 * j:O_Z + 256 * j + 256]))
            assert n0 % RING < RING - 1 and (n0 + 3) % RING < RING - 1
            return n0

        def merge_units(l):
            w, oa, ob, wo = rows(A["w_in"][l]), rows(A["w_oa"][l]), rows(A["w_ob"][l]), rows(A["w_out"][l])
            n0 = len(units)
            for j in range(4):
                c = 256 * j
                n = len(units)
                unit((slot(n, (8, 256)), w[:, :, O_GA + c:O_GA + c + 256]))
                n = len(units)
                unit((slot(n, (8, 256)), w[:, :, O_GB + c:O_GB + c + 256]))
                n = len(units)
                v = slot(n, (8, 256))
                unit((v[:, 0:4, :], oa[:, :, c:c + 256]), (v[:, 4:8, :], ob[:, :, c:c + 256]))
            for j in range(4):
                n = len(units)
                unit((slot(n, (8, 256)), wo[:, :, 256 * j:256 * j + 256]))
            return n0

        def mlp_loads(n0, j, w1, w3, w2, ff):
            pairs = ff // 256
            if j < 2 * pairs:
                w = (w1, w3)[j % 2]
                c = 256 * (j // 2)
                return slot(n0 + j, (8, 256)), w.rearrange("(k p) n -> p k n", p=P)[:, :, c:c + 256]
            r = 256 * (j - 2 * pairs)
            return slot(n0 + j, (2, D)), w2[r:r + 256, :].rearrange("(k p) n -> p k n", p=P)

        N_PROJ, N_MERGE, N_FFN, N_EXP = 14, 16, 3 * D_FF // 256, 3 * D_FFE // 256
        first = {}
        for l in range(DEPTH):
            first["project", l] = project_units(l)
            first["merge", l] = merge_units(l)
            if l == 0:
                first["mlp", l] = len(units)
                for j in range(N_FFN):
                    unit(mlp_loads(first["mlp", 0], j, A["ffn_w1"][0], A["ffn_w3"][0], A["ffn_w2"][0], D_FF))
        moe0 = first["moe"] = len(units)
        for j in range(N_EXP):
            unit(mlp_loads(moe0, j, A["moe_w1"][0, 0], A["moe_w3"][0, 0], A["moe_w2"][0, 0], D_FFE))
        assert N_EXP % RING == 0

        slot_full = [sem(f"slot_full{s}") for s in range(RING)]
        unit_used = sem("unit_used")
        full_at = []
        count = [0] * RING
        for n, loads in enumerate(units):
            count[n % RING] += 16 * len(loads)
            full_at.append(count[n % RING])
        PER_EXPERT = 16 * N_EXP // RING

        loaded = [0]

        def load_units(sp, used):
            hi = min(used + RING, len(units))
            lo, loaded[0] = loaded[0], hi
            for n in range(lo, hi):
                if n >= RING:
                    sp.wait_ge(unit_used, n - RING + 1)
                for dst, src in units[n]:
                    sp.dma_start(dst, src).then_inc(slot_full[n % RING], 16)

        def have(pe, n, experts=0):
            pe.wait_ge(slot_full[n % RING], experts * PER_EXPERT + full_at[n])

        class Release:
            def __init__(self):
                self.due = False

            def mm(self, *a, **k):
                ins = nc.tensor.matmul(*a, **k)
                if self.due:
                    ins.then_inc(unit_used, 1)
                    self.due = False
                return ins
        rel = Release()

        class Chain:
            def __init__(self, eng, s):
                self.eng, self.s, self.n, self.base = eng, s, 0, 0

            def __call__(self, ins):
                ins.then_inc(self.s, 1)
                self.n += 1

            def sync(self):
                self.eng.wait_ge(self.s, self.base + self.n)

            def link(self, ins):
                self(ins)
                self.sync()

        dve_step, act_step, pool_step = sem("dve_step"), sem("act_step"), sem("pool_step")
        steps = {"dve": 0, "act": 0, "pool": 0}

        def chain(eng, which):
            c = Chain(eng, {"dve": dve_step, "act": act_step, "pool": pool_step}[which])
            c.n = steps[which]
            return c

        def keep(c, which):
            steps[which] = c.n

        x_in, ln_in = sem("x_in"), sem("ln_in")
        const_ready, ln_turned = sem("const_ready"), sem("ln_turned")
        lnrow = arena[0:80, 0:P]
        with nc.Block() as block:
            @block.sync
            def _(sp):
                sp.dma_start(resid[:, 0:2, :], A["x_prompt"][0].rearrange("(i p) d -> p i d", p=P)).then_inc(x_in, 16)
                sp.dma_start(resid[0:DEC, 2, :], A["x_sample"][0]).then_inc(x_in, 16)
                vec = [A["ln_in_g"], A["ln_in_b"]]
                for l in range(DEPTH):
                    vec += [A["ln1_g"][l], A["ln1_b"][l], A["ln2_g"][l], A["ln2_b"][l]]
                for j, v in enumerate(vec):
                    sp.dma_start(arena[KD * j:KD * j + KD, 0:P], v.rearrange("(k p) -> k p", p=P)).then_inc(ln_in, 16)
                load_units(sp, 0)

            @block.gpsimd
            def _(pool):
                c = chain(pool, "pool")
                c.link(nc.gpsimd.memset(ident[:], 0.0))
                c.link(nc.gpsimd.memset(ones[:], 1.0))
                c.link(nc.gpsimd.memset(cumU[:], 0.0))
                c.link(nc.gpsimd.memset(blk[:], 0.0))
                c.link(nc.gpsimd.memset(negL[:], 0.0))
                c.link(nc.gpsimd.memset(negU[:], 0.0))
                c.link(nc.gpsimd.memset(before[:], 1.0))
                c.link(nc.gpsimd.memset(adm[:], 0.0))
                c.link(nc.gpsimd.memset(d16[:], 0.0))
                c.link(nc.gpsimd.memset(mv[:], 1.0))
                c.link(nc.gpsimd.memset(wsm[:], 0.0))
                c.sync()
                for a in range(0, P, CHUNK):
                    s = slice(a, a + CHUNK)
                    c.link(nc.gpsimd.memset(cumU[s, s], 1.0))
                    c.link(nc.gpsimd.memset(blk[s, s], 1.0))
                for i in range(2):
                    for half in range(2):
                        k0 = (2 * i + half + 1) * CHUNK
                        if k0 < SEQ:
                            c.link(nc.gpsimd.memset(adm[half * CHUNK:half * CHUNK + CHUNK, i, k0:SEQ], NEG))
                c.link(nc.gpsimd.affine_select(out=ident[:], in_=ident[:], compare_op=ALU.not_equal, fill=1.0, base=0,
                                          pattern=[[-1, P]], channel_multiplier=1))
                c.link(nc.gpsimd.affine_select(out=before[:], in_=before[:], compare_op=ALU.is_gt, fill=0.0, base=0,
                                          pattern=[[1, P]], channel_multiplier=-1))
                c.sync()
                c.link(nc.gpsimd.memset(d16[:], 1.0))
                d16v = d16[:].rearrange("p (b c) -> p b c", c=16)
                c.link(nc.gpsimd.affine_select(out=d16v, in_=d16v, compare_op=ALU.is_ge, fill=0.0, base=0,
                                               pattern=[[-16, 8], [0, 16]], channel_multiplier=1))
                c.link(nc.gpsimd.affine_select(out=d16v, in_=d16v, compare_op=ALU.is_ge, fill=0.0, base=15,
                                               pattern=[[16, 8], [0, 16]], channel_multiplier=-1))
                c.link(nc.gpsimd.affine_select(out=d16[:], in_=d16[:], compare_op=ALU.is_gt, fill=0.0, base=0,
                                               pattern=[[-1, P]], channel_multiplier=1))
                c.link(nc.gpsimd.affine_select(out=cumU[:], in_=cumU[:], compare_op=ALU.is_ge, fill=0.0, base=0,
                                               pattern=[[1, P]], channel_multiplier=-1))
                c.link(nc.gpsimd.affine_select(out=off16[:], in_=blk[:], compare_op=ALU.is_gt, fill=0.0, base=0,
                                               pattern=[[-1, P]], channel_multiplier=1))
                c.link(nc.gpsimd.tensor_tensor(off16[:], off16[:], d16[:], ALU.subtract))
                c.link(nc.gpsimd.affine_select(out=negL[:], in_=blk[:], compare_op=ALU.is_ge, fill=0.0, base=0,
                                               pattern=[[-1, P]], channel_multiplier=1))
                c.link(nc.gpsimd.tensor_scalar(negL[:], negL[:], 1.0, 1e30, ALU.subtract, ALU.mult))
                c.link(nc.gpsimd.tensor_scalar(negU[:], cumU[:], 1.0, 1e30, ALU.subtract, ALU.mult))
                c.link(nc.gpsimd.iota(itmp[:, 0:CAP], pattern=[[1, CAP]], base=0, channel_multiplier=0))
                c.link(nc.gpsimd.tensor_copy(iota[:], itmp[:, 0:CAP]))
                for i in range(NT):
                    c.link(nc.gpsimd.iota(itmp[:, 0:PAST + DEC], pattern=[[1, PAST + DEC]], base=-TILES[i][0],
                                          channel_multiplier=-1))
                    c.link(nc.gpsimd.tensor_copy(ndist[:, i, :], itmp[:, 0:PAST + DEC]))
                nc.gpsimd.memset(std[:], 1.0).then_inc(const_ready, 1)
                keep(c, "pool")

            @block.tensor
            def _(pe):
                pe.wait_ge(const_ready, 1)
                pe.wait_ge(ln_in, 160)
                nc.tensor.transpose(ps[0][:, 0:80], lnrow, ident[0:80, 0:80]).then_inc(ln_turned, 1)

            @block.vector
            def _(dve):
                dve.wait_ge(ln_turned, 1)
                dve.wait_ge(x_in, 32)
                c = chain(dve, "dve")
                c.link(nc.vector.scalar_tensor_tensor(out=ndist[:], in0=ndist[:], scalar=-1.0, in1=ndist[:],
                                                      op0=ALU.mult, op1=ALU.min))
                c.link(nc.vector.tensor_copy(lnp[:], ps[0][:, 0:80].rearrange("p (j k) -> p j k", k=KD)))
                keep(c, "dve")

        gb_in = sem("gb_in")
        var_ready, std_ready, hat_ready = sem("var_ready"), sem("std_ready"), sem("hat_ready")
        nrm_turned, nrm_evac, pool_h, out_stored = sem("nrm_turned"), sem("nrm_evac"), sem("pool_h"), sem("out_stored")

        def norm(call, j, g_vec, b_vec, keep_h=None, final=False):
            gb = arena[:, ARENA - 2 * D:ARENA].rearrange("p (a b) -> p a b", a=2)
            with nc.Block() as block:
                @block.sync
                def _(sp):
                    sp.dma_start(gb[:, 0, :], g_vec.partition_broadcast(P)).then_inc(gb_in, 16)
                    sp.dma_start(gb[:, 1, :], b_vec.partition_broadcast(P)).then_inc(gb_in, 16)
                    if final:
                        sp.wait_ge(pool_h, NT * (call + 1))
                        sp.dma_start(OUT["y_prompt"][0].rearrange("(i p) d -> p i d", p=P), resid[:, 0:2, :]).then_inc(out_stored, 16)
                        sp.dma_start(OUT["y_sample"][0], resid[0:DEC, 2, :]).then_inc(out_stored, 16)
                        sp.wait_ge(out_stored, 32)

                @block.vector
                def _(dve):
                    c = chain(dve, "dve")
                    for i, (t0, n) in enumerate(TILES):
                        for a in range(2):
                            c(nc.vector.bn_stats(stats[0:n, i, a, :], resid[0:n, i, 512 * a:512 * a + 512]))
                    for i, (t0, n) in enumerate(TILES):
                        c.sync() if i == 0 else None
                        c(nc.vector.bn_aggr(mv[0:n, i, :], stats[0:n, i, :, :].rearrange("p a b -> p (a b)")))
                    c.sync()
                    nc.vector.tensor_scalar(rstd[:], mv[:, :, 1], LN_EPS, None, ALU.add).then_inc(var_ready, 1)
                    dve.wait_ge(std_ready, call + 1)
                    c.link(nc.vector.reciprocal(rstd[:], std[:]))
                    for i, (t0, n) in enumerate(TILES):
                        nc.vector.tensor_scalar(resid[0:n, i, :], resid[0:n, i, :], mv[0:n, i, 0:1], rstd[0:n, i:i + 1],
                                                ALU.subtract, ALU.mult).then_inc(hat_ready, 1)
                    keep(c, "dve")

                @block.scalar
                def _(act):
                    act.wait_ge(var_ready, call + 1)
                    nc.scalar.activation(std[:], rstd[:], ACT.Sqrt).then_inc(std_ready, 1)
                    if final:
                        return
                    for i, (t0, n) in enumerate(TILES):
                        for k in range(KD):
                            act.wait_ge(nrm_turned, KD * NT * call + KD * i + k + 1)
                            nc.scalar.activation(hT[:, k, t0:t0 + n], ps[k][:, 128 * i:128 * i + n], ACT.Identity,
                                                 bias=lnp[:, 2 * j + 1, k:k + 1], scale=lnp[:, 2 * j, k:k + 1]
                                                 ).then_inc(nrm_evac, 1)

                @block.tensor
                def _(pe):
                    if final:
                        return
                    for i, (t0, n) in enumerate(TILES):
                        pe.wait_ge(hat_ready, NT * call + i + 1)
                        for k in range(KD):
                            if i:
                                pe.wait_ge(nrm_evac, KD * NT * call + KD * (i - 1) + k + 1)
                            nc.tensor.transpose(ps[k][:, 128 * i:128 * i + n], resid[0:n, i, 128 * k:128 * k + 128],
                                                ident[0:n, 0:n]).then_inc(nrm_turned, 1)

                @block.gpsimd
                def _(pool):
                    c = chain(pool, "pool")
                    pool.wait_ge(gb_in, 32 * (call + 1))
                    for i, (t0, n) in enumerate(TILES):
                        pool.wait_ge(hat_ready, NT * call + i + 1)
                        if not final:
                            pool.wait_ge(nrm_turned, KD * NT * call + KD * (i + 1))
                        r = resid[0:n, i, :]
                        c.link(nc.gpsimd.tensor_tensor(r, r, gb[0:n, 0, :], ALU.mult))
                        h = keep_h[0:n, i, :] if keep_h is not None else r
                        if final:
                            nc.gpsimd.tensor_tensor(h, r, gb[0:n, 1, :], ALU.add).then_inc(pool_h, 1)
                            continue
                        c.link(nc.gpsimd.tensor_tensor(h, r, gb[0:n, 1, :], ALU.add))
                        nc.gpsimd.tensor_scalar(r, h, ALPHA, None, ALU.mult).then_inc(pool_h, 1)
                    keep(c, "pool")

        mix_in, pre_turned, pre_evac = sem("mix_in"), sem("pre_turned"), sem("pre_evac")
        pj_done, pj_evac, conv_ready, silu_ready = sem("pj_done"), sem("pj_evac"), sem("conv_ready"), sem("silu_ready")
        post_turned, post_evac, new_stored, last_ready = sem("post_turned"), sem("post_evac"), sem("new_stored"), sem("last_ready")
        N_CH = 28

        def project(l):
            u0 = first["project", l]
            with nc.Block() as block:
                @block.sync
                def _(sp):
                    load_units(sp, u0 + N_PROJ - 1)
                    sp.wait_ge(post_evac, 6 * (l + 1))
                    for name, src, w in (("k", knew, 2 * HD), ("v", None, 2 * HD), ("idx_k", inew, HD)):
                        op, os = OUT[f"new_{name}_p"][l, 0], OUT[f"new_{name}_s"][l, 0]
                        if name != "idx_k":
                            op, os = op.rearrange("t g d -> t (g d)"), os.rearrange("t g d -> t (g d)")
                        main = vtok[:, 0:2, :] if src is None else src[:, 0:2, :]
                        tail = vtok[0:DEC, 4, :] if src is None else src[0:DEC, 2, :]
                        sp.dma_start(op.rearrange("(i p) c -> p i c", p=P), main).then_inc(new_stored, 16)
                        sp.dma_start(os, tail).then_inc(new_stored, 16)
                    sp.dma_start(OUT["new_conv_p"][l, 0], lrow[0:3, :]).then_inc(new_stored, 16)
                    sp.dma_start(OUT["new_conv_s"][l, 0], lrow[3:6, :]).then_inc(new_stored, 16)
                    sp.wait_ge(new_stored, 160 * l + 128)

                @block.scalar
                def _(act):
                    act.dma_start(crow[0:CW, :], A["conv_w"][l]).then_inc(mix_in, 16)
                    act.dma_start(crow[CW:CW + 3, :], A["state_conv"][l, 0]).then_inc(mix_in, 16)
                    act.dma_start(ktok, A["cache_k"][l, 0].rearrange("(i p) g d -> p i (g d)", p=P)).then_inc(mix_in, 16)
                    act.dma_start(vtok[:, 2:4, :], A["cache_v"][l, 0].rearrange("(i p) g d -> p i (g d)", p=P)).then_inc(mix_in, 16)
                    for a in range(2):
                        act.dma_start(kitok[:, :, HD * a:HD * a + HD], A["cache_idx_k"][l, 0].rearrange("(i p) d -> p i d", p=P)
                                      ).then_inc(mix_in, 16)

                    def split(dst, src, at, smp, func=ACT.Copy):
                        nc.scalar.activation(dst[:, at:at + SEQ], src[:, 0:SEQ], func)
                        return nc.scalar.activation(dst[:, smp:smp + DEC], src[:, SEQ:T], func)

                    def silu(j):
                        act.wait_ge(conv_ready, CT * l + j + 1)
                        nc.scalar.activation(cT[:, j, :], cT[:, j, :], ACT.Silu).then_inc(silu_ready, 1)
                    for m in range(N_CH):
                        act.wait_ge(pj_done, N_CH * l + m + 1)
                        src = ps[m % 4][:, 0:T]
                        if m < 4:
                            ins = nc.scalar.activation(qaT[:, m, :], src, ACT.Copy, scale=HD ** -0.5)
                        elif m == 4:
                            ins = split(kT, src, 0, K_SMP)
                        elif m == 5:
                            ins = nc.scalar.activation(vT, src, ACT.Copy)
                        elif m < 10:
                            ins = nc.scalar.activation(qiT[:, m - 6, :], src, ACT.Copy)
                        elif m == 10:
                            ins = split(kiT, src, 0, K_SMP)
                        elif m == 11:
                            for i, (t0, n) in enumerate(TILES):
                                ins = nc.scalar.activation(wsm[0:n, i, :], ps[m % 4][0:n, 16 * i:16 * i + 16], ACT.Copy)
                        elif m < 24:
                            j = m - 12
                            ins = split(cin[:, j, :], src, CW - 1, 2 * (CW - 1) + SEQ)
                        else:
                            ins = nc.scalar.activation(zT[:, m - 24, :], src, ACT.Silu)
                        ins.then_inc(pj_evac, 1)
                        if m >= 16:
                            silu(m - 16)

                @block.tensor
                def _(pe):
                    def product(m, lhs, unit_of, last_use):
                        if m >= 4:
                            pe.wait_ge(pj_evac, N_CH * l + m - 3)
                        for k in range(KD):
                            if unit_of(k) is not None:
                                have(pe, unit_of(k))
                            ins = rel.mm(ps[m % 4][:, 0:T], lhs(k), hT[:, k, :], start=(k == 0), stop=(k == KD - 1))
                            if last_use and k == 3 and last_use == "pair":
                                rel.due = True
                        ins.then_inc(pj_done, 1)
                        if last_use:
                            rel.due = True

                    def pairview(n):
                        s = (n % RING) * SLOT
                        return ring[:, s:s + 2 * SLOT].rearrange("p (k c) -> p k c", c=512)
                    qw = pairview(u0)
                    for c in range(4):
                        product(c, lambda k: qw[:, k, P * c:P * c + P], lambda k: u0 + k // 4 if c == 0 and k % 4 == 0 else None, "pair" if c == 3 else "")
                    pe.wait_ge(mix_in, 96 * (l + 1))
                    for j in range(CT):
                        ins = nc.tensor.transpose(ps[4][:, 8 * j:8 * j + 7], crow[0:7, P * j:P * j + P], ident[0:7, 0:7])
                    for i in range(2):
                        nc.tensor.transpose(ps[5][:, P * i:P * i + P], ktok[:, i, :], ident[:])
                    for i in range(2):
                        ins = nc.tensor.transpose(ps[5][:, 256 + P * i:256 + P * i + P], kitok[:, i, :], ident[:])
                    ins.then_inc(pre_turned, 1)
                    kv = slot(u0 + 2, (8, 256))
                    for c in range(2):
                        product(4 + c, lambda k: kv[:, k, P * c:P * c + P], lambda k: u0 + 2 if k == 0 else None, c == 1)
                    iw = pairview(u0 + 3)
                    for c in range(4):
                        product(6 + c, lambda k: iw[:, k, P * c:P * c + P],
                                lambda k: u0 + 3 + k // 4 if c == 0 and k % 4 == 0 else None, "pair" if c == 3 else "")
                    sw = slot(u0 + 5, (8, 80))
                    pe.wait_ge(pj_evac, N_CH * l + 10 - 3)
                    have(pe, u0 + 5)
                    for half in range(2):
                        for k in range(KD):
                            ins = rel.mm(ps[10 % 4][64 * half:64 * half + 64, 0:T], sw[:, k, 0:HD], hT[:, k, :],
                                         start=(k == 0), stop=(k == KD - 1))
                    ins.then_inc(pj_done, 1)
                    pe.wait_ge(pj_evac, N_CH * l + 11 - 3)
                    for i, (t0, n) in enumerate(TILES):
                        for k in range(KD):
                            ins = rel.mm(ps[11 % 4][0:n, 16 * i:16 * i + 16], hT[:, k, t0:t0 + n], sw[:, k, HD:80],
                                         start=(k == 0), stop=(k == KD - 1))
                    ins.then_inc(pj_done, 1)
                    rel.due = True
                    for j in range(8):
                        n = u0 + 6 + j
                        w = slot(n, (8, 256))
                        for c in range(2):
                            product(12 + 2 * j + c, lambda k: w[:, k, P * c:P * c + P], lambda k: n if k == 0 else None, c == 1)
                    for i, (t0, n) in enumerate(TILES):
                        ins = nc.tensor.transpose(ps[5][0:n, P * i:P * i + P], vT[:, t0:t0 + n], ident[:])
                    ins.then_inc(post_turned, 1)
                    for i, (t0, n) in enumerate(TILES):
                        k0 = t0 if i < 2 else K_SMP
                        ins = nc.tensor.transpose(ps[6][0:n, P * i:P * i + P], kT[:, k0:k0 + n], ident[:])
                    ins.then_inc(post_turned, 1)
                    for i, (t0, n) in enumerate(TILES):
                        k0 = t0 if i < 2 else K_SMP
                        ins = nc.tensor.transpose(ps[7][0:n, HD * i:HD * i + HD], kiT[0:HD, k0:k0 + n], ident[0:HD, 0:HD])
                    ins.then_inc(post_turned, 1)
                    pe.wait_ge(last_ready, l + 1)
                    pe.wait_ge(pj_evac, N_CH * l + 24)
                    for g, b in enumerate((4, 0, 1)):
                        if b < 4:
                            pe.wait_ge(pj_evac, N_CH * l + 25 + b)
                        for j in range(4):
                            ins = nc.tensor.transpose(ps[b][0:6, P * j:P * j + P], last[:, 4 * g + j, :], ident[:])
                        ins.then_inc(post_turned, 1)

                @block.vector
                def _(dve):
                    c = chain(dve, "dve")
                    nc.vector.memset(cin[:, :, 0:3], 0.0).then_inc(pre_evac, 1)
                    dve.wait_ge(pre_turned, l + 1)
                    cwv = ps[4][:, 0:8 * CT].rearrange("p (j a) -> p j a", a=8)
                    c(nc.vector.tensor_copy(cw[:, :, 0:7], cwv[:, :, 0:7]))
                    nc.vector.tensor_copy(cin[:, :, CW - 1 + SEQ:2 * (CW - 1) + SEQ], cwv[:, :, CW:CW + 3]).then_inc(pre_evac, 1)
                    nc.vector.tensor_copy(kT[:, K_CACHE:K_SMP], ps[5][:, 0:256]).then_inc(pre_evac, 1)
                    nc.vector.tensor_copy(kiT[:, K_CACHE:K_SMP], ps[5][:, 256:512]).then_inc(pre_evac, 1)
                    dve.wait_ge(pre_evac, 4 * (l + 1))
                    c.sync()
                    for j in range(CT):
                        dve.wait_ge(pj_evac, N_CH * l + 12 + j + 1)
                        for a in range(CW):
                            tap = cw[:, j, a:a + 1]
                            src = cin[:, j, a:a + CO]
                            if a == 0:
                                c.link(nc.vector.tensor_scalar(cT[:, j, :], src, tap, None, ALU.mult))
                            else:
                                ins = nc.vector.scalar_tensor_tensor(out=cT[:, j, :], in0=src, scalar=tap, in1=cT[:, j, :],
                                                                     op0=ALU.mult, op1=ALU.add)
                                if a < CW - 1:
                                    c.link(ins)
                                else:
                                    ins.then_inc(conv_ready, 1)
                        nc.vector.tensor_copy(last[:, j, 0:3], cin[:, j, SEQ:SEQ + 3])
                        ins = nc.vector.tensor_copy(last[:, j, 3:6], cin[:, j, CI - 3:CI])
                    ins.then_inc(last_ready, 1)
                    dve.wait_ge(post_turned, 6 * l + 1)
                    nc.vector.tensor_copy(vtok[:, 0:2, :], ps[5][:, 0:256].rearrange("p (i c) -> p i c", i=2))
                    nc.vector.tensor_copy(vtok[0:DEC, 4, :], ps[5][0:DEC, 256:384]).then_inc(post_evac, 1)
                    dve.wait_ge(post_turned, 6 * l + 2)
                    nc.vector.tensor_copy(knew[:, 0:2, :], ps[6][:, 0:256].rearrange("p (i c) -> p i c", i=2))
                    nc.vector.tensor_copy(knew[0:DEC, 2, :], ps[6][0:DEC, 256:384]).then_inc(post_evac, 1)
                    dve.wait_ge(post_turned, 6 * l + 3)
                    nc.vector.tensor_copy(inew[:, 0:2, :], ps[7][:, 0:128].rearrange("p (i c) -> p i c", i=2))
                    nc.vector.tensor_copy(inew[0:DEC, 2, :], ps[7][0:DEC, 128:192]).then_inc(post_evac, 1)
                    for g, b in enumerate((4, 0, 1)):
                        dve.wait_ge(post_turned, 6 * l + 4 + g)
                        nc.vector.tensor_copy(lrow[0:6, 512 * g:512 * g + 512], ps[b][0:6, :]).then_inc(post_evac, 1)
                    keep(c, "dve")

        idx_done, relu_done, score_ready = sem("idx_done"), sem("relu_done"), sem("score_ready")
        lg_done, lg_ready, nm_ready, exp_done = sem("lg_done"), sem("lg_ready"), sem("nm_ready"), sem("exp_done")
        p_ready, pt_done, pt_evac, pv_done, oa_ready = sem("p_ready"), sem("pt_done"), sem("pt_evac"), sem("pv_done"), sem("oa_ready")
        at_ = Area()
        at_.at = ATT0
        SMAX = PAST + DEC
        relu = at_(IH, SMAX)
        lg = at_(A_HEADS, SMAX)
        prob = at_(A_HEADS, SMAX)
        probT = at_(3, A_HEADS * P)
        score = at_(SMAX)
        top8 = at_(8)
        away = at_(SMAX)
        pen = at_(2, SMAX)
        mx = at_(A_HEADS)
        nmx = at_(A_HEADS)
        den = at_(A_HEADS)
        rden = at_(A_HEADS)
        wis = at_(NT, IH)
        PT_OF = [2 * len(v) for v in VT]
        PT0 = [sum(PT_OF[:i]) for i in range(NT + 1)]

        def attend(l):
            def b8(i, h):
                return (l * NT + i) * 8 + h
            with nc.Block() as block:
                @block.tensor
                def _(pe):
                    def indexer(i):
                        (t0, n), (k0, s) = TILES[i], KEYS[i]
                        for h in range(IH):
                            if h >= 4:
                                pe.wait_ge(relu_done, b8(i, h) - 3)
                            elif i:
                                pe.wait_ge(relu_done, b8(i - 1, 8))
                            r = slice(HD * (h % 2), HD * (h % 2) + HD)
                            nc.tensor.matmul(ps[h % 4][0:n, 0:s], qiT[r, h // 2, t0:t0 + n], kiT[r, k0:k0 + s],
                                             start=True, stop=True).then_inc(idx_done, 1)

                    def logits(i):
                        (t0, n), (k0, s) = TILES[i], KEYS[i]
                        for h in range(A_HEADS):
                            if h >= 4:
                                pe.wait_ge(lg_ready, b8(i, h) - 3)
                            elif i:
                                pe.wait_ge(oa_ready, l * NT + i)
                            r = slice(HD * (h // 4), HD * (h // 4) + HD)
                            nc.tensor.matmul(ps[4 + h % 4][0:n, 0:s], qaT[r, h % 4, t0:t0 + n], kT[r, k0:k0 + s],
                                             start=True, stop=True).then_inc(lg_done, 1)

                    def turn(i):
                        (t0, n), (k0, s) = TILES[i], KEYS[i]
                        pe.wait_ge(p_ready, l * NT + i + 1)
                        for g in range(PT_OF[i]):
                            ck, j = g // 2, g % 2
                            kc = min(P, s - P * ck)
                            if g >= 4:
                                pe.wait_ge(pt_evac, l * PT0[NT] + PT0[i] + g - 3)
                            else:
                                pe.wait_ge(relu_done, b8(min(i + 1, NT - 1), 8))
                            for q in range(4):
                                ins = nc.tensor.transpose(ps[g % 4][0:kc, n * q:n * q + n],
                                                          prob[0:n, 4 * j + q, P * ck:P * ck + kc], ident[0:n, 0:n])
                            ins.then_inc(pt_done, 1)

                    def values(i):
                        (t0, n), (k0, s) = TILES[i], KEYS[i]
                        pe.wait_ge(pt_evac, l * PT0[NT] + PT0[i + 1])
                        pe.wait_ge(lg_ready, b8(i, 8))
                        for h in range(A_HEADS):
                            r = slice(HD * (h % 2), HD * (h % 2) + HD)
                            g = h // 4
                            for ck, vt in enumerate(VT[i]):
                                kc = min(P, s - P * ck)
                                ins = nc.tensor.matmul(ps[4][r, (h // 2) * P:(h // 2) * P + n], vtok[0:kc, vt, HD * g:HD * g + HD],
                                                       probT[0:kc, ck, n * h:n * h + n], start=(ck == 0),
                                                       stop=(ck == len(VT[i]) - 1))
                        ins.then_inc(pv_done, 1)

                    indexer(0)
                    for i in range(NT):
                        logits(i)
                        if i + 1 < NT:
                            if i:
                                pe.wait_ge(pt_evac, l * PT0[NT] + PT0[i])
                            indexer(i + 1)
                        turn(i)
                        values(i)

                @block.scalar
                def _(act):
                    def relus(i):
                        (t0, n), (k0, s) = TILES[i], KEYS[i]
                        if i or l:
                            act.wait_ge(score_ready, l * NT + i)
                        for h in range(IH):
                            act.wait_ge(idx_done, b8(i, h) + 1)
                            nc.scalar.activation(relu[0:n, h, 0:s], ps[h % 4][0:n, 0:s], ACT.Relu).then_inc(relu_done, 1)
                    relus(0)
                    for i in range(NT):
                        (t0, n), (k0, s) = TILES[i], KEYS[i]
                        if i + 1 < NT:
                            relus(i + 1)
                        act.wait_ge(nm_ready, l * NT + i + 1)
                        if i:
                            act.wait_ge(pt_done, l * PT0[NT] + PT0[i])
                        for h in range(A_HEADS):
                            nc.scalar.activation(prob[0:n, h, 0:s], lg[0:n, h, 0:s], ACT.Exp, bias=nmx[0:n, h:h + 1],
                                                 accum_out=den[0:n, h:h + 1]).then_inc(exp_done, 1)
                        for g in range(PT_OF[i]):
                            ck, j = g // 2, g % 2
                            kc = min(P, s - P * ck)
                            act.wait_ge(pt_done, l * PT0[NT] + PT0[i] + g + 1)
                            if i and g == 0:
                                act.wait_ge(pv_done, l * NT + i)
                            nc.scalar.activation(probT[0:kc, ck, 4 * j * n:4 * j * n + 4 * n], ps[g % 4][0:kc, 0:4 * n],
                                                 ACT.Copy).then_inc(pt_evac, 1)
                        act.wait_ge(pv_done, l * NT + i + 1)
                        nc.scalar.activation(oaT[:, :, t0:t0 + n], ps[4][:, :].rearrange("p (c t) -> p c t", c=4)[:, :, 0:n],
                                             ACT.Copy).then_inc(oa_ready, 1)

                @block.vector
                def _(dve):
                    c = chain(dve, "dve")
                    c.link(nc.vector.tensor_scalar(wis, wsm[:, :, 0:IH], HD ** -0.5, None, ALU.mult))

                    def choose(i):
                        (t0, n), (k0, s) = TILES[i], KEYS[i]
                        sc = score[0:n, 0:s]
                        for h in range(IH):
                            dve.wait_ge(relu_done, b8(i, h) + 1)
                            w = wis[0:n, i, h:h + 1]
                            if h == 0:
                                c.link(nc.vector.tensor_scalar(sc, relu[0:n, h, 0:s], w, None, ALU.mult))
                            else:
                                ins = nc.vector.scalar_tensor_tensor(out=sc, in0=relu[0:n, h, 0:s], scalar=w, in1=sc,
                                                                     op0=ALU.mult, op1=ALU.add)
                                if h < IH - 1:
                                    c.link(ins)
                                else:
                                    ins.then_inc(score_ready, 1)
                        dve.wait_ge(score_ready, l * NT + i + 1)
                        if i < 2:
                            c.link(nc.vector.tensor_tensor(sc, sc, adm[0:n, i, 0:s], ALU.add))
                        assert NSEL[i] % 8 == 0
                        for _ in range(NSEL[i] // 8):
                            c.link(nc.vector.max(top8[0:n], sc))
                            c.link(nc.vector.match_replace(out=sc, in_to_replace=top8[0:n], in_values=sc, imm_value=TAKEN))
                        c.link(nc.vector.tensor_scalar(away[0:n, 0:s], sc, TAKEN, -1e30, ALU.not_equal, ALU.mult))

                    choose(0)
                    for i in range(NT):
                        (t0, n), (k0, s) = TILES[i], KEYS[i]
                        if i:
                            dve.wait_ge(exp_done, b8(i - 1, 8))
                        for h in range(A_HEADS):
                            c.link(nc.vector.scalar_tensor_tensor(out=pen[0:n, h % 2, 0:s], in0=ndist[0:n, i, 0:s],
                                                                  scalar=2.0 ** -(h + 1), in1=away[0:n, 0:s],
                                                                  op0=ALU.mult, op1=ALU.add))
                            dve.wait_ge(lg_done, b8(i, h) + 1)
                            nc.vector.tensor_tensor(lg[0:n, h, 0:s], ps[4 + h % 4][0:n, 0:s], pen[0:n, h % 2, 0:s],
                                                    ALU.add).then_inc(lg_ready, 1)
                        dve.wait_ge(lg_ready, b8(i, 8))
                        c.link(nc.vector.tensor_reduce(mx[0:n], lg[0:n, :, 0:s], AX.X, ALU.max))
                        nc.vector.tensor_scalar(nmx[0:n], mx[0:n], -1.0, None, ALU.mult).then_inc(nm_ready, 1)
                        if i + 1 < NT:
                            choose(i + 1)
                        dve.wait_ge(exp_done, b8(i, 8))
                        c.link(nc.vector.reciprocal(rden[0:n], den[0:n]))
                        for h in range(A_HEADS):
                            ins = nc.vector.tensor_scalar(prob[0:n, h, 0:s], prob[0:n, h, 0:s], rden[0:n, h:h + 1], None,
                                                          ALU.mult)
                        ins.then_inc(p_ready, 1)
                    keep(c, "dve")

        PREP = ["norm", "qk", "v", "grow", "qT", "kT", "qdT", "KK", "QKT", "MdT", "MoT", "P2", "P2T", "X1", "P4", "P4T",
                "X2", "P8", "X3", "X3T", "B", "BT", "Y1", "B2", "TT", "u", "wT"]
        BY_DVE = {"norm", "qk", "v", "grow", "KK", "QKT", "X1", "X2", "X3", "Y1", "TT"}
        RN = {r: k for k, r in enumerate(PREP)}
        DV = [r for r in PREP if r in BY_DVE]
        AC = [r for r in PREP if r not in BY_DVE]
        dl_in, sq_ready, g_ready, beta_ready = sem("dl_in"), sem("sq_ready"), sem("g_ready"), sem("beta_ready")
        prep_done, prep_dve, prep_act = sem("prep_done"), sem("prep_dve"), sem("prep_act")
        sm_dve, sm_act, egl_done, egl_ready = sem("sm_dve"), sem("sm_act"), sem("egl_done"), sem("egl_ready")
        dec_in, dec_ready, x_ready = sem("dec_in"), sem("dec_ready"), sem("x_ready")
        ws_done, vnew_ready, o_done, o_ready = sem("ws_done"), sem("vnew_ready"), sem("o_done"), sem("o_ready")
        ds_done, s_ready, on_ready, ot_done, ob_ready = (sem("ds_done"), sem("s_ready"), sem("on_ready"), sem("ot_done"),
                                                         sem("ob_ready"))
        ssq_ready, rn_ready = sem("ssq_ready"), sem("rn_ready")
        H4 = B_HEADS
        da = Area()
        sq = da(2 * H4, CO)
        SQ_END = da.at
        da.at = 0
        USES = [("q", "Md", "P4T", "XT", "vnew"), ("k", "Mo", "X", "TT"), ("qd", "MdT", "u"),
                ("gtri", "qT", "PT", "P8", "B2", "on"), ("kT", "P", "BT", "o"), ("E", "MoT", "wT"), ("ET", "P4", "B"),
                ("QKT",), ("qdT",), ("kbG",), ("kt",), ("vb",)]
        WIDE = {"q", "k", "qd", "u", "vnew", "o", "on", "kbG", "kt", "vb"}
        tl = []
        for i in range(NT):
            n = TILES[i][1]
            d = {}
            for names in USES:
                at = da.at
                da.at += H4 * (BD if WIDE & set(names) else n)
                for x in names:
                    w = BD if x in WIDE else n
                    d[x] = arena[:, at:at + H4 * w].rearrange("p (h x) -> p h x", h=H4)
            tl.append(d)
        osq = da(H4, BD)
        da.at = max(da.at, SQ_END)
        state = da(2, H4 * BD).rearrange("p s (h v) -> p s h v", h=H4)
        prm = da(2, H4)
        gn = da(2)
        sp_ = da(3, NT * H4).rearrange("p a (i h) -> p a i h", i=NT)
        gv = da(NT, H4)
        nG = da(NT, H4)
        nbeta = da(NT, H4)
        nrm16 = da(NT, 16)
        sc = da(NT, 6 * H4).rearrange("p i (a h) -> p i a h", a=6)
        eg = da(5, H4)
        rr = da(NT, H4)
        SC_Q, SC_QD, SC_K, SC_KBG, SC_KT, SC_VB = range(6)
        SEQS = [(0, 0, 0, 0), (2, 0, 1, 4), (0, 64, 0, 1), (1, 0, 0, 2), (1, 64, 0, 3)]

        def delta(l):
            NR = len(PREP)
            sb_ = l * NT

            def at_round(r, i):
                return (l * NR + RN[r]) * NT + i + 1

            def evac_of(r, i):
                if r in BY_DVE:
                    return prep_dve, (l * len(DV) + DV.index(r)) * NT + i + 1
                return prep_act, (l * len(AC) + AC.index(r)) * NT + i + 1

            def bank(r, i):
                return ps[2 * i + RN[r] % 2]

            def v4(ap, n, w):
                return ap[0:n, 0:H4 * w].rearrange("p (h x) -> p h x", h=H4)

            with nc.Block() as block:
                @block.sync
                def _(sp):
                    sp.dma_start(prm[:, 0, :], A["a_log"][l].partition_broadcast(P)).then_inc(dl_in, 16)
                    sp.dma_start(prm[:, 1, :], A["dt_bias"][l].partition_broadcast(P)).then_inc(dl_in, 16)
                    sp.dma_start(gn[:, 0:1], A["gnorm_g"][l].rearrange("(p a) -> p a", a=1)).then_inc(dl_in, 16)
                    sp.dma_start(state[:, 1, :, :], A["state_gdn"][l, 0].rearrange("h k v -> k h v")).then_inc(dl_in, 16)
                    sp.wait_ge(s_ready, len(SEQS) * (l + 1))
                    sp.dma_start(OUT["new_gdn_p"][l, 0].rearrange("h k v -> k h v"), state[:, 0, :, :]).then_inc(new_stored, 16)
                    sp.dma_start(OUT["new_gdn_s"][l, 0].rearrange("h k v -> k h v"), state[:, 1, :, :]).then_inc(new_stored, 16)
                    sp.wait_ge(new_stored, 160 * (l + 1))

                @block.gpsimd
                def _(pool):
                    nc.gpsimd.tensor_tensor(sq, cT[:, 0:2 * H4, :], cT[:, 0:2 * H4, :], ALU.mult).then_inc(sq_ready, 1)

                @block.tensor
                def _(pe):
                    def need(r, i):
                        s, v = evac_of(r, i)
                        pe.wait_ge(s, v)
                    pe.wait_ge(sq_ready, l + 1)
                    pe.wait_ge(g_ready, l + 1)
                    for i, (t0, n) in enumerate(TILES):
                        b = ps[6]
                        if i:
                            need("norm", i - 1)
                        for h in range(2 * H4):
                            nc.tensor.matmul(b[0:n, 16 * i + h:16 * i + h + 1], sq[:, h, CCOL[i]:CCOL[i] + n], ones[:, 0:1],
                                             start=True, stop=True)
                        nc.tensor.matmul(b[0:n, 16 * i + 8:16 * i + 12], cumU[0:n, 0:n], gv[0:n, i, :], start=True, stop=True)
                        nc.tensor.matmul(b[0:n, 16 * i + 12:16 * i + 16], blk[0:n, 0:n], gv[0:n, i, :], start=True,
                                         stop=True).then_inc(prep_done, 1)
                    for (i, r0, s, ch) in SEQS:
                        n = TILES[i][1]
                        ins = nc.tensor.matmul(ps[7][:, H4 * ch:H4 * ch + H4], blk[0:n, r0:r0 + 1].to_broadcast([n, P]),
                                               gv[0:n, i, :], start=True, stop=True)
                    ins.then_inc(egl_done, 1)

                    def turns(r, src, w_in, w_out):
                        def f(i, n, h, b):
                            ri, wi_ = (n if w_in is None else w_in), (n if w_out is None else w_out)
                            return nc.tensor.transpose(v4(b, wi_, ri)[:, h, :], src(i, h), ident[0:ri, 0:ri])
                        return f

                    def mul(lhs, rhs, w=None):
                        def f(i, n, h, b):
                            ww = n if w is None else w
                            d = tl[i]
                            return nc.tensor.matmul(v4(b, n, ww)[:, h, :], d[lhs][0:n, h, :], d[rhs][0:n, h, :],
                                                    start=True, stop=True)
                        return f

                    def deep(lhs, rhs):
                        def f(i, n, h, b):
                            d = tl[i]
                            return nc.tensor.matmul(v4(b, n, n)[:, h, :], d[lhs][:, h, :], d[rhs][:, h, :],
                                                    start=True, stop=True)
                        return f

                    def tok(c0):
                        def f(i, n, h, b):
                            return nc.tensor.transpose(v4(b, n, BD)[:, h, :], cT[:, c0 + h, CCOL[i]:CCOL[i] + n], ident[:])
                        return f

                    for i, (t0, n) in enumerate(TILES):
                        for h in range(H4):
                            tok(0)(i, n, h, ps[2 * i])
                        for h in range(H4):
                            ins = tok(H4)(i, n, h, ps[2 * i + 1])
                        ins.then_inc(prep_done, 1)
                    T3 = {
                        "v": (tok(2 * H4), ["qk"]),
                        "grow": (lambda i, n, h, b: nc.tensor.matmul(
                            v4(b, n, n)[:, h, :], ones[0:n, 0:n], tl[i]["gtri"][0:n, h, :], start=True, stop=True), ["qk"]),
                        "qT": (lambda i, n, h, b: nc.tensor.transpose(
                            v4(b, BD, n)[:, h, :], tl[i]["q"][0:n, h, :], ident[0:n, 0:n]), ["v"]),
                        "kT": (lambda i, n, h, b: nc.tensor.transpose(
                            v4(b, BD, n)[:, h, :], tl[i]["k"][0:n, h, :], ident[0:n, 0:n]), ["grow"]),
                        "qdT": (lambda i, n, h, b: nc.tensor.transpose(
                            v4(b, BD, n)[:, h, :], tl[i]["qd"][0:n, h, :], ident[0:n, 0:n]), ["qT"]),
                        "KK": (deep("kT", "kT"), ["kT"]),
                        "QKT": (deep("kT", "qT"), ["qdT"]),
                        "MdT": (lambda i, n, h, b: nc.tensor.transpose(
                            v4(b, n, n)[:, h, :], tl[i]["Md"][0:n, h, :], ident[0:n, 0:n]), ["KK"]),
                        "MoT": (lambda i, n, h, b: nc.tensor.transpose(
                            v4(b, n, n)[:, h, :], tl[i]["Mo"][0:n, h, :], ident[0:n, 0:n]), ["QKT"]),
                        "P2": (mul("MdT", "Md"), ["MdT"]),
                        "P2T": (mul("Md", "MdT"), ["MoT"]),
                        "X1": (mul("P", "X"), ["P2"]),
                        "P4": (mul("PT", "P"), ["P2T"]),
                        "P4T": (mul("P", "PT"), ["X1"]),
                        "X2": (mul("P4", "X"), ["P4"]),
                        "P8": (mul("P4T", "P4"), ["P4T"]),
                        "X3": (mul("P8", "X"), ["X2", "P8"]),
                        "X3T": (lambda i, n, h, b: nc.tensor.transpose(
                            v4(b, n, n)[:, h, :], tl[i]["X"][0:n, h, :], ident[0:n, 0:n]), ["X3"]),
                        "B": (mul("MoT", "XT"), ["X3T"]),
                        "BT": (mul("XT", "MoT"), ["X3T"]),
                        "Y1": (mul("B", "X"), ["B"]),
                        "B2": (mul("BT", "B"), ["BT"]),
                        "TT": (mul("B2", "X"), ["B2", "Y1"]),
                        "u": (mul("TT", "vb", BD), ["TT"]),
                        "wT": (lambda i, n, h, b: nc.tensor.matmul(
                            v4(b, BD, n)[:, h, :], tl[i]["kbG"][0:n, h, :], tl[i]["TT"][0:n, h, :], start=True, stop=True),
                            ["TT"]),
                    }
                    for r in PREP[2:]:
                        f, needs = T3[r]
                        for i, (t0, n) in enumerate(TILES):
                            prev = PREP[RN[r] - 2]
                            if RN[r] - 2 >= 1:
                                need(prev, i)
                            for x in needs:
                                need(x, i)
                            if r == "grow":
                                pe.wait_ge(dec_in, sb_ + i + 1)
                            if r == "X1":
                                pe.wait_ge(x_ready, sb_ + i + 1)
                            for h in range(H4):
                                ins = f(i, n, h, bank(r, i))
                            ins.then_inc(prep_done, 1)

                    for q, (i, r0, s, ch) in enumerate(SEQS):
                        n = min(CHUNK, TILES[i][1])
                        R = slice(r0, r0 + n)
                        d = tl[i]
                        g = len(SEQS) * l + q
                        need("u", i)
                        need("wT", i)
                        if q == 0:
                            pe.wait_ge(egl_ready, l + 1)
                        elif q == 1:
                            pe.wait_ge(dl_in, 64 * (l + 1))
                        else:
                            pe.wait_ge(s_ready, g)
                        if q:
                            pe.wait_ge(vnew_ready, g)
                        A_, B_, C_ = ps[6], ps[7], ps[0]
                        for h in range(H4):
                            ins = nc.tensor.matmul(A_[R, BD * h:BD * h + BD], d["wT"][:, h, R], state[:, s, h, :],
                                                   start=True, stop=True)
                        ins.then_inc(ws_done, 1)
                        pe.wait_ge(vnew_ready, g + 1)
                        if q:
                            pe.wait_ge(o_ready, g)
                            pe.wait_ge(s_ready, g)
                        for h in range(H4):
                            ins = nc.tensor.matmul(C_[:, BD * h:BD * h + BD], d["kt"][R, h, :], d["vnew"][R, h, :],
                                                   start=True, stop=True)
                        ins.then_inc(ds_done, 1)
                        for h in range(H4):
                            nc.tensor.matmul(B_[R, BD * h:BD * h + BD], d["qdT"][:, h, R], state[:, s, h, :],
                                             start=True, stop=False)
                            ins = nc.tensor.matmul(B_[R, BD * h:BD * h + BD], d["QKT"][R, h, R], d["vnew"][R, h, :],
                                                   start=False, stop=True)
                        ins.then_inc(o_done, 1)
                    for i, (t0, n) in enumerate(TILES):
                        pe.wait_ge(on_ready, sb_ + i + 1)
                        for h in range(H4):
                            ins = nc.tensor.transpose(v4(ps[1 + i], BD, n)[:, h, :], tl[i]["on"][0:n, h, :], ident[0:n, 0:n])
                        ins.then_inc(ot_done, 1)

                @block.scalar
                def _(act):
                    c = chain(act, "act")
                    act.wait_ge(dl_in, 64 * (l + 1))
                    c.link(nc.scalar.activation(prm[:, 0, :], prm[:, 0, :], ACT.Exp))
                    act.wait_ge(sm_dve, 2 * l + 1)
                    c.link(nc.scalar.activation(sp_[:, 1, :, :], sp_[:, 1, :, :], ACT.Exp))
                    c.link(nc.scalar.activation(sp_[:, 1, :, :], sp_[:, 1, :, :], ACT.Ln, bias=1.0))
                    nc.scalar.activation(sp_[:, 2, :, :], wsm[:, :, 12:16], ACT.Exp, scale=-1.0).then_inc(sm_act, 1)
                    act.wait_ge(sm_dve, 2 * l + 2)
                    c.link(nc.scalar.activation(nrm16[:, :, 0:8], nrm16[:, :, 0:8], ACT.Ln))
                    c.link(nc.scalar.activation(nrm16[:, :, 0:8], nrm16[:, :, 0:8], ACT.Exp, scale=-0.5))
                    c.link(nc.scalar.activation(nrm16[:, :, 12:16], nrm16[:, :, 12:16], ACT.Exp))
                    c.link(nc.scalar.activation(sp_[:, 0, :, :], nrm16[:, :, 8:12], ACT.Exp))
                    act.wait_ge(egl_done, l + 1)
                    nc.scalar.activation(eg.rearrange("p a h -> p (a h)"), ps[7][:, 0:20], ACT.Exp).then_inc(sm_act, 1)

                    def copies(r, dst, scale=1.0):
                        for i, (t0, n) in enumerate(TILES):
                            act.wait_ge(prep_done, at_round(r, i))
                            dd = tl[i][dst]
                            rows_ = BD if r in ("qT", "kT", "qdT", "wT") else n
                            w = BD if r == "u" else n
                            nc.scalar.activation(dd[0:rows_], v4(bank(r, i), rows_, w), ACT.Copy, scale=scale
                                                 ).then_inc(prep_act, 1)
                    for r in AC:
                        if r == "kT":
                            for i, (t0, n) in enumerate(TILES):
                                act.wait_ge(prep_dve, evac_of("grow", i)[1])
                                for h in range(H4):
                                    nc.scalar.activation(tl[i]["E"][0:n, h, :], tl[i]["E"][0:n, h, :], ACT.Exp,
                                                         bias=nrm16[0:n, i, 8 + h:9 + h])
                                    ins = nc.scalar.activation(tl[i]["ET"][0:n, h, :], tl[i]["ET"][0:n, h, :], ACT.Exp,
                                                               bias=nG[0:n, i, h:h + 1])
                                ins.then_inc(dec_ready, 1)
                        copies(r, {"P2": "P", "P2T": "PT", "X3T": "XT"}.get(r, r), -1.0 if r == "wT" else 1.0)
                    for q, (i, r0, s, ch) in enumerate(SEQS):
                        n = min(CHUNK, TILES[i][1])
                        g = len(SEQS) * l + q
                        act.wait_ge(o_done, g + 1)
                        nc.scalar.activation(tl[i]["o"][r0:r0 + n], v4(ps[7][r0:r0 + n], n, BD), ACT.Copy).then_inc(o_ready, 1)
                    act.wait_ge(ssq_ready, l + 1)
                    c.link(nc.scalar.activation(rr, rr, ACT.Ln))
                    nc.scalar.activation(rr, rr, ACT.Exp, scale=-0.5).then_inc(rn_ready, 1)
                    keep(c, "act")

                @block.vector
                def _(dve):
                    c = chain(dve, "dve")
                    V = nc.vector
                    c(V.memset(rr, 1.0))
                    c(V.memset(nrm16, 1.0))
                    dve.wait_ge(dl_in, 64 * (l + 1))
                    for i in range(NT):
                        ins = V.tensor_tensor(sp_[:, 0, i, :], wsm[:, i, 8:12], prm[:, 1, :], ALU.add)
                    c.link(ins)
                    c.link(V.scalar_tensor_tensor(out=sp_[:, 1, :, :], in0=sp_[:, 0, :, :], scalar=-1.0, in1=sp_[:, 0, :, :],
                                                  op0=ALU.mult, op1=ALU.min))
                    V.tensor_scalar(sp_[:, 0, :, :], sp_[:, 0, :, :], 0.0, None, ALU.max).then_inc(sm_dve, 1)
                    dve.wait_ge(sm_act, 2 * l + 1)
                    c.link(V.tensor_tensor(sp_[:, 0, :, :], sp_[:, 0, :, :], sp_[:, 1, :, :], ALU.add))
                    for i in range(NT):
                        ins = V.scalar_tensor_tensor(out=gv[:, i, :], in0=sp_[:, 0, i, :], scalar=-1.0, in1=prm[:, 0, :],
                                                     op0=ALU.mult, op1=ALU.mult)
                    ins.then_inc(g_ready, 1)
                    c.link(V.tensor_scalar(sp_[:, 2, :, :], sp_[:, 2, :, :], 1.0, None, ALU.add))
                    c.link(V.reciprocal(sp_[:, 2, :, :], sp_[:, 2, :, :]))
                    c.link(V.tensor_scalar(nbeta, sp_[:, 2, :, :], -1.0, None, ALU.mult))
                    for i, (t0, n) in enumerate(TILES):
                        dve.wait_ge(prep_done, at_round("norm", i))
                        c.link(V.tensor_copy(nrm16[0:n, i, :], ps[6][0:n, 16 * i:16 * i + 16]))
                        V.tensor_scalar(nG[0:n, i, :], nrm16[0:n, i, 8:12], -1.0, None, ALU.mult).then_inc(prep_dve, 1)
                    dve.wait_ge(prep_dve, evac_of("norm", NT - 1)[1])
                    c.link(V.tensor_tensor(nrm16[:, :, 12:16], nrm16[:, :, 12:16], nrm16[:, :, 8:12], ALU.subtract))
                    V.tensor_scalar(nrm16[:, :, 0:8], nrm16[:, :, 0:8], RMS_EPS, None, ALU.add).then_inc(sm_dve, 1)
                    dve.wait_ge(sm_act, 2 * l + 2)
                    rq, rk, eT, eG, beta = (nrm16[:, :, 0:4], nrm16[:, :, 4:8], nrm16[:, :, 12:16], sp_[:, 0, :, :],
                                            sp_[:, 2, :, :])
                    c.link(V.tensor_scalar(sc[:, :, SC_Q, :], rq, BD ** -0.5, None, ALU.mult))
                    c.link(V.tensor_tensor(sc[:, :, SC_QD, :], sc[:, :, SC_Q, :], eG, ALU.mult))
                    c.link(V.tensor_copy(sc[:, :, SC_K, :], rk))
                    c.link(V.tensor_tensor(sc[:, :, SC_KT, :], rk, eT, ALU.mult))
                    c.link(V.tensor_copy(sc[:, :, SC_VB, :], beta))
                    c.link(V.tensor_tensor(sc[:, :, SC_KBG, :], rk, eG, ALU.mult))
                    c.link(V.tensor_tensor(sc[:, :, SC_KBG, :], sc[:, :, SC_KBG, :], beta, ALU.mult))
                    dve.wait_ge(sm_act, 2 * l + 2)
                    V.memset(state[:, 0, :, :], 0.0).then_inc(egl_ready, 1)

                    def scaled(dst, src, i, n, which):
                        f = sc[0:n, i, which, :].unsqueeze(2).to_broadcast([n, H4, BD])
                        return V.tensor_tensor(dst[0:n], v4(src, n, BD), f, ALU.mult)
                    for i, (t0, n) in enumerate(TILES):
                        d = tl[i]
                        dve.wait_ge(prep_done, at_round("qk", i))
                        c(scaled(d["q"], ps[2 * i], i, n, SC_Q))
                        c(scaled(d["qd"], ps[2 * i], i, n, SC_QD))
                        c(scaled(d["k"], ps[2 * i + 1], i, n, SC_K))
                        c(scaled(d["kbG"], ps[2 * i + 1], i, n, SC_KBG))
                        for h in range(H4):
                            ins = V.tensor_scalar(d["gtri"][0:n, h, :], cumU[0:n, 0:n], gv[0:n, i, h:h + 1], None, ALU.mult)
                        ins.then_inc(dec_in, 1)
                        scaled(d["kt"], ps[2 * i + 1], i, n, SC_KT).then_inc(prep_dve, 1)
                    for i, (t0, n) in enumerate(TILES):
                        dve.wait_ge(prep_done, at_round("v", i))
                        scaled(tl[i]["vb"], bank("v", i), i, n, SC_VB).then_inc(prep_dve, 1)

                    def allh(m, n):
                        return m[0:n, 0:n].unsqueeze(1).to_broadcast([n, H4, n])
                    for i, (t0, n) in enumerate(TILES):
                        d = tl[i]
                        dve.wait_ge(prep_done, at_round("grow", i))
                        gr = v4(bank("grow", i), n, n)
                        for h in range(H4):
                            V.scalar_tensor_tensor(out=d["E"][0:n, h, :], in0=gr[:, h, :], scalar=-1.0, in1=negL[0:n, 0:n],
                                                   op0=ALU.mult, op1=ALU.add)
                        V.tensor_tensor(d["ET"][0:n], gr, allh(negU, n), ALU.add).then_inc(prep_dve, 1)
                    for i, (t0, n) in enumerate(TILES):
                        d = tl[i]
                        dve.wait_ge(prep_done, at_round("KK", i))
                        dve.wait_ge(dec_ready, sb_ + i + 1)
                        dve.wait_ge(prep_act, evac_of("qdT", i)[1])
                        kk = v4(bank("KK", i), n, n)
                        for h in range(H4):
                            ins = V.scalar_tensor_tensor(out=d["E"][0:n, h, :], in0=kk[:, h, :], scalar=nbeta[0:n, i, h:h + 1],
                                                         in1=d["E"][0:n, h, :], op0=ALU.mult, op1=ALU.mult)
                        c.link(ins)
                        V.tensor_tensor(d["Mo"][0:n], d["E"][0:n], allh(off16, n), ALU.mult)
                        V.tensor_tensor(d["Md"][0:n], d["E"][0:n], allh(d16, n), ALU.mult).then_inc(prep_dve, 1)
                    for i, (t0, n) in enumerate(TILES):
                        d = tl[i]
                        dve.wait_ge(prep_done, at_round("QKT", i))
                        V.tensor_tensor(d["QKT"][0:n], v4(bank("QKT", i), n, n), d["ET"][0:n], ALU.mult).then_inc(prep_dve, 1)
                    for i, (t0, n) in enumerate(TILES):
                        d = tl[i]
                        dve.wait_ge(prep_act, evac_of("MoT", i)[1])
                        V.tensor_tensor(d["X"][0:n], d["MdT"][0:n], allh(ident, n), ALU.add).then_inc(x_ready, 1)
                    for r in ("X1", "X2", "X3", "Y1", "TT"):
                        for i, (t0, n) in enumerate(TILES):
                            d = tl[i]
                            dve.wait_ge(prep_done, at_round(r, i))
                            if r == "X1":
                                dve.wait_ge(x_ready, sb_ + i + 1)
                            else:
                                prev = {"X2": "X1", "X3": "X2", "Y1": "X3", "TT": "Y1"}[r]
                                dve.wait_ge(prep_dve, evac_of(prev, i)[1])
                            V.tensor_tensor(d["X"][0:n], d["X"][0:n], v4(bank(r, i), n, n), ALU.add).then_inc(prep_dve, 1)

                    for q, (i, r0, s, ch) in enumerate(SEQS):
                        n = min(CHUNK, TILES[i][1])
                        R = slice(r0, r0 + n)
                        d = tl[i]
                        g = len(SEQS) * l + q
                        dve.wait_ge(ws_done, g + 1)
                        dve.wait_ge(prep_act, evac_of("u", i)[1])
                        V.tensor_tensor(d["vnew"][R], v4(ps[6][R], n, BD), d["u"][R], ALU.add).then_inc(vnew_ready, 1)
                        dve.wait_ge(ds_done, g + 1)
                        dve.wait_ge(o_done, g + 1)
                        for h in range(H4):
                            ins = V.scalar_tensor_tensor(out=state[:, s, h, :], in0=state[:, s, h, :], scalar=eg[:, ch, h:h + 1],
                                                         in1=ps[0][:, BD * h:BD * h + BD], op0=ALU.mult, op1=ALU.add)
                        ins.then_inc(s_ready, 1)
                    dve.wait_ge(o_ready, len(SEQS) * (l + 1))
                    for i, (t0, n) in enumerate(TILES):
                        c.link(V.tensor_tensor(osq[0:n], tl[i]["o"][0:n], tl[i]["o"][0:n], ALU.mult))
                        c.link(V.tensor_reduce(rr[0:n, i, :], osq[0:n], AX.X, ALU.add))
                    V.tensor_scalar(rr, rr, 1.0 / BD, RMS_EPS, ALU.mult, ALU.add).then_inc(ssq_ready, 1)
                    dve.wait_ge(rn_ready, l + 1)
                    for i, (t0, n) in enumerate(TILES):
                        f = rr[0:n, i, :].unsqueeze(2).to_broadcast([n, H4, BD])
                        V.tensor_tensor(tl[i]["on"][0:n], tl[i]["o"][0:n], f, ALU.mult).then_inc(on_ready, 1)
                    for i, (t0, n) in enumerate(TILES):
                        dve.wait_ge(ot_done, sb_ + i + 1)
                        V.scalar_tensor_tensor(out=obT[:, :, t0:t0 + n], in0=v4(ps[1 + i], BD, n), scalar=gn[:, 0:1],
                                               in1=zT[:, :, t0:t0 + n], op0=ALU.mult, op1=ALU.mult).then_inc(ob_ready, 1)
                    keep(c, "dve")

        mg_done, mg_tanh, mg_read, m_ready, mo_done, mo_added = (sem("mg_done"), sem("mg_tanh"), sem("mg_read"),
                                                                 sem("m_ready"), sem("mo_done"), sem("mo_added"))
        ma = Area()
        mT = ma(KD, T)
        th = ma(2, 2 * T)
        mo_ = ma(2, 2 * T)

        def merge(l):
            u0 = first["merge", l]
            with nc.Block() as block:
                @block.sync
                def _(sp):
                    load_units(sp, u0 + N_MERGE - 1)

                @block.tensor
                def _(pe):
                    for c in range(KD):
                        b = 4 * (c % 2)
                        un = u0 + 3 * (c // 2)
                        off = P * (c % 2)
                        if c >= 2:
                            pe.wait_ge(mg_read, KD * l + c - 1)
                        for g in range(2):
                            w = slot(un + g, (8, 256))
                            have(pe, un + g)
                            for k in range(KD):
                                ins = rel.mm(ps[b + g][:, 0:T], w[:, k, off:off + P], hT[:, k, :], start=(k == 0),
                                             stop=(k == KD - 1))
                            if c % 2:
                                rel.due = True
                            ins.then_inc(mg_done, 1)
                        w = slot(un + 2, (8, 256))
                        have(pe, un + 2)
                        for g, o in enumerate((oaT, obT)):
                            for k in range(4):
                                ins = rel.mm(ps[b + 2 + g][:, 0:T], w[:, 4 * g + k, off:off + P], o[:, k, :], start=(k == 0),
                                             stop=(k == 3))
                        if c % 2:
                            rel.due = True
                        ins.then_inc(mg_done, 1)
                    pe.wait_ge(m_ready, KD * (l + 1))
                    for j in range(4):
                        w = slot(u0 + 12 + j, (8, 256))
                        have(pe, u0 + 12 + j)
                        for i, (t0, n) in enumerate(TILES):
                            g = NT * j + i
                            if g >= 8:
                                pe.wait_ge(mo_added, 4 * NT * l + g - 7)
                            for k in range(KD):
                                ins = rel.mm(ps[g % 8][0:n, 0:256], mT[:, k, t0:t0 + n], w[:, k, :], start=(k == 0),
                                             stop=(k == KD - 1))
                            ins.then_inc(mo_done, 1)
                        rel.due = True

                @block.scalar
                def _(act):
                    for c in range(KD):
                        b = 4 * (c % 2)
                        if c >= 2:
                            act.wait_ge(mg_read, KD * l + c - 1)
                        for g in range(2):
                            act.wait_ge(mg_done, 3 * (KD * l + c) + g + 1)
                            nc.scalar.activation(th[:, c % 2, T * g:T * g + T], ps[b + g][:, 0:T], ACT.Tanh, scale=0.5
                                                 ).then_inc(mg_tanh, 1)

                @block.vector
                def _(dve):
                    c_ = chain(dve, "dve")
                    for c in range(KD):
                        b = 4 * (c % 2)
                        dve.wait_ge(mg_tanh, 2 * (KD * l + c + 1))
                        dve.wait_ge(mg_done, 3 * (KD * l + c + 1))
                        for g in range(2):
                            s = slice(T * g, T * g + T)
                            ins = nc.vector.scalar_tensor_tensor(out=mo_[:, c % 2, s], in0=th[:, c % 2, s], scalar=1.0,
                                                                 in1=ps[b + 2 + g][:, 0:T], op0=ALU.add, op1=ALU.mult)
                        ins.then_inc(mg_read, 1)
                        dve.wait_ge(mg_read, KD * l + c + 1)
                        nc.vector.tensor_tensor(mT[:, c, :], mo_[:, c % 2, 0:T], mo_[:, c % 2, T:2 * T], ALU.add
                                                ).then_inc(m_ready, 1)
                    for j in range(4):
                        for i, (t0, n) in enumerate(TILES):
                            g = NT * j + i
                            dve.wait_ge(mo_done, 4 * NT * l + g + 1)
                            r = resid[0:n, i, 256 * j:256 * j + 256]
                            nc.vector.scalar_tensor_tensor(out=r, in0=ps[g % 8][0:n, 0:256], scalar=0.5, in1=r,
                                                           op0=ALU.mult, op1=ALU.add).then_inc(mo_added, 1)
                    keep(c_, "dve")

        up_done, silu_done, g_read, w2_done, y_added = (sem("up_done"), sem("silu_done"), sem("g_read"), sem("w2_done"),
                                                        sem("y_added"))

        def up_products(pe, n0, chunks, x, n, base, experts=0):
            for m in range(chunks):
                if m >= 2 or not isinstance(base, int):
                    pe.wait_ge(g_read, base + m - 1)
                for g in range(2):
                    un = n0 + 2 * (m // 2) + g
                    if m % 2 == 0:
                        have(pe, un, experts)
                    w = slot(un, (8, 256))
                    for k in range(KD):
                        ins = rel.mm(ps[2 * g + m % 2][:, 0:n], w[:, k, P * (m % 2):P * (m % 2) + P], x[:, k, 0:n],
                                     start=(k == 0), stop=(k == KD - 1))
                    if m % 2:
                        rel.due = True
                    ins.then_inc(up_done, 1)

        def silus(act, chunks, n, sl, base):
            for m in range(chunks):
                act.wait_ge(up_done, 2 * (base + m) + 1)
                if m >= 2 or not isinstance(base, int) or base:
                    act.wait_ge(g_read, base + m - 1)
                nc.scalar.activation(sl[:, m % 2, 0:n], ps[m % 2][:, 0:n], ACT.Silu).then_inc(silu_done, 1)

        def gated(dve, chunks, n, sl, gT, base):
            for m in range(chunks):
                dve.wait_ge(up_done, 2 * (base + m) + 2)
                dve.wait_ge(silu_done, base + m + 1)
                nc.vector.tensor_tensor(gT[:, m, 0:n], sl[:, m % 2, 0:n], ps[2 + m % 2][:, 0:n], ALU.mult).then_inc(g_read, 1)

        FCH, ECH = D_FF // P, D_FFE // P

        def dense_mlp():
            fa = Area()
            gT = fa(FCH, T)
            sl = fa(2, T)
            n0 = first["mlp", 0]
            with nc.Block() as block:
                @block.sync
                def _(sp):
                    load_units(sp, n0 + N_FFN - 1)

                @block.tensor
                def _(pe):
                    up_products(pe, n0, FCH, hT, T, 0)
                    pe.wait_ge(g_read, FCH)
                    for j in range(FCH // 2):
                        un = n0 + FCH + j
                        w = slot(un, (2, D))
                        have(pe, un)
                        for q in range(2):
                            f = 2 * j + q
                            for i, (t0, n) in enumerate(TILES):
                                for c in range(2):
                                    ins = rel.mm(ps[2 * i + c][0:n, :], gT[:, f, t0:t0 + n],
                                                 w[:, q, 512 * c:512 * c + 512], start=(f == 0), stop=(f == FCH - 1))
                                    if f == FCH - 1:
                                        ins.then_inc(w2_done, 1)
                        rel.due = True

                @block.scalar
                def _(act):
                    silus(act, FCH, T, sl, 0)

                @block.vector
                def _(dve):
                    gated(dve, FCH, T, sl, gT, 0)
                    for i, (t0, n) in enumerate(TILES):
                        for c in range(2):
                            dve.wait_ge(w2_done, 2 * i + c + 1)
                            r = resid[0:n, i, 512 * c:512 * c + 512]
                            nc.vector.tensor_tensor(r, r, ps[2 * i + c][0:n, :], ALU.add).then_inc(y_added, 1)

        lgt_in, rt_done, sel_ready, pos_done, flag_ready, pos_ready = (sem("lgt_in"), sem("rt_done"), sem("sel_ready"),
                                                                       sem("pos_done"), sem("flag_ready"), sem("pos_ready"))
        rt_read, rt_exp, rt_top = sem("rt_read"), sem("rt_exp"), sem("rt_top")
        oh_ready, ga_done, xg_ready, ohg_ready, ohT_done, ohT_ready = (sem("oh_ready"), sem("ga_done"), sem("xg_ready"),
                                                                       sem("ohg_ready"), sem("ohT_done"), sem("ohT_ready"))
        y_done, y_ready, sc_done, sc_added = sem("y_done"), sem("y_ready"), sem("sc_done"), sem("sc_added")
        ea = Area()
        htok = ea(NT, D)
        router = ea(KD, NE)
        xg = ea(KD, CAP)
        gE = ea(ECH, CAP)
        slE = ea(2, CAP)
        yE = ea(D)
        oh = ea(NT, CAP)
        ohg = ea(NT, CAP)
        ohT = ea(NT, P)
        rlog = ea(NT, NE)
        rtop = ea(NT, 8)
        rsel = ea(NT, 2 * NE)
        selm = ea(NT, NE)
        gate = ea(NT, NE)
        ridx = ea(NT, 8)
        rw = ea(NT, 4)
        posr = ea(NT, ROUNDS * NE + 1)
        cnt = ea(NE)
        cmx = ea(2)

        def moe():
            iu = itmp
            with nc.Block() as block:
                def expert_tensor(pe, r, e):
                    i = r * NE + e
                    pe.wait_ge(xg_ready, 8 * i + 8)
                    up_products(pe, moe0, ECH, xg, CAP, FCH + ECH * i, i)
                    gather(pe, i + 1)
                    pe.wait_ge(g_read, FCH + ECH * (i + 1))
                    for j in range(ECH // 2):
                        un = moe0 + ECH + j
                        w = slot(un, (2, D))
                        have(pe, un, i)
                        for q in range(2):
                            f = 2 * j + q
                            for c in range(2):
                                ins = rel.mm(ps[4 + c][0:CAP, :], gE[:, f, :], w[:, q, 512 * c:512 * c + 512],
                                             start=(f == 0), stop=(f == ECH - 1))
                        if j == ECH // 2 - 1:
                            ins.then_inc(y_done, 1)
                        rel.due = True
                    pe.wait_ge(ohg_ready, i + 1)
                    pe.wait_ge(xg_ready, 8 * i + 16)
                    for t in range(NT):
                        n = TILES[t][1]
                        ins = rel.mm(ps[6][0:CAP, P * t:P * t + n], ohg[0:n, t, :], ident[0:n, 0:n], is_transpose=True,
                                     start=True, stop=True)
                    ins.then_inc(ohT_done, 1)
                    pe.wait_ge(ohT_ready, i + 1)
                    pe.wait_ge(y_ready, i + 1)
                    for t in range(NT):
                        n = TILES[t][1]
                        for c in range(2):
                            if t == 0 and c == 0:
                                pe.wait_ge(ohT_ready, i + 1)
                            if 2 * t + c >= 2:
                                pe.wait_ge(sc_added, 6 * i + 2 * t + c)
                            nc.tensor.matmul(ps[6 + c][0:n, :], ohT[0:CAP, t, 0:n], yE[0:CAP, 512 * c:512 * c + 512],
                                             start=True, stop=True).then_inc(sc_done, 1)

                def gather(pe, i):
                    pe.wait_ge(oh_ready, i + 1)
                    for k in range(KD):
                        if k >= 2:
                            pe.wait_ge(xg_ready, 8 * i + k - 1)
                        elif not isinstance(i, int):
                            pe.wait_ge(sc_added, 6 * (i - 1) + 1)
                        for t in range(NT):
                            n = TILES[t][1]
                            ins = rel.mm(ps[6 + k % 2][:, 0:CAP], htok[0:n, t, P * k:P * k + P], oh[0:n, t, :],
                                         start=(t == 0), stop=(t == NT - 1))
                        ins.then_inc(ga_done, 1)

                def expert_scalar(act, r, e):
                    i = r * NE + e
                    base = FCH + ECH * i
                    for m in range(ECH):
                        act.wait_ge(up_done, 2 * (base + m) + 1)
                        act.wait_ge(g_read, base + m - 1)
                        nc.scalar.activation(slE[:, m % 2, :], ps[m % 2][:, 0:CAP], ACT.Silu).then_inc(silu_done, 1)
                    gathered(act, i + 1)
                    act.wait_ge(ohT_done, i + 1)
                    nc.scalar.activation(ohT[0:CAP, 0:2, :], ps[6][0:CAP, 0:256].rearrange("p (t c) -> p t c", t=2), ACT.Copy)
                    nc.scalar.activation(ohT[0:CAP, 2, 0:DEC], ps[6][0:CAP, 256:256 + DEC], ACT.Copy).then_inc(ohT_ready, 1)
                    act.wait_ge(y_done, i + 1)
                    nc.scalar.activation(yE[0:CAP, 0:512], ps[4][0:CAP, :], ACT.Copy)
                    nc.scalar.activation(yE[0:CAP, 512:D], ps[5][0:CAP, :], ACT.Copy).then_inc(y_ready, 1)

                def gathered(act, i):
                    for k in range(KD):
                        act.wait_ge(ga_done, 8 * i + k + 1)
                        nc.scalar.activation(xg[:, k, :], ps[6 + k % 2][:, 0:CAP], ACT.Copy).then_inc(xg_ready, 1)

                def onehot(i):
                    for t in range(NT):
                        n = TILES[t][1]
                        ins = nc.vector.tensor_scalar(oh[0:n, t, :], iota[0:n, :], posr[0:n, t, bass.ds(i, 1)], None, ALU.is_equal)
                    ins.then_inc(oh_ready, 1)

                def expert_vector(dve, r, e):
                    i = r * NE + e
                    base = FCH + ECH * i
                    dve.wait_ge(ga_done, 8 * i + 8)
                    onehot(i + 1)
                    for t in range(NT):
                        n = TILES[t][1]
                        ins = nc.vector.tensor_scalar(ohg[0:n, t, :], iota[0:n, :], posr[0:n, t, bass.ds(i, 1)],
                                                      gate[0:n, t, bass.ds(e, 1)], ALU.is_equal, ALU.mult)
                    ins.then_inc(ohg_ready, 1)
                    for m in range(ECH):
                        dve.wait_ge(up_done, 2 * (base + m) + 2)
                        dve.wait_ge(silu_done, base + m + 1)
                        nc.vector.tensor_tensor(gE[:, m, :], slE[:, m % 2, :], ps[2 + m % 2][:, 0:CAP], ALU.mult
                                                ).then_inc(g_read, 1)
                    for t in range(NT):
                        n = TILES[t][1]
                        for c in range(2):
                            dve.wait_ge(sc_done, 6 * i + 2 * t + c + 1)
                            q = resid[0:n, t, 512 * c:512 * c + 512]
                            nc.vector.tensor_tensor(q, q, ps[6 + c][0:n, :], ALU.add).then_inc(sc_added, 1)

                def expert_loads(sp, r, e, lo):
                    i = r * NE + e
                    for j in range(lo, N_EXP):
                        sp.wait_ge(unit_used, moe0 + N_EXP * i + j - RING + 1)
                        w = [A[x][0, bass.ds(e, 1)].squeeze(0) if not isinstance(e, int) else A[x][0, e]
                             for x in ("moe_w1", "moe_w3", "moe_w2")]
                        dst, src = mlp_loads(moe0, j, *w, D_FFE)
                        sp.dma_start(dst, src).then_inc(slot_full[(moe0 + j) % RING], 16)

                def rounds(eng, body, peel=None):
                    if peel is not None:
                        peel()
                    with eng.Fori(0 if peel is None else 1, NE) as e:
                        body(0, e)
                    eng.wait_ge(flag_ready, 1)
                    more = eng.value_load(iu[0:1, 0:1], min_val=0, max_val=1)
                    with eng.If(more > 0):
                        with eng.Fori(1, ROUNDS) as r:
                            with eng.Fori(0, NE) as e:
                                body(r, e)

                @block.sync
                def _(sp):
                    sp.dma_start(router, A["moe_router"][0].rearrange("(k p) e -> p k e", p=P)).then_inc(lgt_in, 16)
                    rounds(sp, lambda r, e: expert_loads(sp, r, e, 0), lambda: expert_loads(sp, 0, 0, RING - 1))

                @block.tensor
                def _(pe):
                    pe.wait_ge(lgt_in, 16)
                    for i, (t0, n) in enumerate(TILES):
                        for k in range(KD):
                            ins = rel.mm(ps[0][0:n, NE * i:NE * i + NE], hT[:, k, t0:t0 + n], router[:, k, :],
                                         start=(k == 0), stop=(k == KD - 1))
                    ins.then_inc(rt_done, 1)
                    pe.wait_ge(sel_ready, 1)
                    for i, (t0, n) in enumerate(TILES):
                        for j in range(i):
                            nc.tensor.matmul(ps[1][0:n, NE * i:NE * i + NE], ones[:, 0:n], selm[:, j, :], start=(j == 0), stop=False)
                        ins = nc.tensor.matmul(ps[1][0:n, NE * i:NE * i + NE], before[0:n, 0:n], selm[0:n, i, :],
                                               start=(i == 0), stop=True)
                    for i, (t0, n) in enumerate(TILES):
                        ins = nc.tensor.matmul(ps[1][:, 32:32 + NE], ones[0:n, :], selm[0:n, i, :], start=(i == 0), stop=(i == NT - 1))
                    ins.then_inc(pos_done, 1)
                    pe.wait_ge(pos_ready, 1)
                    gather(pe, 0)
                    rounds(pe, lambda r, e: expert_tensor(pe, r, e))

                @block.scalar
                def _(act):
                    act.wait_ge(rt_top, 1)
                    nc.scalar.activation(rw[:, :, 1:2], rw[:, :, 0:1], ACT.Exp).then_inc(rt_exp, 1)
                    gathered(act, 0)
                    rounds(act, lambda r, e: expert_scalar(act, r, e))

                @block.vector
                def _(dve):
                    c = chain(dve, "dve")
                    V = nc.vector
                    c.link(V.memset(rlog, 0.0))
                    dve.wait_ge(rt_done, 1)
                    for i, (t0, n) in enumerate(TILES):
                        ins = V.tensor_copy(rlog[0:n, i, :], ps[0][0:n, NE * i:NE * i + NE])
                    c.link(ins)
                    for i in range(NT):
                        c.link(V.max(rtop[:, i, :], rlog[:, i, :]))
                        c.link(V.max_index(ridx[:, i, :].bitcast(U32), rtop[:, i, :], rlog[:, i, :]))
                    V.tensor_tensor(rw[:, :, 0:1], rtop[:, :, 1:2], rtop[:, :, 0:1], ALU.subtract).then_inc(rt_top, 1)
                    c.link(V.tensor_copy(rtop[:, :, 2:4], ridx[:, :, 0:2].bitcast(U32)))
                    dve.wait_ge(rt_exp, 1)
                    c.link(V.tensor_scalar(rw[:, :, 2:3], rw[:, :, 1:2], 1.0, None, ALU.add))
                    c.link(V.reciprocal(rw[:, :, 2:3], rw[:, :, 2:3]))
                    c.link(V.tensor_tensor(rw[:, :, 3:4], rw[:, :, 2:3], rw[:, :, 1:2], ALU.mult))
                    for i in range(NT):
                        for q in range(2):
                            c.link(V.tensor_scalar(rsel[:, i, NE * q:NE * q + NE], iota[:, 0:NE], rtop[:, i, 2 + q:3 + q], None,
                                                   ALU.is_equal))
                        c.link(V.tensor_tensor(selm[:, i, :], rsel[:, i, 0:NE], rsel[:, i, NE:2 * NE], ALU.add))
                        c.link(V.tensor_scalar(gate[:, i, :], rsel[:, i, 0:NE], rw[:, i, 2:3], None, ALU.mult))
                        ins = V.scalar_tensor_tensor(out=gate[:, i, :], in0=rsel[:, i, NE:2 * NE], scalar=rw[:, i, 3:4],
                                                     in1=gate[:, i, :], op0=ALU.mult, op1=ALU.add)
                        if i < NT - 1:
                            c.link(ins)
                    ins.then_inc(sel_ready, 1)
                    c.link(V.memset(posr, -1.0))
                    dve.wait_ge(pos_done, 1)
                    c.link(V.tensor_reduce(cmx[:, 0:1], ps[1][:, 32:32 + NE], AX.X, ALU.max))
                    c.link(V.tensor_scalar(cmx[:, 1:2], cmx[:, 0:1], float(CAP), None, ALU.is_gt))
                    V.tensor_copy(iu[:, 0:1], cmx[:, 1:2]).then_inc(flag_ready, 1)
                    for i, (t0, n) in enumerate(TILES):
                        c.link(V.scalar_tensor_tensor(out=posr[0:n, i, 0:NE], in0=ps[1][0:n, NE * i:NE * i + NE], scalar=1.0,
                                                      in1=selm[0:n, i, :], op0=ALU.add, op1=ALU.mult))
                        c.link(V.tensor_scalar(posr[0:n, i, 0:NE], posr[0:n, i, 0:NE], -1.0, None, ALU.add))
                        for r in range(1, ROUNDS):
                            c(V.tensor_scalar(posr[0:n, i, NE * r:NE * r + NE], posr[0:n, i, 0:NE], -float(CAP * r), None, ALU.add))
                    c.sync()
                    V.memset(cmx[:, 0:1], 0.0).then_inc(sc_added, 1)
                    V.memset(cnt, 0.0).then_inc(pos_ready, 1)
                    onehot(0)
                    keep(c, "dve")
                    rounds(dve, lambda r, e: expert_vector(dve, r, e))

        norm(0, 0, A["ln_in_g"], A["ln_in_b"])
        calls = 1
        for l in range(DEPTH):
            if upto < 10 * l + 1:
                return
            project(l)
            attend(l)
            delta(l)
            if upto < 10 * l + 2:
                return
            merge(l)
            norm(calls, 1 + 2 * l, A["ln1_g"][l], A["ln1_b"][l], htok if l == 1 else None)
            if upto < 10 * l + 3:
                return
            dense_mlp() if l == 0 else moe()
            norm(calls + 1, 2 + 2 * l, A["ln2_g"][l], A["ln2_b"][l], final=(l == DEPTH - 1))
            calls += 2


_SHAPES = {
    "y_prompt": (1, SEQ, D), "y_sample": (1, DEC, D),
    "new_k_p": (DEPTH, 1, SEQ, A_KV, HD), "new_v_p": (DEPTH, 1, SEQ, A_KV, HD), "new_idx_k_p": (DEPTH, 1, SEQ, HD),
    "new_conv_p": (DEPTH, 1, CW - 1, CCH), "new_gdn_p": (DEPTH, 1, B_HEADS, BD, BD),
    "new_k_s": (DEPTH, 1, DEC, A_KV, HD), "new_v_s": (DEPTH, 1, DEC, A_KV, HD), "new_idx_k_s": (DEPTH, 1, DEC, HD),
    "new_conv_s": (DEPTH, 1, CW - 1, CCH), "new_gdn_s": (DEPTH, 1, B_HEADS, BD, BD),
}


_INS = ["x_prompt", "x_sample", "cache_k", "cache_v", "cache_idx_k", "state_conv", "state_gdn", "ln_in_g", "ln_in_b",
        "w_in", "conv_w", "a_log", "dt_bias", "gnorm_g", "w_oa", "w_ob", "w_out", "ln1_g", "ln1_b", "ln2_g", "ln2_b",
        "ffn_w1", "ffn_w3", "ffn_w2", "moe_router", "moe_w1", "moe_w3", "moe_w2"]


def kernel(**inputs):
    import numpy as np
    import concourse.bacc as bacc
    from concourse.bass_utils import run_bass_kernel_spmd

    nc = bacc.Bacc("TRN2", target_bir_lowering=False, num_devices=1)
    arrays, A, OUT = {}, {}, {}
    for name in _INS:
        a = np.ascontiguousarray(inputs[name])
        arrays[f"in_{name}"] = a
        A[name] = nc.dram_tensor(f"in_{name}", a.shape, mybir.dt.from_np(a.dtype), kind="ExternalInput").ap()
    for name, shape in _SHAPES.items():
        OUT[name] = nc.dram_tensor(f"out_{name}", shape, F32, kind="ExternalOutput").ap()
    program(nc, A, OUT)
    r = run_bass_kernel_spmd(nc, [arrays], core_ids=[0])
    return tuple(r.results[0][f"out_{name}"] for name in _SHAPES)
```

```python
from contextlib import ExitStack

import concourse.bass as bass
from concourse import mybir

F32 = mybir.dt.float32
F32R = mybir.dt.float32r
I32 = mybir.dt.int32
U32 = mybir.dt.uint32
ALU = mybir.AluOpType
ACT = mybir.ActivationFunctionType
AX = mybir.AxisListType

P = 128
D = 1024
KD = D // P
SEQ, DEC, PAST = 256, 32, 256
T = SEQ + DEC
TILES = [(0, 128), (128, 128), (256, DEC)]
NT = len(TILES)
DEPTH = 2
CHUNK = 64
A_HEADS, A_KV, HD = 8, 2, 64
IH = 8
B_HEADS, BD = 4, 128
CW = 4
CCH = 3 * B_HEADS * BD
CT = CCH // P
D_FF, D_FFE, NE = 2816, 3584, 8
ALPHA = (2 * DEPTH) ** 0.25
LN_EPS, RMS_EPS = 1e-5, 1e-6

O_QA = 0
O_KA = O_QA + A_HEADS * HD
O_VA = O_KA + A_KV * HD
O_QI = O_VA + A_KV * HD
O_KI = O_QI + IH * HD
O_WI = O_KI + HD
O_CV = O_WI + IH
O_AB = O_CV + CCH
O_Z = O_AB + 2 * B_HEADS
O_GA = O_Z + B_HEADS * BD
O_GB = O_GA + D

K_CACHE = SEQ
K_SMP = SEQ + PAST
NK = SEQ + PAST + DEC
KEYS = [(0, SEQ), (0, SEQ), (K_CACHE, PAST + DEC)]
NSEL = [min(256, s // 4) for _, s in KEYS]
VT = [[0, 1], [0, 1], [2, 3, 4]]
CI = (CW - 1) + SEQ + (CW - 1) + DEC
CO = CI - (CW - 1)
C_SMP = SEQ + CW - 1
CCOL = [0, 128, C_SMP]
NEG = -3.0e38
TAKEN = -3.4e38

RING, SLOT = 6, 2048
WS = 3
AHEAD = WS - 1
CAP = 128
ROUNDS = -(-T // CAP)


def program(nc, A, OUT, upto=99):
    ctx = ExitStack()
    with ctx:
        def sb(name, shape, dt=F32):
            return ctx.enter_context(nc.sbuf_tensor(name, shape, dt))

        def sem(name):
            return ctx.enter_context(nc.semaphore(name))

        ps = [ctx.enter_context(nc.psum_tensor(f"ps{b}", [P, 512], F32)) for b in range(8)]

        ring = sb("ring", [P, RING * SLOT])
        resid = sb("resid", [P, NT, D])
        hT = sb("hT", [P, KD, T])
        lnp = sb("lnp", [P, 10, KD])
        stats = sb("stats", [P, NT, 2, 6])
        mv = sb("mv", [P, NT, 2])
        std = sb("std", [P, NT])
        rstd = sb("rstd", [P, NT])
        ident = sb("ident", [P, P])
        ones = sb("ones", [P, P])
        cumU = sb("cumU", [P, P])
        blk = sb("blk", [P, P])
        d16 = sb("d16", [P, P])
        off16 = sb("off16", [P, P])
        negL = sb("negL", [P, P])
        negU = sb("negU", [P, P])
        before = sb("before", [P, P])
        iota = sb("iota", [P, CAP])
        itmp = sb("itmp", [P, 320], I32)
        adm = sb("adm", [P, 2, SEQ])
        ndist = sb("ndist", [P, NT, PAST + DEC])
        wsm = sb("wsm", [P, NT, 16])

        def layout(*tensors):
            with ExitStack() as mem:
                return [mem.enter_context(nc.sbuf_tensor(*t)) for t in (t if len(t) == 3 else (*t, F32) for t in tensors)]

        SHARED = (nc.sbuf_usable_end - nc.sbuf_base) // 4 - 64
        ARENA = 20000
        OAB0 = SHARED - 2 * 4 * T
        cT, zT, arena, _, oaT, obT = layout(
            ("cT", [P, CT, CO]),
            ("zT", [P, B_HEADS, T]), ("arena", [P, ARENA]),
            ("pad", [P, OAB0 - CT * CO - B_HEADS * T - ARENA]), ("oaT", [P, 4, T]), ("obT", [P, 4, T]))
        wh, wl, hTh, hTl, oabh, oabl, mTh, mTl, th, mo_ = layout(
            ("wh", [P, WS, SLOT], F32R), ("wl", [P, WS, SLOT], F32R),
            ("hTh", [P, KD, T], F32R), ("hTl", [P, KD, T], F32R), ("oabh", [P, 8, T], F32R), ("oabl", [P, 8, T], F32R),
            ("mTh", [P, KD, T], F32R), ("mTl", [P, KD, T], F32R), ("th", [P, 2, 2 * T]), ("mo_", [P, 2, 2 * T]))
        assert 2 * WS * SLOT + 6 * KD * T + 8 * T <= OAB0
        _, slT, gfull, gTh, gTl = layout(
            ("common", [P, 2 * WS * SLOT + 2 * KD * T]), ("slT", [P, 2, T]), ("gfull", [P, 2, T]),
            ("gTh", [P, D_FF // P, T], F32R), ("gTl", [P, D_FF // P, T], F32R))
        assert 2 * WS * SLOT + (2 * KD + 4 + D_FF // P + 8) * T <= SHARED - 2 * D
        _, xgh, xgl, gEh, gEl, htok, experts = layout(
            ("weights", [P, 2 * WS * SLOT]), ("xgh", [P, KD, CAP], F32R), ("xgl", [P, KD, CAP], F32R),
            ("gEh", [P, D_FFE // P, CAP], F32R), ("gEl", [P, D_FFE // P, CAP], F32R), ("htok", [P, NT, D]),
            ("experts", [P, 4500]))
        _, gb_all = layout(("below", [P, SHARED - 2 * D]), ("gb", [P, 2, D]))

        class Area:
            def __init__(self, where=None):
                self.at, self.where = 0, arena if where is None else where

            def __call__(self, *dims):
                n = 1
                for d in dims:
                    n *= d
                v = self.where[:, self.at:self.at + n]
                self.at += n
                assert self.at <= self.where.shape[1], (self.at, self.where.shape)
                if len(dims) == 2:
                    v = v.rearrange("p (a b) -> p a b", a=dims[0])
                if len(dims) == 3:
                    v = v.rearrange("p (a b c) -> p a b c", a=dims[0], b=dims[1])
                return v

        ar = Area()
        qaT = ar(4, T)
        kT = ar(NK)
        kiT = ar(NK)
        qiT = ar(4, T)
        vtok = ar(5, A_KV * HD)
        ATT0 = ar.at
        cin = ar(CT, CI)
        vT = ar(T)
        ktok = ar(2, A_KV * HD)
        kitok = ar(2, 2 * HD)
        crow = ar(CCH)
        cw = ar(CT, 8)
        last = ar(CT, 6)
        lrow = ar(CCH)
        knew = ar(NT, A_KV * HD)
        inew = ar(NT, HD)

        units = []

        def slot(n, dims):
            s = (n % RING) * SLOT
            size = 1
            for d in dims:
                size *= d
            v = ring[:, s:s + size]
            return v.rearrange("p (a b) -> p a b", a=dims[0])

        def unit(*loads):
            n = len(units)
            units.append(loads)
            return n

        def rows(w):
            return w.rearrange("(k p) n -> p k n", p=P)

        def project_units(l):
            w = rows(A["w_in"][l])
            n0 = len(units)
            for k in (0, 4):
                v = slot(len(units), (4, 512)).rearrange("p k (c a x) -> p k c a x", a=2, x=HD)
                unit(*[(v[:, q, :, a, :], w[:, k + q, O_QA + 256 * a:O_QA + 256 * a + 256]
                        .rearrange("p (c x) -> p c x", x=HD)) for q in range(4) for a in range(2)])
            n = len(units)
            unit((slot(n, (8, 256)), w[:, :, O_KA:O_KA + 256]))
            for k in (0, 4):
                n = len(units)
                unit((slot(n, (4, 512)), w[:, k:k + 4, O_QI:O_QI + 512]))
            n = len(units)
            v = slot(n, (8, 80))
            unit((v[:, :, 0:72], w[:, :, O_KI:O_KI + 72]), (v[:, :, 72:80], w[:, :, O_AB:O_AB + 8]))
            for j in range(6):
                n = len(units)
                unit((slot(n, (8, 256)), w[:, :, O_CV + 256 * j:O_CV + 256 * j + 256]))
            for j in range(2):
                n = len(units)
                unit((slot(n, (8, 256)), w[:, :, O_Z + 256 * j:O_Z + 256 * j + 256]))
            assert n0 % RING < RING - 1 and (n0 + 3) % RING < RING - 1
            return n0

        def merge_units(l):
            w, oa, ob, wo = rows(A["w_in"][l]), rows(A["w_oa"][l]), rows(A["w_ob"][l]), rows(A["w_out"][l])
            n0 = len(units)
            for j in range(4):
                c = 256 * j
                n = len(units)
                unit((slot(n, (8, 256)), w[:, :, O_GA + c:O_GA + c + 256]))
                n = len(units)
                unit((slot(n, (8, 256)), w[:, :, O_GB + c:O_GB + c + 256]))
                n = len(units)
                v = slot(n, (8, 256))
                unit((v[:, 0:4, :], oa[:, :, c:c + 256]), (v[:, 4:8, :], ob[:, :, c:c + 256]))
            for j in range(4):
                n = len(units)
                unit((slot(n, (8, 256)), wo[:, :, 256 * j:256 * j + 256]))
            return n0

        def mlp_loads(n0, j, w1, w3, w2, ff):
            pairs = ff // 256
            if j < 2 * pairs:
                w = (w1, w3)[j % 2]
                c = 256 * (j // 2)
                return slot(n0 + j, (8, 256)), w.rearrange("(k p) n -> p k n", p=P)[:, :, c:c + 256]
            r = 256 * (j - 2 * pairs)
            return slot(n0 + j, (2, D)), w2[r:r + 256, :].rearrange("(k p) n -> p k n", p=P)

        N_PROJ, N_MERGE, N_FFN, N_EXP = 14, 16, 3 * D_FF // 256, 3 * D_FFE // 256
        first = {}
        for l in range(DEPTH):
            first["project", l] = project_units(l)
            first["merge", l] = merge_units(l)
            if l == 0:
                first["mlp", l] = len(units)
                for j in range(N_FFN):
                    unit(mlp_loads(first["mlp", 0], j, A["ffn_w1"][0], A["ffn_w3"][0], A["ffn_w2"][0], D_FF))
        moe0 = first["moe"] = len(units)
        for j in range(N_EXP):
            unit(mlp_loads(moe0, j, A["moe_w1"][0, 0], A["moe_w3"][0, 0], A["moe_w2"][0, 0], D_FFE))
        assert N_EXP % RING == 0

        slot_full = [sem(f"slot_full{s}") for s in range(RING)]
        unit_used = sem("unit_used")
        full_at = []
        count = [0] * RING
        for n, loads in enumerate(units):
            count[n % RING] += 16 * len(loads)
            full_at.append(count[n % RING])
        PER_EXPERT = 16 * N_EXP // RING

        loaded = [0]

        def load_units(sp, used):
            hi = min(used + RING, len(units))
            lo, loaded[0] = loaded[0], hi
            for n in range(lo, hi):
                if n >= RING:
                    sp.wait_ge(unit_used, n - RING + 1)
                for dst, src in units[n]:
                    sp.dma_start(dst, src).then_inc(slot_full[n % RING], 16)

        def have(pe, n, experts=0):
            pe.wait_ge(slot_full[n % RING], experts * PER_EXPERT + full_at[n])

        class Release:
            def __init__(self):
                self.due = None

            def mm(self, *a, **k):
                ins = nc.tensor.matmul(*a, **k)
                if self.due:
                    ins.then_inc(self.due, 1)
                    self.due = None
                return ins
        rel = Release()

        hi_ready, split_free = sem("hi_ready"), sem("split_free")

        def split_index(n):
            return sum(1 for m in range(n) if is_split(m))

        def is_split(m):
            return m >= moe0 or any(first[w, l] <= m < first[w, l] + c
                                    for w, l, c in (("merge", 0, N_MERGE), ("merge", 1, N_MERGE), ("mlp", 0, N_FFN)))

        def split_high(act, n, experts=0):
            k = split_index(n)
            have(act, n, experts)
            if k >= WS:
                act.wait_ge(split_free, k - WS + 1 + N_EXP * experts)
            s = (n % RING) * SLOT
            nc.scalar.activation(wh[:, k % WS, :], ring[:, s:s + SLOT], ACT.Copy).then_inc(hi_ready, 1)

        def split_low(dve, n, experts=0):
            k = split_index(n)
            dve.wait_ge(hi_ready, k + 1 + N_EXP * experts)
            s = (n % RING) * SLOT
            nc.vector.tensor_tensor(wl[:, k % WS, :], ring[:, s:s + SLOT], wh[:, k % WS, :].bitcast(F32), ALU.subtract
                                    ).then_inc(unit_used, 1)

        def halves(n, dims):
            k = split_index(n) % WS
            return [w[:, k, :].rearrange("p (a b) -> p a b", a=dims[0]) for w in (wh, wl)]

        def have_split(pe, n, experts=0):
            pe.wait_ge(unit_used, n + 1 + N_EXP * experts)

        def product(out, terms):
            for k, (a, b) in enumerate(terms):
                for q, (x, y) in enumerate(((a[0], b[0]), (a[0], b[1]), (a[1], b[0]))):
                    ins = rel.mm(out, x, y, start=(k == 0 and q == 0), stop=(k == len(terms) - 1 and q == 2))
            return ins

        x_high, x_low = sem("x_high"), sem("x_low")

        def inputs_high(act, at, pairs):
            for j, (x, h, _) in enumerate(pairs):
                nc.scalar.activation(h, x, ACT.Copy).then_inc(x_high, 1)

        def inputs_low(dve, at, pairs):
            for j, (x, h, l) in enumerate(pairs):
                dve.wait_ge(x_high, at + j + 1)
                nc.vector.tensor_tensor(l, x, h.bitcast(F32), ALU.subtract).then_inc(x_low, 1)

        class Chain:
            def __init__(self, eng, s):
                self.eng, self.s, self.n, self.base = eng, s, 0, 0

            def __call__(self, ins):
                ins.then_inc(self.s, 1)
                self.n += 1

            def sync(self):
                self.eng.wait_ge(self.s, self.base + self.n)

            def link(self, ins):
                self(ins)
                self.sync()

        dve_step, act_step, pool_step = sem("dve_step"), sem("act_step"), sem("pool_step")
        steps = {"dve": 0, "act": 0, "pool": 0}

        def chain(eng, which):
            c = Chain(eng, {"dve": dve_step, "act": act_step, "pool": pool_step}[which])
            c.n = steps[which]
            return c

        def keep(c, which):
            steps[which] = c.n

        x_in, ln_in = sem("x_in"), sem("ln_in")
        const_ready, ln_turned = sem("const_ready"), sem("ln_turned")
        lnrow = arena[0:80, 0:P]
        with nc.Block() as block:
            @block.sync
            def _(sp):
                sp.dma_start(resid[:, 0:2, :], A["x_prompt"][0].rearrange("(i p) d -> p i d", p=P)).then_inc(x_in, 16)
                sp.dma_start(resid[0:DEC, 2, :], A["x_sample"][0]).then_inc(x_in, 16)
                vec = [A["ln_in_g"], A["ln_in_b"]]
                for l in range(DEPTH):
                    vec += [A["ln1_g"][l], A["ln1_b"][l], A["ln2_g"][l], A["ln2_b"][l]]
                for j, v in enumerate(vec):
                    sp.dma_start(arena[KD * j:KD * j + KD, 0:P], v.rearrange("(k p) -> k p", p=P)).then_inc(ln_in, 16)
                load_units(sp, 0)

            @block.gpsimd
            def _(pool):
                c = chain(pool, "pool")
                c.link(nc.gpsimd.memset(ident[:], 0.0))
                c.link(nc.gpsimd.affine_select(out=ident[:], in_=ident[:], compare_op=ALU.not_equal, fill=1.0, base=0,
                                          pattern=[[-1, P]], channel_multiplier=1))
                c.link(nc.gpsimd.memset(mv[:], 1.0))
                c.link(nc.gpsimd.memset(wsm[:], 0.0))
                nc.gpsimd.memset(std[:], 1.0).then_inc(const_ready, 1)
                keep(c, "pool")

            @block.tensor
            def _(pe):
                pe.wait_ge(const_ready, 1)
                pe.wait_ge(ln_in, 160)
                nc.tensor.transpose(ps[0][:, 0:80], lnrow, ident[0:80, 0:80]).then_inc(ln_turned, 1)

            @block.vector
            def _(dve):
                dve.wait_ge(ln_turned, 1)
                dve.wait_ge(x_in, 32)
                c = chain(dve, "dve")
                c.link(nc.vector.tensor_copy(lnp[:], ps[0][:, 0:80].rearrange("p (j k) -> p j k", k=KD)))
                keep(c, "dve")

        masks_ready = sem("masks_ready")

        def masks(pool):
            c = chain(pool, "pool")
            c.link(nc.gpsimd.memset(ones[:], 1.0))
            c.link(nc.gpsimd.memset(cumU[:], 0.0))
            c.link(nc.gpsimd.memset(blk[:], 0.0))
            c.link(nc.gpsimd.memset(negL[:], 0.0))
            c.link(nc.gpsimd.memset(negU[:], 0.0))
            c.link(nc.gpsimd.memset(before[:], 1.0))
            c.link(nc.gpsimd.memset(adm[:], 0.0))
            c.link(nc.gpsimd.memset(d16[:], 0.0))
            c.sync()
            for a in range(0, P, CHUNK):
                s = slice(a, a + CHUNK)
                c.link(nc.gpsimd.memset(cumU[s, s], 1.0))
                c.link(nc.gpsimd.memset(blk[s, s], 1.0))
            for i in range(2):
                for half in range(2):
                    k0 = (2 * i + half + 1) * CHUNK
                    if k0 < SEQ:
                        c.link(nc.gpsimd.memset(adm[half * CHUNK:half * CHUNK + CHUNK, i, k0:SEQ], NEG))
            c.link(nc.gpsimd.affine_select(out=before[:], in_=before[:], compare_op=ALU.is_gt, fill=0.0, base=0,
                                      pattern=[[1, P]], channel_multiplier=-1))
            c.sync()
            c.link(nc.gpsimd.memset(d16[:], 1.0))
            d16v = d16[:].rearrange("p (b c) -> p b c", c=16)
            c.link(nc.gpsimd.affine_select(out=d16v, in_=d16v, compare_op=ALU.is_ge, fill=0.0, base=0,
                                           pattern=[[-16, 8], [0, 16]], channel_multiplier=1))
            c.link(nc.gpsimd.affine_select(out=d16v, in_=d16v, compare_op=ALU.is_ge, fill=0.0, base=15,
                                           pattern=[[16, 8], [0, 16]], channel_multiplier=-1))
            c.link(nc.gpsimd.affine_select(out=d16[:], in_=d16[:], compare_op=ALU.is_gt, fill=0.0, base=0,
                                           pattern=[[-1, P]], channel_multiplier=1))
            c.link(nc.gpsimd.affine_select(out=cumU[:], in_=cumU[:], compare_op=ALU.is_ge, fill=0.0, base=0,
                                           pattern=[[1, P]], channel_multiplier=-1))
            c.link(nc.gpsimd.affine_select(out=off16[:], in_=blk[:], compare_op=ALU.is_gt, fill=0.0, base=0,
                                           pattern=[[-1, P]], channel_multiplier=1))
            c.link(nc.gpsimd.tensor_tensor(off16[:], off16[:], d16[:], ALU.subtract))
            c.link(nc.gpsimd.affine_select(out=negL[:], in_=blk[:], compare_op=ALU.is_ge, fill=0.0, base=0,
                                           pattern=[[-1, P]], channel_multiplier=1))
            c.link(nc.gpsimd.tensor_scalar(negL[:], negL[:], 1.0, 1e30, ALU.subtract, ALU.mult))
            c.link(nc.gpsimd.tensor_scalar(negU[:], cumU[:], 1.0, 1e30, ALU.subtract, ALU.mult))
            c.link(nc.gpsimd.iota(itmp[:, 0:CAP], pattern=[[1, CAP]], base=0, channel_multiplier=0))
            c.link(nc.gpsimd.tensor_copy(iota[:], itmp[:, 0:CAP]))
            for i in range(NT):
                c.link(nc.gpsimd.iota(itmp[:, 0:PAST + DEC], pattern=[[1, PAST + DEC]], base=-TILES[i][0],
                                      channel_multiplier=-1))
                c.link(nc.gpsimd.tensor_copy(ndist[:, i, :], itmp[:, 0:PAST + DEC]))
            nc.gpsimd.memset(std[:], 1.0).then_inc(masks_ready, 1)
            keep(c, "pool")

        gb_in = sem("gb_in")
        var_ready, std_ready, hat_ready = sem("var_ready"), sem("std_ready"), sem("hat_ready")
        nrm_turned, stream_done, out_stored = sem("nrm_turned"), sem("stream_done"), sem("out_stored")

        def norm(call, j, g_vec, b_vec, keep_h=None, final=False):
            gb = gb_all
            whole = final or keep_h is not None
            src = resid if keep_h is None else keep_h
            with nc.Block() as block:
                @block.sync
                def _(sp):
                    sp.dma_start(gb[:, 0, :], g_vec.partition_broadcast(P)).then_inc(gb_in, 16)
                    sp.dma_start(gb[:, 1, :], b_vec.partition_broadcast(P)).then_inc(gb_in, 16)
                    if final:
                        for i in range(2):
                            sp.wait_ge(hat_ready, NT * call + i + 1)
                            sp.dma_start(OUT["y_prompt"][0, P * i:P * i + P, :], resid[:, i, :]).then_inc(out_stored, 16)
                        sp.wait_ge(hat_ready, NT * (call + 1))
                        sp.dma_start(OUT["y_sample"][0], resid[0:DEC, 2, :]).then_inc(out_stored, 16)
                        sp.wait_ge(out_stored, 48)

                @block.vector
                def _(dve):
                    c = chain(dve, "dve")
                    for i, (t0, n) in enumerate(TILES):
                        for a in range(2):
                            c(nc.vector.bn_stats(stats[0:n, i, a, :], resid[0:n, i, 512 * a:512 * a + 512]))
                    for i, (t0, n) in enumerate(TILES):
                        c.sync() if i == 0 else None
                        c(nc.vector.bn_aggr(mv[0:n, i, :], stats[0:n, i, :, :].rearrange("p a b -> p (a b)")))
                    c.sync()
                    nc.vector.tensor_scalar(rstd[:], mv[:, :, 1], LN_EPS, None, ALU.add).then_inc(var_ready, 1)
                    if whole:
                        dve.wait_ge(gb_in, 32 * (call + 1))
                        for i, (t0, n) in enumerate(TILES):
                            c(nc.vector.scalar_tensor_tensor(out=src[0:n, i, :], in0=resid[0:n, i, :], scalar=mv[0:n, i, 0:1],
                                                             in1=gb[0:n, 0, :], op0=ALU.subtract, op1=ALU.mult))
                    dve.wait_ge(std_ready, call + 1)
                    c.link(nc.vector.reciprocal(rstd[:], std[:]))
                    for i, (t0, n) in enumerate(TILES):
                        if whole:
                            ins = nc.vector.scalar_tensor_tensor(out=src[0:n, i, :], in0=src[0:n, i, :], scalar=rstd[0:n, i:i + 1],
                                                                 in1=gb[0:n, 1, :], op0=ALU.mult, op1=ALU.add)
                        else:
                            ins = nc.vector.tensor_scalar(resid[0:n, i, :], resid[0:n, i, :], mv[0:n, i, 0:1],
                                                          rstd[0:n, i:i + 1], ALU.subtract, ALU.mult)
                        ins.then_inc(hat_ready, 1)
                    for k in range(1, 0 if final else KD, 2):
                        dve.wait_ge(nrm_turned, KD * call + k + 1)
                        if whole:
                            nc.vector.tensor_copy(hT[:, k, :], ps[k][:, 0:T])
                        else:
                            nc.vector.tensor_scalar(hT[:, k, :], ps[k][:, 0:T], lnp[:, 2 * j, k:k + 1],
                                                    lnp[:, 2 * j + 1, k:k + 1], ALU.mult, ALU.add)
                    keep(c, "dve")

                @block.scalar
                def _(act):
                    act.wait_ge(var_ready, call + 1)
                    nc.scalar.activation(std[:], rstd[:], ACT.Sqrt).then_inc(std_ready, 1)
                    for k in range(0, 0 if final else KD, 2):
                        act.wait_ge(nrm_turned, KD * call + k + 1)
                        if whole:
                            nc.scalar.activation(hT[:, k, :], ps[k][:, 0:T], ACT.Copy)
                        else:
                            nc.scalar.activation(hT[:, k, :], ps[k][:, 0:T], ACT.Identity,
                                                 bias=lnp[:, 2 * j + 1, k:k + 1], scale=lnp[:, 2 * j, k:k + 1])

                @block.tensor
                def _(pe):
                    for k in range(0 if final else KD):
                        for i, (t0, n) in enumerate(TILES):
                            if k == 0:
                                pe.wait_ge(hat_ready, NT * call + i + 1)
                            ins = nc.tensor.transpose(ps[k][:, t0:t0 + n], src[0:n, i, 128 * k:128 * k + 128], ident[0:n, 0:n])
                        ins.then_inc(nrm_turned, 1)

        def finish_stream(pool, call):
            c = chain(pool, "pool")
            pool.wait_ge(gb_in, 32 * (call + 1))
            for i, (t0, n) in enumerate(TILES):
                r = resid[0:n, i, :]
                c.link(nc.gpsimd.tensor_tensor(r, r, gb_all[0:n, 0, :], ALU.mult))
                c.link(nc.gpsimd.tensor_tensor(r, r, gb_all[0:n, 1, :], ALU.add))
                c.link(nc.gpsimd.tensor_scalar(r, r, ALPHA, None, ALU.mult))
            nc.gpsimd.memset(std[:], 1.0).then_inc(stream_done, 1)
            keep(c, "pool")

        mix_in, pre_turned, pre_evac = sem("mix_in"), sem("pre_turned"), sem("pre_evac")
        pj_done, pj_evac, conv_ready, silu_ready = sem("pj_done"), sem("pj_evac"), sem("conv_ready"), sem("silu_ready")
        post_turned, post_evac, new_stored, last_ready = sem("post_turned"), sem("post_evac"), sem("new_stored"), sem("last_ready")
        N_CH = 28

        def project(l):
            u0 = first["project", l]
            with nc.Block() as block:
                @block.sync
                def _(sp):
                    load_units(sp, u0 + N_PROJ - 1)
                    sp.wait_ge(post_evac, 6 * (l + 1))
                    for name, src, w in (("k", knew, 2 * HD), ("v", None, 2 * HD), ("idx_k", inew, HD)):
                        op, os = OUT[f"new_{name}_p"][l, 0], OUT[f"new_{name}_s"][l, 0]
                        if name != "idx_k":
                            op, os = op.rearrange("t g d -> t (g d)"), os.rearrange("t g d -> t (g d)")
                        main = vtok[:, 0:2, :] if src is None else src[:, 0:2, :]
                        tail = vtok[0:DEC, 4, :] if src is None else src[0:DEC, 2, :]
                        sp.dma_start(op.rearrange("(i p) c -> p i c", p=P), main).then_inc(new_stored, 16)
                        sp.dma_start(os, tail).then_inc(new_stored, 16)
                    sp.dma_start(OUT["new_conv_p"][l, 0], lrow[0:3, :]).then_inc(new_stored, 16)
                    sp.dma_start(OUT["new_conv_s"][l, 0], lrow[3:6, :]).then_inc(new_stored, 16)
                    sp.wait_ge(new_stored, 160 * l + 128)

                @block.scalar
                def _(act):
                    act.dma_start(crow[0:CW, :], A["conv_w"][l]).then_inc(mix_in, 16)
                    act.dma_start(crow[CW:CW + 3, :], A["state_conv"][l, 0]).then_inc(mix_in, 16)
                    act.dma_start(ktok, A["cache_k"][l, 0].rearrange("(i p) g d -> p i (g d)", p=P)).then_inc(mix_in, 16)
                    act.dma_start(vtok[:, 2:4, :], A["cache_v"][l, 0].rearrange("(i p) g d -> p i (g d)", p=P)).then_inc(mix_in, 16)
                    for a in range(2):
                        act.dma_start(kitok[:, :, HD * a:HD * a + HD], A["cache_idx_k"][l, 0].rearrange("(i p) d -> p i d", p=P)
                                      ).then_inc(mix_in, 16)

                    def split(dst, src, at, smp, func=ACT.Copy):
                        nc.scalar.activation(dst[:, at:at + SEQ], src[:, 0:SEQ], func)
                        return nc.scalar.activation(dst[:, smp:smp + DEC], src[:, SEQ:T], func)

                    def silu(j):
                        act.wait_ge(conv_ready, CT * l + j + 1)
                        nc.scalar.activation(cT[:, j, :], cT[:, j, :], ACT.Silu).then_inc(silu_ready, 1)
                    for m in range(N_CH):
                        act.wait_ge(pj_done, N_CH * l + m + 1)
                        src = ps[m % 4][:, 0:T]
                        if m < 4:
                            ins = nc.scalar.activation(qaT[:, m, :], src, ACT.Copy, scale=HD ** -0.5)
                        elif m == 4:
                            ins = split(kT, src, 0, K_SMP)
                        elif m == 5:
                            ins = nc.scalar.activation(vT, src, ACT.Copy)
                        elif m < 10:
                            ins = nc.scalar.activation(qiT[:, m - 6, :], src, ACT.Copy)
                        elif m == 10:
                            ins = split(kiT, src, 0, K_SMP)
                        elif m == 11:
                            for i, (t0, n) in enumerate(TILES):
                                ins = nc.scalar.activation(wsm[0:n, i, :], ps[m % 4][0:n, 16 * i:16 * i + 16], ACT.Copy)
                        elif m < 24:
                            j = m - 12
                            ins = split(cin[:, j, :], src, CW - 1, 2 * (CW - 1) + SEQ)
                        else:
                            ins = nc.scalar.activation(zT[:, m - 24, :], src, ACT.Silu)
                        ins.then_inc(pj_evac, 1)
                        if m >= 16:
                            silu(m - 16)

                @block.tensor
                def _(pe):
                    def product(m, lhs, unit_of, last_use):
                        if m >= 4:
                            pe.wait_ge(pj_evac, N_CH * l + m - 3)
                        for k in range(KD):
                            if unit_of(k) is not None:
                                have(pe, unit_of(k))
                            ins = rel.mm(ps[m % 4][:, 0:T], lhs(k), hT[:, k, :], start=(k == 0), stop=(k == KD - 1))
                            if last_use and k == 3 and last_use == "pair":
                                rel.due = unit_used
                        ins.then_inc(pj_done, 1)
                        if last_use:
                            rel.due = unit_used

                    def pairview(n):
                        s = (n % RING) * SLOT
                        return ring[:, s:s + 2 * SLOT].rearrange("p (k c) -> p k c", c=512)
                    qw = pairview(u0)
                    for c in range(4):
                        product(c, lambda k: qw[:, k, P * c:P * c + P], lambda k: u0 + k // 4 if c == 0 and k % 4 == 0 else None, "pair" if c == 3 else "")
                    pe.wait_ge(mix_in, 96 * (l + 1))
                    for j in range(CT):
                        ins = nc.tensor.transpose(ps[4][:, 8 * j:8 * j + 7], crow[0:7, P * j:P * j + P], ident[0:7, 0:7])
                    for i in range(2):
                        nc.tensor.transpose(ps[5][:, P * i:P * i + P], ktok[:, i, :], ident[:])
                    for i in range(2):
                        ins = nc.tensor.transpose(ps[5][:, 256 + P * i:256 + P * i + P], kitok[:, i, :], ident[:])
                    ins.then_inc(pre_turned, 1)
                    kv = slot(u0 + 2, (8, 256))
                    for c in range(2):
                        product(4 + c, lambda k: kv[:, k, P * c:P * c + P], lambda k: u0 + 2 if k == 0 else None, c == 1)
                    iw = pairview(u0 + 3)
                    for c in range(4):
                        product(6 + c, lambda k: iw[:, k, P * c:P * c + P],
                                lambda k: u0 + 3 + k // 4 if c == 0 and k % 4 == 0 else None, "pair" if c == 3 else "")
                    sw = slot(u0 + 5, (8, 80))
                    pe.wait_ge(pj_evac, N_CH * l + 10 - 3)
                    have(pe, u0 + 5)
                    for half in range(2):
                        for k in range(KD):
                            ins = rel.mm(ps[10 % 4][64 * half:64 * half + 64, 0:T], sw[:, k, 0:HD], hT[:, k, :],
                                         start=(k == 0), stop=(k == KD - 1))
                    ins.then_inc(pj_done, 1)
                    pe.wait_ge(pj_evac, N_CH * l + 11 - 3)
                    for i, (t0, n) in enumerate(TILES):
                        for k in range(KD):
                            ins = rel.mm(ps[11 % 4][0:n, 16 * i:16 * i + 16], hT[:, k, t0:t0 + n], sw[:, k, HD:80],
                                         start=(k == 0), stop=(k == KD - 1))
                    ins.then_inc(pj_done, 1)
                    rel.due = unit_used
                    for j in range(8):
                        n = u0 + 6 + j
                        w = slot(n, (8, 256))
                        for c in range(2):
                            product(12 + 2 * j + c, lambda k: w[:, k, P * c:P * c + P], lambda k: n if k == 0 else None, c == 1)
                    for i, (t0, n) in enumerate(TILES):
                        ins = rel.mm(ps[5][0:n, P * i:P * i + P], vT[:, t0:t0 + n], ident[:], is_transpose=True,
                                     start=True, stop=True)
                    ins.then_inc(post_turned, 1)
                    for i, (t0, n) in enumerate(TILES):
                        k0 = t0 if i < 2 else K_SMP
                        ins = nc.tensor.transpose(ps[6][0:n, P * i:P * i + P], kT[:, k0:k0 + n], ident[:])
                    ins.then_inc(post_turned, 1)
                    for i, (t0, n) in enumerate(TILES):
                        k0 = t0 if i < 2 else K_SMP
                        ins = nc.tensor.transpose(ps[7][0:n, HD * i:HD * i + HD], kiT[0:HD, k0:k0 + n], ident[0:HD, 0:HD])
                    ins.then_inc(post_turned, 1)
                    pe.wait_ge(last_ready, l + 1)
                    pe.wait_ge(pj_evac, N_CH * l + 24)
                    for g, b in enumerate((4, 0, 1)):
                        if b < 4:
                            pe.wait_ge(pj_evac, N_CH * l + 25 + b)
                        for j in range(4):
                            ins = nc.tensor.transpose(ps[b][0:6, P * j:P * j + P], last[:, 4 * g + j, :], ident[:])
                        ins.then_inc(post_turned, 1)

                @block.gpsimd
                def _(pool):
                    if l == 0:
                        masks(pool)
                    finish_stream(pool, 2 * l)

                @block.vector
                def _(dve):
                    c = chain(dve, "dve")
                    nc.vector.memset(cin[:, :, 0:3], 0.0).then_inc(pre_evac, 1)
                    dve.wait_ge(pre_turned, l + 1)
                    cwv = ps[4][:, 0:8 * CT].rearrange("p (j a) -> p j a", a=8)
                    c(nc.vector.tensor_copy(cw[:, :, 0:7], cwv[:, :, 0:7]))
                    nc.vector.tensor_copy(cin[:, :, CW - 1 + SEQ:2 * (CW - 1) + SEQ], cwv[:, :, CW:CW + 3]).then_inc(pre_evac, 1)
                    nc.vector.tensor_copy(kT[:, K_CACHE:K_SMP], ps[5][:, 0:256]).then_inc(pre_evac, 1)
                    nc.vector.tensor_copy(kiT[:, K_CACHE:K_SMP], ps[5][:, 256:512]).then_inc(pre_evac, 1)
                    dve.wait_ge(pre_evac, 4 * (l + 1))
                    c.sync()
                    for j in range(CT):
                        dve.wait_ge(pj_evac, N_CH * l + 12 + j + 1)
                        for a in range(CW):
                            tap = cw[:, j, a:a + 1]
                            src = cin[:, j, a:a + CO]
                            if a == 0:
                                c.link(nc.vector.tensor_scalar(cT[:, j, :], src, tap, None, ALU.mult))
                            else:
                                ins = nc.vector.scalar_tensor_tensor(out=cT[:, j, :], in0=src, scalar=tap, in1=cT[:, j, :],
                                                                     op0=ALU.mult, op1=ALU.add)
                                if a < CW - 1:
                                    c.link(ins)
                                else:
                                    ins.then_inc(conv_ready, 1)
                        nc.vector.tensor_copy(last[:, j, 0:3], cin[:, j, SEQ:SEQ + 3])
                        ins = nc.vector.tensor_copy(last[:, j, 3:6], cin[:, j, CI - 3:CI])
                    ins.then_inc(last_ready, 1)
                    dve.wait_ge(post_turned, 6 * l + 1)
                    nc.vector.tensor_copy(vtok[:, 0:2, :], ps[5][:, 0:256].rearrange("p (i c) -> p i c", i=2))
                    nc.vector.tensor_copy(vtok[0:DEC, 4, :], ps[5][0:DEC, 256:384]).then_inc(post_evac, 1)
                    dve.wait_ge(post_turned, 6 * l + 2)
                    nc.vector.tensor_copy(knew[:, 0:2, :], ps[6][:, 0:256].rearrange("p (i c) -> p i c", i=2))
                    nc.vector.tensor_copy(knew[0:DEC, 2, :], ps[6][0:DEC, 256:384]).then_inc(post_evac, 1)
                    dve.wait_ge(post_turned, 6 * l + 3)
                    nc.vector.tensor_copy(inew[:, 0:2, :], ps[7][:, 0:128].rearrange("p (i c) -> p i c", i=2))
                    nc.vector.tensor_copy(inew[0:DEC, 2, :], ps[7][0:DEC, 128:192]).then_inc(post_evac, 1)
                    for g, b in enumerate((4, 0, 1)):
                        dve.wait_ge(post_turned, 6 * l + 4 + g)
                        nc.vector.tensor_copy(lrow[0:6, 512 * g:512 * g + 512], ps[b][0:6, :]).then_inc(post_evac, 1)
                    if l == 0:
                        dve.wait_ge(masks_ready, 1)
                        c.link(nc.vector.scalar_tensor_tensor(out=ndist[:], in0=ndist[:], scalar=-1.0, in1=ndist[:],
                                                              op0=ALU.mult, op1=ALU.min))
                    keep(c, "dve")

        idx_done, relu_done, score_ready = sem("idx_done"), sem("relu_done"), sem("score_ready")
        lg_done, lg_ready, nm_ready, exp_done = sem("lg_done"), sem("lg_ready"), sem("nm_ready"), sem("exp_done")
        p_ready, pt_done, pt_evac, pv_done, oa_ready = sem("p_ready"), sem("pt_done"), sem("pt_evac"), sem("pv_done"), sem("oa_ready")
        at_ = Area()
        at_.at = ATT0
        SMAX = PAST + DEC
        relu = at_(IH, SMAX)
        lg = at_(A_HEADS, SMAX)
        prob = at_(A_HEADS, SMAX)
        probT = at_(3, A_HEADS * P)
        score = at_(SMAX)
        top8 = at_(8)
        away = at_(SMAX)
        pen = at_(2, SMAX)
        mx = at_(A_HEADS)
        nmx = at_(A_HEADS)
        den = at_(A_HEADS)
        rden = at_(A_HEADS)
        wis = at_(NT, IH)
        PT_OF = [2 * len(v) for v in VT]
        PT0 = [sum(PT_OF[:i]) for i in range(NT + 1)]

        def attend(l):
            def b8(i, h):
                return (l * NT + i) * 8 + h
            with nc.Block() as block:
                @block.tensor
                def _(pe):
                    def indexer(i):
                        (t0, n), (k0, s) = TILES[i], KEYS[i]
                        for h in range(IH):
                            if h >= 4:
                                pe.wait_ge(relu_done, b8(i, h) - 3)
                            elif i:
                                pe.wait_ge(relu_done, b8(i - 1, 8))
                            r = slice(HD * (h % 2), HD * (h % 2) + HD)
                            nc.tensor.matmul(ps[h % 4][0:n, 0:s], qiT[r, h // 2, t0:t0 + n], kiT[r, k0:k0 + s],
                                             start=True, stop=True).then_inc(idx_done, 1)

                    def logits(i):
                        (t0, n), (k0, s) = TILES[i], KEYS[i]
                        for h in range(A_HEADS):
                            if h >= 4:
                                pe.wait_ge(lg_ready, b8(i, h) - 3)
                            elif i:
                                pe.wait_ge(oa_ready, l * NT + i)
                            r = slice(HD * (h // 4), HD * (h // 4) + HD)
                            nc.tensor.matmul(ps[4 + h % 4][0:n, 0:s], qaT[r, h % 4, t0:t0 + n], kT[r, k0:k0 + s],
                                             start=True, stop=True).then_inc(lg_done, 1)

                    def turn(i):
                        (t0, n), (k0, s) = TILES[i], KEYS[i]
                        pe.wait_ge(p_ready, l * NT + i + 1)
                        for g in range(PT_OF[i]):
                            ck, j = g // 2, g % 2
                            kc = min(P, s - P * ck)
                            if g >= 4:
                                pe.wait_ge(pt_evac, l * PT0[NT] + PT0[i] + g - 3)
                            else:
                                pe.wait_ge(relu_done, b8(min(i + 1, NT - 1), 8))
                            for q in range(4):
                                ins = nc.tensor.transpose(ps[g % 4][0:kc, n * q:n * q + n],
                                                          prob[0:n, 4 * j + q, P * ck:P * ck + kc], ident[0:n, 0:n])
                            ins.then_inc(pt_done, 1)

                    def values(i):
                        (t0, n), (k0, s) = TILES[i], KEYS[i]
                        pe.wait_ge(pt_evac, l * PT0[NT] + PT0[i + 1])
                        pe.wait_ge(lg_ready, b8(i, 8))
                        for h in range(A_HEADS):
                            r = slice(HD * (h % 2), HD * (h % 2) + HD)
                            g = h // 4
                            for ck, vt in enumerate(VT[i]):
                                kc = min(P, s - P * ck)
                                ins = nc.tensor.matmul(ps[4][r, (h // 2) * P:(h // 2) * P + n], vtok[0:kc, vt, HD * g:HD * g + HD],
                                                       probT[0:kc, ck, n * h:n * h + n], start=(ck == 0),
                                                       stop=(ck == len(VT[i]) - 1))
                        ins.then_inc(pv_done, 1)

                    indexer(0)
                    for i in range(NT):
                        logits(i)
                        if i + 1 < NT:
                            if i:
                                pe.wait_ge(pt_evac, l * PT0[NT] + PT0[i])
                            indexer(i + 1)
                        turn(i)
                        values(i)

                @block.scalar
                def _(act):
                    def relus(i):
                        (t0, n), (k0, s) = TILES[i], KEYS[i]
                        if i or l:
                            act.wait_ge(score_ready, l * NT + i)
                        for h in range(IH):
                            act.wait_ge(idx_done, b8(i, h) + 1)
                            nc.scalar.activation(relu[0:n, h, 0:s], ps[h % 4][0:n, 0:s], ACT.Relu).then_inc(relu_done, 1)
                    relus(0)
                    for i in range(NT):
                        (t0, n), (k0, s) = TILES[i], KEYS[i]
                        if i + 1 < NT:
                            relus(i + 1)
                        act.wait_ge(nm_ready, l * NT + i + 1)
                        if i:
                            act.wait_ge(pt_done, l * PT0[NT] + PT0[i])
                        for h in range(A_HEADS):
                            nc.scalar.activation(prob[0:n, h, 0:s], lg[0:n, h, 0:s], ACT.Exp, bias=nmx[0:n, h:h + 1],
                                                 accum_out=den[0:n, h:h + 1]).then_inc(exp_done, 1)
                        for g in range(PT_OF[i]):
                            ck, j = g // 2, g % 2
                            kc = min(P, s - P * ck)
                            act.wait_ge(pt_done, l * PT0[NT] + PT0[i] + g + 1)
                            if i and g == 0:
                                act.wait_ge(pv_done, l * NT + i)
                            nc.scalar.activation(probT[0:kc, ck, 4 * j * n:4 * j * n + 4 * n], ps[g % 4][0:kc, 0:4 * n],
                                                 ACT.Copy).then_inc(pt_evac, 1)
                        act.wait_ge(pv_done, l * NT + i + 1)
                        nc.scalar.activation(oaT[:, :, t0:t0 + n], ps[4][:, :].rearrange("p (c t) -> p c t", c=4)[:, :, 0:n],
                                             ACT.Copy).then_inc(oa_ready, 1)

                @block.vector
                def _(dve):
                    c = chain(dve, "dve")
                    c.link(nc.vector.tensor_scalar(wis, wsm[:, :, 0:IH], HD ** -0.5, None, ALU.mult))

                    def choose(i):
                        (t0, n), (k0, s) = TILES[i], KEYS[i]
                        sc = score[0:n, 0:s]
                        for h in range(IH):
                            dve.wait_ge(relu_done, b8(i, h) + 1)
                            w = wis[0:n, i, h:h + 1]
                            if h == 0:
                                c.link(nc.vector.tensor_scalar(sc, relu[0:n, h, 0:s], w, None, ALU.mult))
                            else:
                                ins = nc.vector.scalar_tensor_tensor(out=sc, in0=relu[0:n, h, 0:s], scalar=w, in1=sc,
                                                                     op0=ALU.mult, op1=ALU.add)
                                if h < IH - 1:
                                    c.link(ins)
                                else:
                                    ins.then_inc(score_ready, 1)
                        dve.wait_ge(score_ready, l * NT + i + 1)
                        if i < 2:
                            c.link(nc.vector.tensor_tensor(sc, sc, adm[0:n, i, 0:s], ALU.add))
                        assert NSEL[i] % 8 == 0
                        for _ in range(NSEL[i] // 8):
                            c.link(nc.vector.max(top8[0:n], sc))
                            c.link(nc.vector.match_replace(out=sc, in_to_replace=top8[0:n], in_values=sc, imm_value=TAKEN))
                        c.link(nc.vector.tensor_scalar(away[0:n, 0:s], sc, TAKEN, -1e30, ALU.not_equal, ALU.mult))

                    choose(0)
                    for i in range(NT):
                        (t0, n), (k0, s) = TILES[i], KEYS[i]
                        if i:
                            dve.wait_ge(exp_done, b8(i - 1, 8))
                        for h in range(A_HEADS):
                            c.link(nc.vector.scalar_tensor_tensor(out=pen[0:n, h % 2, 0:s], in0=ndist[0:n, i, 0:s],
                                                                  scalar=2.0 ** -(h + 1), in1=away[0:n, 0:s],
                                                                  op0=ALU.mult, op1=ALU.add))
                            dve.wait_ge(lg_done, b8(i, h) + 1)
                            nc.vector.tensor_tensor(lg[0:n, h, 0:s], ps[4 + h % 4][0:n, 0:s], pen[0:n, h % 2, 0:s],
                                                    ALU.add).then_inc(lg_ready, 1)
                        dve.wait_ge(lg_ready, b8(i, 8))
                        c.link(nc.vector.tensor_reduce(mx[0:n], lg[0:n, :, 0:s], AX.X, ALU.max))
                        nc.vector.tensor_scalar(nmx[0:n], mx[0:n], -1.0, None, ALU.mult).then_inc(nm_ready, 1)
                        if i + 1 < NT:
                            choose(i + 1)
                        dve.wait_ge(exp_done, b8(i, 8))
                        c.link(nc.vector.reciprocal(rden[0:n], den[0:n]))
                        for h in range(A_HEADS):
                            ins = nc.vector.tensor_scalar(prob[0:n, h, 0:s], prob[0:n, h, 0:s], rden[0:n, h:h + 1], None,
                                                          ALU.mult)
                        ins.then_inc(p_ready, 1)
                    keep(c, "dve")

        PREP = ["norm", "qk", "v", "grow", "qT", "kT", "qdT", "KK", "QKT", "MdT", "MoT", "P2", "P2T", "X1", "P4", "P4T",
                "X2", "P8", "X3", "X3T", "B", "BT", "Y1", "B2", "TT", "u", "wT"]
        BY_DVE = {"norm", "qk", "v", "grow", "KK", "QKT", "X1", "X2", "X3", "Y1", "TT"}
        RN = {r: k for k, r in enumerate(PREP)}
        DV = [r for r in PREP if r in BY_DVE]
        AC = [r for r in PREP if r not in BY_DVE]
        dl_in, sq_ready, g_ready, beta_ready = sem("dl_in"), sem("sq_ready"), sem("g_ready"), sem("beta_ready")
        prep_done, prep_dve, prep_act = sem("prep_done"), sem("prep_dve"), sem("prep_act")
        sm_dve, sm_act, egl_done, egl_ready = sem("sm_dve"), sem("sm_act"), sem("egl_done"), sem("egl_ready")
        dec_in, dec_ready, x_ready = sem("dec_in"), sem("dec_ready"), sem("x_ready")
        ws_done, vnew_ready, o_done, o_ready = sem("ws_done"), sem("vnew_ready"), sem("o_done"), sem("o_ready")
        ds_done, s_ready, on_ready, ot_done, ob_ready = (sem("ds_done"), sem("s_ready"), sem("on_ready"), sem("ot_done"),
                                                         sem("ob_ready"))
        ssq_ready, rn_ready = sem("ssq_ready"), sem("rn_ready")
        H4 = B_HEADS
        da = Area()
        sq = da(2 * H4, CO)
        SQ_END = da.at
        da.at = 0
        USES = [("q", "Md", "P4T", "XT", "vnew"), ("k", "Mo", "X", "TT"), ("qd", "MdT", "u"),
                ("gtri", "qT", "PT", "P8", "B2", "on"), ("kT", "P", "BT", "o"), ("E", "MoT", "wT"), ("ET", "P4", "B"),
                ("QKT",), ("qdT",), ("kbG",), ("kt",), ("vb",)]
        WIDE = {"q", "k", "qd", "u", "vnew", "o", "on", "kbG", "kt", "vb"}
        tl = []
        for i in range(NT):
            n = TILES[i][1]
            d = {}
            for names in USES:
                at = da.at
                da.at += H4 * (BD if WIDE & set(names) else n)
                for x in names:
                    w = BD if x in WIDE else n
                    d[x] = arena[:, at:at + H4 * w].rearrange("p (h x) -> p h x", h=H4)
            tl.append(d)
        osq = da(H4, BD)
        da.at = max(da.at, SQ_END)
        state = da(2, H4 * BD).rearrange("p s (h v) -> p s h v", h=H4)
        prm = da(2, H4)
        gn = da(2)
        sp_ = da(3, NT * H4).rearrange("p a (i h) -> p a i h", i=NT)
        gv = da(NT, H4)
        nG = da(NT, H4)
        nbeta = da(NT, H4)
        nrm16 = da(NT, 16)
        sc = da(NT, 6 * H4).rearrange("p i (a h) -> p i a h", a=6)
        eg = da(5, H4)
        rr = da(NT, H4)
        SC_Q, SC_QD, SC_K, SC_KBG, SC_KT, SC_VB = range(6)
        SEQS = [(0, 0, 0, 0), (2, 0, 1, 4), (0, 64, 0, 1), (1, 0, 0, 2), (1, 64, 0, 3)]

        def delta(l):
            NR = len(PREP)
            sb_ = l * NT

            def at_round(r, i):
                return (l * NR + RN[r]) * NT + i + 1

            def evac_of(r, i):
                if r in BY_DVE:
                    return prep_dve, (l * len(DV) + DV.index(r)) * NT + i + 1
                return prep_act, (l * len(AC) + AC.index(r)) * NT + i + 1

            def bank(r, i):
                return ps[2 * i + RN[r] % 2]

            def v4(ap, n, w):
                return ap[0:n, 0:H4 * w].rearrange("p (h x) -> p h x", h=H4)

            with nc.Block() as block:
                @block.sync
                def _(sp):
                    sp.dma_start(prm[:, 0, :], A["a_log"][l].partition_broadcast(P)).then_inc(dl_in, 16)
                    sp.dma_start(prm[:, 1, :], A["dt_bias"][l].partition_broadcast(P)).then_inc(dl_in, 16)
                    sp.dma_start(gn[:, 0:1], A["gnorm_g"][l].rearrange("(p a) -> p a", a=1)).then_inc(dl_in, 16)
                    sp.dma_start(state[:, 1, :, :], A["state_gdn"][l, 0].rearrange("h k v -> k h v")).then_inc(dl_in, 16)
                    sp.wait_ge(s_ready, len(SEQS) * (l + 1))
                    sp.dma_start(OUT["new_gdn_p"][l, 0].rearrange("h k v -> k h v"), state[:, 0, :, :]).then_inc(new_stored, 16)
                    sp.dma_start(OUT["new_gdn_s"][l, 0].rearrange("h k v -> k h v"), state[:, 1, :, :]).then_inc(new_stored, 16)
                    sp.wait_ge(new_stored, 160 * (l + 1))

                @block.gpsimd
                def _(pool):
                    nc.gpsimd.tensor_tensor(sq, cT[:, 0:2 * H4, :], cT[:, 0:2 * H4, :], ALU.mult).then_inc(sq_ready, 1)

                @block.tensor
                def _(pe):
                    def need(r, i):
                        s, v = evac_of(r, i)
                        pe.wait_ge(s, v)
                    pe.wait_ge(sq_ready, l + 1)
                    pe.wait_ge(g_ready, l + 1)
                    for i, (t0, n) in enumerate(TILES):
                        b = ps[6]
                        if i:
                            need("norm", i - 1)
                        for h in range(2 * H4):
                            nc.tensor.matmul(b[0:n, 16 * i + h:16 * i + h + 1], sq[:, h, CCOL[i]:CCOL[i] + n], ones[:, 0:1],
                                             start=True, stop=True)
                        nc.tensor.matmul(b[0:n, 16 * i + 8:16 * i + 12], cumU[0:n, 0:n], gv[0:n, i, :], start=True, stop=True)
                        nc.tensor.matmul(b[0:n, 16 * i + 12:16 * i + 16], blk[0:n, 0:n], gv[0:n, i, :], start=True,
                                         stop=True).then_inc(prep_done, 1)
                    for (i, r0, s, ch) in SEQS:
                        n = TILES[i][1]
                        ins = nc.tensor.matmul(ps[7][:, H4 * ch:H4 * ch + H4], blk[0:n, r0:r0 + 1].to_broadcast([n, P]),
                                               gv[0:n, i, :], start=True, stop=True)
                    ins.then_inc(egl_done, 1)

                    def turns(r, src, w_in, w_out):
                        def f(i, n, h, b):
                            ri, wi_ = (n if w_in is None else w_in), (n if w_out is None else w_out)
                            return nc.tensor.transpose(v4(b, wi_, ri)[:, h, :], src(i, h), ident[0:ri, 0:ri])
                        return f

                    def mul(lhs, rhs, w=None):
                        def f(i, n, h, b):
                            ww = n if w is None else w
                            d = tl[i]
                            return nc.tensor.matmul(v4(b, n, ww)[:, h, :], d[lhs][0:n, h, :], d[rhs][0:n, h, :],
                                                    start=True, stop=True)
                        return f

                    def deep(lhs, rhs):
                        def f(i, n, h, b):
                            d = tl[i]
                            return nc.tensor.matmul(v4(b, n, n)[:, h, :], d[lhs][:, h, :], d[rhs][:, h, :],
                                                    start=True, stop=True)
                        return f

                    def tok(c0):
                        def f(i, n, h, b):
                            return nc.tensor.transpose(v4(b, n, BD)[:, h, :], cT[:, c0 + h, CCOL[i]:CCOL[i] + n], ident[:])
                        return f

                    for i, (t0, n) in enumerate(TILES):
                        for h in range(H4):
                            tok(0)(i, n, h, ps[2 * i])
                        for h in range(H4):
                            ins = tok(H4)(i, n, h, ps[2 * i + 1])
                        ins.then_inc(prep_done, 1)
                    T3 = {
                        "v": (tok(2 * H4), ["qk"]),
                        "grow": (lambda i, n, h, b: nc.tensor.matmul(
                            v4(b, n, n)[:, h, :], ones[0:n, 0:n], tl[i]["gtri"][0:n, h, :], start=True, stop=True), ["qk"]),
                        "qT": (lambda i, n, h, b: nc.tensor.transpose(
                            v4(b, BD, n)[:, h, :], tl[i]["q"][0:n, h, :], ident[0:n, 0:n]), ["v"]),
                        "kT": (lambda i, n, h, b: nc.tensor.transpose(
                            v4(b, BD, n)[:, h, :], tl[i]["k"][0:n, h, :], ident[0:n, 0:n]), ["grow"]),
                        "qdT": (lambda i, n, h, b: nc.tensor.transpose(
                            v4(b, BD, n)[:, h, :], tl[i]["qd"][0:n, h, :], ident[0:n, 0:n]), ["qT"]),
                        "KK": (deep("kT", "kT"), ["kT"]),
                        "QKT": (deep("kT", "qT"), ["qdT"]),
                        "MdT": (lambda i, n, h, b: nc.tensor.transpose(
                            v4(b, n, n)[:, h, :], tl[i]["Md"][0:n, h, :], ident[0:n, 0:n]), ["KK"]),
                        "MoT": (lambda i, n, h, b: nc.tensor.transpose(
                            v4(b, n, n)[:, h, :], tl[i]["Mo"][0:n, h, :], ident[0:n, 0:n]), ["QKT"]),
                        "P2": (mul("MdT", "Md"), ["MdT"]),
                        "P2T": (mul("Md", "MdT"), ["MoT"]),
                        "X1": (mul("P", "X"), ["P2"]),
                        "P4": (mul("PT", "P"), ["P2T"]),
                        "P4T": (mul("P", "PT"), ["X1"]),
                        "X2": (mul("P4", "X"), ["P4"]),
                        "P8": (mul("P4T", "P4"), ["P4T"]),
                        "X3": (mul("P8", "X"), ["X2", "P8"]),
                        "X3T": (lambda i, n, h, b: nc.tensor.transpose(
                            v4(b, n, n)[:, h, :], tl[i]["X"][0:n, h, :], ident[0:n, 0:n]), ["X3"]),
                        "B": (mul("MoT", "XT"), ["X3T"]),
                        "BT": (mul("XT", "MoT"), ["X3T"]),
                        "Y1": (mul("B", "X"), ["B"]),
                        "B2": (mul("BT", "B"), ["BT"]),
                        "TT": (mul("B2", "X"), ["B2", "Y1"]),
                        "u": (mul("TT", "vb", BD), ["TT"]),
                        "wT": (lambda i, n, h, b: nc.tensor.matmul(
                            v4(b, BD, n)[:, h, :], tl[i]["kbG"][0:n, h, :], tl[i]["TT"][0:n, h, :], start=True, stop=True),
                            ["TT"]),
                    }
                    for r in PREP[2:]:
                        f, needs = T3[r]
                        for i, (t0, n) in enumerate(TILES):
                            prev = PREP[RN[r] - 2]
                            if RN[r] - 2 >= 1:
                                need(prev, i)
                            for x in needs:
                                need(x, i)
                            if r == "grow":
                                pe.wait_ge(dec_in, sb_ + i + 1)
                            if r == "X1":
                                pe.wait_ge(x_ready, sb_ + i + 1)
                            for h in range(H4):
                                ins = f(i, n, h, bank(r, i))
                            ins.then_inc(prep_done, 1)

                    for q, (i, r0, s, ch) in enumerate(SEQS):
                        n = min(CHUNK, TILES[i][1])
                        R = slice(r0, r0 + n)
                        d = tl[i]
                        g = len(SEQS) * l + q
                        need("u", i)
                        need("wT", i)
                        if q == 0:
                            pe.wait_ge(egl_ready, l + 1)
                        elif q == 1:
                            pe.wait_ge(dl_in, 64 * (l + 1))
                        else:
                            pe.wait_ge(s_ready, g)
                        if q:
                            pe.wait_ge(vnew_ready, g)
                        A_, B_, C_ = ps[6], ps[7], ps[0]
                        for h in range(H4):
                            ins = nc.tensor.matmul(A_[R, BD * h:BD * h + BD], d["wT"][:, h, R], state[:, s, h, :],
                                                   start=True, stop=True)
                        ins.then_inc(ws_done, 1)
                        pe.wait_ge(vnew_ready, g + 1)
                        if q:
                            pe.wait_ge(o_ready, g)
                            pe.wait_ge(s_ready, g)
                        for h in range(H4):
                            ins = nc.tensor.matmul(C_[:, BD * h:BD * h + BD], d["kt"][R, h, :], d["vnew"][R, h, :],
                                                   start=True, stop=True)
                        ins.then_inc(ds_done, 1)
                        for h in range(H4):
                            nc.tensor.matmul(B_[R, BD * h:BD * h + BD], d["qdT"][:, h, R], state[:, s, h, :],
                                             start=True, stop=False)
                            ins = nc.tensor.matmul(B_[R, BD * h:BD * h + BD], d["QKT"][R, h, R], d["vnew"][R, h, :],
                                                   start=False, stop=True)
                        ins.then_inc(o_done, 1)
                    for i, (t0, n) in enumerate(TILES):
                        pe.wait_ge(on_ready, sb_ + i + 1)
                        for h in range(H4):
                            ins = nc.tensor.transpose(v4(ps[1 + i], BD, n)[:, h, :], tl[i]["on"][0:n, h, :], ident[0:n, 0:n])
                        ins.then_inc(ot_done, 1)

                @block.scalar
                def _(act):
                    c = chain(act, "act")
                    act.wait_ge(dl_in, 64 * (l + 1))
                    c.link(nc.scalar.activation(prm[:, 0, :], prm[:, 0, :], ACT.Exp))
                    act.wait_ge(sm_dve, 2 * l + 1)
                    c.link(nc.scalar.activation(sp_[:, 1, :, :], sp_[:, 1, :, :], ACT.Exp))
                    c.link(nc.scalar.activation(sp_[:, 1, :, :], sp_[:, 1, :, :], ACT.Ln, bias=1.0))
                    nc.scalar.activation(sp_[:, 2, :, :], wsm[:, :, 12:16], ACT.Exp, scale=-1.0).then_inc(sm_act, 1)
                    act.wait_ge(sm_dve, 2 * l + 2)
                    c.link(nc.scalar.activation(nrm16[:, :, 0:8], nrm16[:, :, 0:8], ACT.Ln))
                    c.link(nc.scalar.activation(nrm16[:, :, 0:8], nrm16[:, :, 0:8], ACT.Exp, scale=-0.5))
                    c.link(nc.scalar.activation(nrm16[:, :, 12:16], nrm16[:, :, 12:16], ACT.Exp))
                    c.link(nc.scalar.activation(sp_[:, 0, :, :], nrm16[:, :, 8:12], ACT.Exp))
                    act.wait_ge(egl_done, l + 1)
                    nc.scalar.activation(eg.rearrange("p a h -> p (a h)"), ps[7][:, 0:20], ACT.Exp).then_inc(sm_act, 1)

                    def copies(r, dst, scale=1.0):
                        for i, (t0, n) in enumerate(TILES):
                            act.wait_ge(prep_done, at_round(r, i))
                            dd = tl[i][dst]
                            rows_ = BD if r in ("qT", "kT", "qdT", "wT") else n
                            w = BD if r == "u" else n
                            nc.scalar.activation(dd[0:rows_], v4(bank(r, i), rows_, w), ACT.Copy, scale=scale
                                                 ).then_inc(prep_act, 1)
                    for r in AC:
                        if r == "kT":
                            for i, (t0, n) in enumerate(TILES):
                                act.wait_ge(prep_dve, evac_of("grow", i)[1])
                                for h in range(H4):
                                    nc.scalar.activation(tl[i]["E"][0:n, h, :], tl[i]["E"][0:n, h, :], ACT.Exp,
                                                         bias=nrm16[0:n, i, 8 + h:9 + h])
                                    ins = nc.scalar.activation(tl[i]["ET"][0:n, h, :], tl[i]["ET"][0:n, h, :], ACT.Exp,
                                                               bias=nG[0:n, i, h:h + 1])
                                ins.then_inc(dec_ready, 1)
                        copies(r, {"P2": "P", "P2T": "PT", "X3T": "XT"}.get(r, r), -1.0 if r == "wT" else 1.0)
                    for q, (i, r0, s, ch) in enumerate(SEQS):
                        n = min(CHUNK, TILES[i][1])
                        g = len(SEQS) * l + q
                        act.wait_ge(o_done, g + 1)
                        nc.scalar.activation(tl[i]["o"][r0:r0 + n], v4(ps[7][r0:r0 + n], n, BD), ACT.Copy).then_inc(o_ready, 1)
                    act.wait_ge(ssq_ready, l + 1)
                    c.link(nc.scalar.activation(rr, rr, ACT.Ln))
                    nc.scalar.activation(rr, rr, ACT.Exp, scale=-0.5).then_inc(rn_ready, 1)
                    keep(c, "act")

                @block.vector
                def _(dve):
                    c = chain(dve, "dve")
                    V = nc.vector
                    c(V.memset(rr, 1.0))
                    c(V.memset(nrm16, 1.0))
                    dve.wait_ge(dl_in, 64 * (l + 1))
                    for i in range(NT):
                        ins = V.tensor_tensor(sp_[:, 0, i, :], wsm[:, i, 8:12], prm[:, 1, :], ALU.add)
                    c.link(ins)
                    c.link(V.scalar_tensor_tensor(out=sp_[:, 1, :, :], in0=sp_[:, 0, :, :], scalar=-1.0, in1=sp_[:, 0, :, :],
                                                  op0=ALU.mult, op1=ALU.min))
                    V.tensor_scalar(sp_[:, 0, :, :], sp_[:, 0, :, :], 0.0, None, ALU.max).then_inc(sm_dve, 1)
                    dve.wait_ge(sm_act, 2 * l + 1)
                    c.link(V.tensor_tensor(sp_[:, 0, :, :], sp_[:, 0, :, :], sp_[:, 1, :, :], ALU.add))
                    for i in range(NT):
                        ins = V.scalar_tensor_tensor(out=gv[:, i, :], in0=sp_[:, 0, i, :], scalar=-1.0, in1=prm[:, 0, :],
                                                     op0=ALU.mult, op1=ALU.mult)
                    ins.then_inc(g_ready, 1)
                    c.link(V.tensor_scalar(sp_[:, 2, :, :], sp_[:, 2, :, :], 1.0, None, ALU.add))
                    c.link(V.reciprocal(sp_[:, 2, :, :], sp_[:, 2, :, :]))
                    c.link(V.tensor_scalar(nbeta, sp_[:, 2, :, :], -1.0, None, ALU.mult))
                    for i, (t0, n) in enumerate(TILES):
                        dve.wait_ge(prep_done, at_round("norm", i))
                        c.link(V.tensor_copy(nrm16[0:n, i, :], ps[6][0:n, 16 * i:16 * i + 16]))
                        V.tensor_scalar(nG[0:n, i, :], nrm16[0:n, i, 8:12], -1.0, None, ALU.mult).then_inc(prep_dve, 1)
                    dve.wait_ge(prep_dve, evac_of("norm", NT - 1)[1])
                    c.link(V.tensor_tensor(nrm16[:, :, 12:16], nrm16[:, :, 12:16], nrm16[:, :, 8:12], ALU.subtract))
                    V.tensor_scalar(nrm16[:, :, 0:8], nrm16[:, :, 0:8], RMS_EPS, None, ALU.add).then_inc(sm_dve, 1)
                    dve.wait_ge(sm_act, 2 * l + 2)
                    rq, rk, eT, eG, beta = (nrm16[:, :, 0:4], nrm16[:, :, 4:8], nrm16[:, :, 12:16], sp_[:, 0, :, :],
                                            sp_[:, 2, :, :])
                    c.link(V.tensor_scalar(sc[:, :, SC_Q, :], rq, BD ** -0.5, None, ALU.mult))
                    c.link(V.tensor_tensor(sc[:, :, SC_QD, :], sc[:, :, SC_Q, :], eG, ALU.mult))
                    c.link(V.tensor_copy(sc[:, :, SC_K, :], rk))
                    c.link(V.tensor_tensor(sc[:, :, SC_KT, :], rk, eT, ALU.mult))
                    c.link(V.tensor_copy(sc[:, :, SC_VB, :], beta))
                    c.link(V.tensor_tensor(sc[:, :, SC_KBG, :], rk, eG, ALU.mult))
                    c.link(V.tensor_tensor(sc[:, :, SC_KBG, :], sc[:, :, SC_KBG, :], beta, ALU.mult))
                    dve.wait_ge(sm_act, 2 * l + 2)
                    V.memset(state[:, 0, :, :], 0.0).then_inc(egl_ready, 1)

                    def scaled(dst, src, i, n, which):
                        f = sc[0:n, i, which, :].unsqueeze(2).to_broadcast([n, H4, BD])
                        return V.tensor_tensor(dst[0:n], v4(src, n, BD), f, ALU.mult)
                    for i, (t0, n) in enumerate(TILES):
                        d = tl[i]
                        dve.wait_ge(prep_done, at_round("qk", i))
                        c(scaled(d["q"], ps[2 * i], i, n, SC_Q))
                        c(scaled(d["qd"], ps[2 * i], i, n, SC_QD))
                        c(scaled(d["k"], ps[2 * i + 1], i, n, SC_K))
                        c(scaled(d["kbG"], ps[2 * i + 1], i, n, SC_KBG))
                        for h in range(H4):
                            ins = V.tensor_scalar(d["gtri"][0:n, h, :], cumU[0:n, 0:n], gv[0:n, i, h:h + 1], None, ALU.mult)
                        ins.then_inc(dec_in, 1)
                        scaled(d["kt"], ps[2 * i + 1], i, n, SC_KT).then_inc(prep_dve, 1)
                    for i, (t0, n) in enumerate(TILES):
                        dve.wait_ge(prep_done, at_round("v", i))
                        scaled(tl[i]["vb"], bank("v", i), i, n, SC_VB).then_inc(prep_dve, 1)

                    def allh(m, n):
                        return m[0:n, 0:n].unsqueeze(1).to_broadcast([n, H4, n])
                    for i, (t0, n) in enumerate(TILES):
                        d = tl[i]
                        dve.wait_ge(prep_done, at_round("grow", i))
                        gr = v4(bank("grow", i), n, n)
                        for h in range(H4):
                            V.scalar_tensor_tensor(out=d["E"][0:n, h, :], in0=gr[:, h, :], scalar=-1.0, in1=negL[0:n, 0:n],
                                                   op0=ALU.mult, op1=ALU.add)
                        V.tensor_tensor(d["ET"][0:n], gr, allh(negU, n), ALU.add).then_inc(prep_dve, 1)
                    for i, (t0, n) in enumerate(TILES):
                        d = tl[i]
                        dve.wait_ge(prep_done, at_round("KK", i))
                        dve.wait_ge(dec_ready, sb_ + i + 1)
                        dve.wait_ge(prep_act, evac_of("qdT", i)[1])
                        kk = v4(bank("KK", i), n, n)
                        for h in range(H4):
                            ins = V.scalar_tensor_tensor(out=d["E"][0:n, h, :], in0=kk[:, h, :], scalar=nbeta[0:n, i, h:h + 1],
                                                         in1=d["E"][0:n, h, :], op0=ALU.mult, op1=ALU.mult)
                        c.link(ins)
                        V.tensor_tensor(d["Mo"][0:n], d["E"][0:n], allh(off16, n), ALU.mult)
                        V.tensor_tensor(d["Md"][0:n], d["E"][0:n], allh(d16, n), ALU.mult).then_inc(prep_dve, 1)
                    for i, (t0, n) in enumerate(TILES):
                        d = tl[i]
                        dve.wait_ge(prep_done, at_round("QKT", i))
                        V.tensor_tensor(d["QKT"][0:n], v4(bank("QKT", i), n, n), d["ET"][0:n], ALU.mult).then_inc(prep_dve, 1)
                    for i, (t0, n) in enumerate(TILES):
                        d = tl[i]
                        dve.wait_ge(prep_act, evac_of("MoT", i)[1])
                        V.tensor_tensor(d["X"][0:n], d["MdT"][0:n], allh(ident, n), ALU.add).then_inc(x_ready, 1)
                    for r in ("X1", "X2", "X3", "Y1", "TT"):
                        for i, (t0, n) in enumerate(TILES):
                            d = tl[i]
                            dve.wait_ge(prep_done, at_round(r, i))
                            if r == "X1":
                                dve.wait_ge(x_ready, sb_ + i + 1)
                            else:
                                prev = {"X2": "X1", "X3": "X2", "Y1": "X3", "TT": "Y1"}[r]
                                dve.wait_ge(prep_dve, evac_of(prev, i)[1])
                            V.tensor_tensor(d["X"][0:n], d["X"][0:n], v4(bank(r, i), n, n), ALU.add).then_inc(prep_dve, 1)

                    for q, (i, r0, s, ch) in enumerate(SEQS):
                        n = min(CHUNK, TILES[i][1])
                        R = slice(r0, r0 + n)
                        d = tl[i]
                        g = len(SEQS) * l + q
                        dve.wait_ge(ws_done, g + 1)
                        dve.wait_ge(prep_act, evac_of("u", i)[1])
                        V.tensor_tensor(d["vnew"][R], v4(ps[6][R], n, BD), d["u"][R], ALU.add).then_inc(vnew_ready, 1)
                        dve.wait_ge(ds_done, g + 1)
                        dve.wait_ge(o_done, g + 1)
                        for h in range(H4):
                            ins = V.scalar_tensor_tensor(out=state[:, s, h, :], in0=state[:, s, h, :], scalar=eg[:, ch, h:h + 1],
                                                         in1=ps[0][:, BD * h:BD * h + BD], op0=ALU.mult, op1=ALU.add)
                        ins.then_inc(s_ready, 1)
                    dve.wait_ge(o_ready, len(SEQS) * (l + 1))
                    for i, (t0, n) in enumerate(TILES):
                        c.link(V.tensor_tensor(osq[0:n], tl[i]["o"][0:n], tl[i]["o"][0:n], ALU.mult))
                        c.link(V.tensor_reduce(rr[0:n, i, :], osq[0:n], AX.X, ALU.add))
                    V.tensor_scalar(rr, rr, 1.0 / BD, RMS_EPS, ALU.mult, ALU.add).then_inc(ssq_ready, 1)
                    dve.wait_ge(rn_ready, l + 1)
                    for i, (t0, n) in enumerate(TILES):
                        f = rr[0:n, i, :].unsqueeze(2).to_broadcast([n, H4, BD])
                        V.tensor_tensor(tl[i]["on"][0:n], tl[i]["o"][0:n], f, ALU.mult).then_inc(on_ready, 1)
                    for i, (t0, n) in enumerate(TILES):
                        dve.wait_ge(ot_done, sb_ + i + 1)
                        V.scalar_tensor_tensor(out=obT[:, :, t0:t0 + n], in0=v4(ps[1 + i], BD, n), scalar=gn[:, 0:1],
                                               in1=zT[:, :, t0:t0 + n], op0=ALU.mult, op1=ALU.mult).then_inc(ob_ready, 1)
                    keep(c, "dve")

        m_full, m_hi = sem("m_full"), sem("m_hi")
        mg_done, mg_tanh, mg_read, m_ready, mo_done, mo_added = (sem("mg_done"), sem("mg_tanh"), sem("mg_read"),
                                                                 sem("m_ready"), sem("mo_done"), sem("mo_added"))
        def merge(l):
            u0 = first["merge", l]
            inputs = [(hT[:, 0:4, :], hTh[:, 0:4, :], hTl[:, 0:4, :]), (hT[:, 4:8, :], hTh[:, 4:8, :], hTl[:, 4:8, :]),
                      (oaT[:], oabh[:, 0:4, :], oabl[:, 0:4, :]), (obT[:], oabh[:, 4:8, :], oabl[:, 4:8, :])]
            at = (0, 4 + 2)[l]
            with nc.Block() as block:
                @block.sync
                def _(sp):
                    load_units(sp, u0 + N_MERGE)

                @block.tensor
                def _(pe):
                    pe.wait_ge(x_low, at + 2)
                    for j in range(KD // 2):
                        for u in range(3):
                            n = u0 + 3 * j + u
                            w = halves(n, (8, 256))
                            have_split(pe, n)
                            if j:
                                pe.wait_ge(*((mg_tanh, 4 * (4 * l + j - 1) + 2 * u + 2) if u < 2 else (mg_read, KD * l + 2 * j)))
                            if j == 0 and u == 2:
                                pe.wait_ge(x_low, at + 4)
                            for g in range(1 if u < 2 else 2):
                                x, kk = ((hTh, hTl), KD) if u < 2 else ((oabh, oabl), 4)
                                for c in range(2):
                                    product(ps[2 * (u + g) + c][:, 0:T],
                                            [([v[:, 4 * g + k, P * c:P * c + P] for v in w], [v[:, 4 * g + k, :] for v in x])
                                             for k in range(kk)]).then_inc(mg_done, 1)
                            rel.due = split_free
                    pe.wait_ge(mg_read, KD * (l + 1))
                    for j in range(4):
                        n = u0 + 12 + j
                        w = halves(n, (8, 256))
                        have_split(pe, n)
                        if j == 0:
                            pe.wait_ge(m_ready, KD * (l + 1))
                        for i, (t0, m) in enumerate(TILES):
                            g = NT * j + i
                            if g >= 8:
                                pe.wait_ge(mo_added, 4 * NT * l + g - 7)
                            product(ps[g % 8][0:m, 0:256], [([v[:, k, t0:t0 + m] for v in (mTh, mTl)], [v[:, k, :] for v in w])
                                                            for k in range(KD)]).then_inc(mo_done, 1)
                        rel.due = split_free

                def m_high(act, c):
                    act.wait_ge(m_full, KD * l + c + 1)
                    nc.scalar.activation(mTh[:, c, :], mo_[:, c % 2, 0:T], ACT.Copy).then_inc(m_hi, 1)

                @block.scalar
                def _(act):
                    inputs_high(act, at, inputs[0:1])
                    split_high(act, u0)
                    inputs_high(act, at + 1, inputs[1:])
                    split_high(act, u0 + 1)
                    for j in range(KD // 2):
                        for u in range(3):
                            split_high(act, u0 + 3 * j + u + AHEAD)
                            if u == 2:
                                continue
                            for c in range(2):
                                act.wait_ge(mg_done, 8 * (4 * l + j) + 2 * u + c + 1)
                                if j and u == 0:
                                    act.wait_ge(mg_read, KD * l + 2 * (j - 1) + c + 1)
                                nc.scalar.activation(th[:, c, T * u:T * u + T], ps[2 * u + c][:, 0:T], ACT.Tanh, scale=0.5
                                                     ).then_inc(mg_tanh, 1)
                        for c in range(2):
                            m_high(act, 2 * j + c)
                    for j in range(12 + AHEAD, N_MERGE):
                        split_high(act, u0 + j)

                @block.vector
                def _(dve):
                    inputs_low(dve, at, inputs[0:1])
                    split_low(dve, u0)
                    inputs_low(dve, at + 1, inputs[1:])
                    split_low(dve, u0 + 1)
                    for j in range(KD // 2):
                        for u in range(3):
                            split_low(dve, u0 + 3 * j + u + AHEAD)
                        for c in range(2):
                            dve.wait_ge(mg_tanh, 4 * (4 * l + j) + 2 + c + 1)
                            if j:
                                dve.wait_ge(m_ready, KD * l + 2 * j + c - 1)
                            for g in range(2):
                                dve.wait_ge(mg_done, 8 * (4 * l + j) + 4 + 2 * g + c + 1)
                                s = slice(T * g, T * g + T)
                                ins = nc.vector.scalar_tensor_tensor(out=mo_[:, c, s], in0=th[:, c, s], scalar=1.0,
                                                                     in1=ps[4 + 2 * g + c][:, 0:T], op0=ALU.add, op1=ALU.mult)
                            ins.then_inc(mg_read, 1)
                            dve.wait_ge(mg_read, KD * l + 2 * j + c + 1)
                            nc.vector.tensor_tensor(mo_[:, c, 0:T], mo_[:, c, 0:T], mo_[:, c, T:2 * T], ALU.add
                                                    ).then_inc(m_full, 1)
                        for c in range(2):
                            m = 2 * j + c
                            dve.wait_ge(m_hi, KD * l + m + 1)
                            nc.vector.tensor_tensor(mTl[:, m, :], mo_[:, c, 0:T], mTh[:, m, :].bitcast(F32), ALU.subtract
                                                    ).then_inc(m_ready, 1)
                    for j in range(4):
                        if 12 + AHEAD + j < N_MERGE:
                            split_low(dve, u0 + 12 + AHEAD + j)
                        for i, (t0, n) in enumerate(TILES):
                            g = NT * j + i
                            dve.wait_ge(mo_done, 4 * NT * l + g + 1)
                            r = resid[0:n, i, 256 * j:256 * j + 256]
                            nc.vector.scalar_tensor_tensor(out=r, in0=ps[g % 8][0:n, 0:256], scalar=0.5, in1=r,
                                                           op0=ALU.mult, op1=ALU.add).then_inc(mo_added, 1)

        up_done, silu_done, g_full, g_high, gT_ready = (sem("up_done"), sem("silu_done"), sem("g_full"), sem("g_high"),
                                                       sem("gT_ready"))
        w2_done, y_added = sem("w2_done"), sem("y_added")
        FCH, ECH = D_FF // P, D_FFE // P
        EPAIR = ECH // 2

        def dense_mlp():
            n0 = first["mlp", 0]
            inputs = [(hT[:, 0:4, :], hTh[:, 0:4, :], hTl[:, 0:4, :]), (hT[:, 4:8, :], hTh[:, 4:8, :], hTl[:, 4:8, :])]
            at = 4
            with nc.Block() as block:
                @block.sync
                def _(sp):
                    load_units(sp, n0 + N_FFN)

                @block.gpsimd
                def _(pool):
                    finish_stream(pool, 1)

                @block.tensor
                def _(pe):
                    pe.wait_ge(x_low, at + 2)
                    for u in range(FCH):
                        p, g = u // 2, u % 2
                        w = halves(n0 + u, (8, 256))
                        have_split(pe, n0 + u)
                        if p >= 2:
                            pe.wait_ge(g_full, 2 * (p - 1))
                        for c in range(2):
                            product(ps[4 * (p % 2) + 2 * g + c][:, 0:T],
                                    [([v[:, k, P * c:P * c + P] for v in w], (hTh[:, k, :], hTl[:, k, :])) for k in range(KD)]
                                    ).then_inc(up_done, 1)
                        rel.due = split_free
                    pe.wait_ge(g_full, FCH)
                    for j in range(FCH // 2):
                        n = n0 + FCH + j
                        w = halves(n, (2, D))
                        have_split(pe, n)
                        for q in range(2):
                            f = 2 * j + q
                            pe.wait_ge(gT_ready, f + 1)
                            for i, (t0, m) in enumerate(TILES):
                                for a, b, last in ((gTh, w[0], False), (gTh, w[1], False), (gTl, w[0], True)):
                                    for c in range(2):
                                        ins = rel.mm(ps[2 * i + c][0:m, :], a[:, f, t0:t0 + m], b[:, q, 512 * c:512 * c + 512],
                                                     start=(f == 0 and a is gTh and b is w[0]), stop=(f == FCH - 1 and last))
                                        if f == FCH - 1 and last:
                                            ins.then_inc(w2_done, 1)
                        rel.due = split_free

                @block.scalar
                def _(act):
                    inputs_high(act, at, inputs[0:1])
                    split_high(act, n0)
                    inputs_high(act, at + 1, inputs[1:])
                    split_high(act, n0 + 1)
                    for u in range(N_FFN):
                        p = u // 2
                        if u + AHEAD < N_FFN:
                            split_high(act, n0 + u + AHEAD)
                        if u >= FCH:
                            continue
                        for c in range(2):
                            m = 2 * p + c
                            if u % 2 == 0:
                                act.wait_ge(up_done, 4 * p + c + 1)
                                if p:
                                    act.wait_ge(g_full, m - 1)
                                nc.scalar.activation(slT[:, c, :], ps[4 * (p % 2) + c][:, 0:T], ACT.Silu).then_inc(silu_done, 1)
                            else:
                                act.wait_ge(g_full, m + 1)
                                nc.scalar.activation(gTh[:, m, :], gfull[:, c, :], ACT.Copy).then_inc(g_high, 1)

                @block.vector
                def _(dve):
                    inputs_low(dve, at, inputs[0:1])
                    split_low(dve, n0)
                    inputs_low(dve, at + 1, inputs[1:])
                    split_low(dve, n0 + 1)
                    for u in range(N_FFN):
                        p = u // 2
                        if u + AHEAD < N_FFN:
                            split_low(dve, n0 + u + AHEAD)
                        if u >= FCH or u % 2 == 0:
                            continue
                        for c in range(2):
                            m = 2 * p + c
                            dve.wait_ge(up_done, 4 * p + c + 3)
                            dve.wait_ge(silu_done, m + 1)
                            if p:
                                dve.wait_ge(gT_ready, m - 1)
                            nc.vector.tensor_tensor(gfull[:, c, :], slT[:, c, :], ps[4 * (p % 2) + 2 + c][:, 0:T], ALU.mult
                                                    ).then_inc(g_full, 1)
                        for c in range(2):
                            m = 2 * p + c
                            dve.wait_ge(g_high, m + 1)
                            if m == 8:
                                dve.wait_ge(stream_done, 2)
                            nc.vector.tensor_tensor(gTl[:, m, :], gfull[:, c, :], gTh[:, m, :].bitcast(F32), ALU.subtract
                                                    ).then_inc(gT_ready, 1)
                    for i, (t0, n) in enumerate(TILES):
                        for c in range(2):
                            dve.wait_ge(w2_done, 2 * i + c + 1)
                            r = resid[0:n, i, 512 * c:512 * c + 512]
                            nc.vector.tensor_tensor(r, r, ps[2 * i + c][0:n, :], ALU.add).then_inc(y_added, 1)

        lgt_in, rt_done, sel_ready, pos_done, flag_ready, pos_ready = (sem("lgt_in"), sem("rt_done"), sem("sel_ready"),
                                                                       sem("pos_done"), sem("flag_ready"), sem("pos_ready"))
        rt_read, rt_exp, rt_top = sem("rt_read"), sem("rt_exp"), sem("rt_top")
        oh_ready, ga_done, xg_ready, ohg_ready, ohT_done, ohT_ready = (sem("oh_ready"), sem("ga_done"), sem("xg_ready"),
                                                                       sem("ohg_ready"), sem("ohT_done"), sem("ohT_ready"))
        y_ready, sc_done, sc_added = sem("y_ready"), sem("sc_done"), sem("sc_added")
        e_up, e_silu, e_gated, e_turned, e_high, e_ready, xg_high = [sem(x) for x in (
            "e_up", "e_silu", "e_gated", "e_turned", "e_high", "e_ready", "xg_high")]
        ea = Area(experts)
        router = ea(KD, NE)
        gt = ea(2, 256)
        slE = ea(2, 256)
        yE = ea(D)
        oh = ea(NT, CAP)
        ohg = ea(NT, CAP)
        ohT = ea(NT, P)
        rlog = ea(NT, NE)
        rtop = ea(NT, 8)
        rsel = ea(NT, 2 * NE)
        selm = ea(NT, NE)
        gate = ea(NT, NE)
        ridx = ea(NT, 8)
        rw = ea(NT, 4)
        posr = ea(NT, ROUNDS * NE + 1)
        cnt = ea(NE)
        cmx = ea(2)

        def moe():
            iu = itmp
            with nc.Block() as block:
                def expert_tensor(pe, r, e):
                    i = r * NE + e
                    pe.wait_ge(xg_ready, 2 * i + 2)
                    for u in range(ECH):
                        p, g = u // 2, u % 2
                        w = halves(moe0 + u, (8, 256))
                        have_split(pe, moe0 + u, i)
                        if p >= 2:
                            pe.wait_ge(e_gated, EPAIR * i + p - 1)
                        product(ps[2 * g + p % 2][0:CAP, 0:256],
                                [((xgh[:, k, :], xgl[:, k, :]), [v[:, k, :] for v in w]) for k in range(KD)]).then_inc(e_up, 1)
                        rel.due = split_free
                        if g and p:
                            turn_hidden(pe, i, p - 1)
                    for j in range(EPAIR):
                        n = moe0 + ECH + j
                        w = halves(n, (2, D))
                        have_split(pe, n, i)
                        pe.wait_ge(e_ready, EPAIR * i + j + 1)
                        for q in range(2):
                            f = 2 * j + q
                            for a, b, last in ((gEh, w[0], False), (gEh, w[1], False), (gEl, w[0], True)):
                                for c in range(2):
                                    ins = rel.mm(ps[4 + c][0:CAP, :], a[:, f, :], b[:, q, 512 * c:512 * c + 512],
                                                 start=(f == 0 and a is gEh and b is w[0]), stop=(f == ECH - 1 and last))
                        if j == EPAIR - 1:
                            ins.then_inc(split_free, 1)
                        else:
                            rel.due = split_free
                        if j == 0:
                            turn_hidden(pe, i, EPAIR - 1)
                        if j == 1:
                            gather(pe, i + 1)
                            pe.wait_ge(ohg_ready, i + 1)
                            for t in range(NT):
                                m = TILES[t][1]
                                ins = rel.mm(ps[2][0:CAP, P * t:P * t + m], ohg[0:m, t, :], ident[0:m, 0:m],
                                             is_transpose=True, start=True, stop=True)
                            ins.then_inc(ohT_done, 1)
                    pe.wait_ge(ohT_ready, i + 1)
                    pe.wait_ge(y_ready, i + 1)
                    for t in range(NT):
                        m = TILES[t][1]
                        for c in range(2):
                            if 2 * t + c >= 2:
                                pe.wait_ge(sc_added, 6 * i + 2 * t + c)
                            rel.mm(ps[6 + c][0:m, :], ohT[0:CAP, t, 0:m], yE[0:CAP, 512 * c:512 * c + 512],
                                   start=True, stop=True).then_inc(sc_done, 1)

                def turn_hidden(pe, i, p):
                    pe.wait_ge(e_gated, EPAIR * i + p + 1)
                    if p >= 2:
                        pe.wait_ge(e_ready, EPAIR * i + p - 1)
                    for c in range(2):
                        ins = rel.mm(ps[6 + p % 2][:, CAP * c:CAP * c + CAP], gt[0:CAP, p % 2, P * c:P * c + P],
                                     ident[0:CAP, 0:CAP], is_transpose=True, start=True, stop=True)
                    ins.then_inc(e_turned, 1)

                def gather(pe, i):
                    pe.wait_ge(oh_ready, i + 1)
                    for k in range(KD):
                        for t in range(NT):
                            n = TILES[t][1]
                            ins = rel.mm(ps[k // 4][:, CAP * (k % 4):CAP * (k % 4) + CAP], htok[0:n, t, P * k:P * k + P],
                                         oh[0:n, t, :], start=(t == 0), stop=(t == NT - 1))
                        if k % 4 == 3:
                            ins.then_inc(ga_done, 1)

                def expert_scalar(act, r, e):
                    i = r * NE + e
                    for u in range(AHEAD):
                        split_high(act, moe0 + u, i)
                    for u in range(N_EXP):
                        p = u // 2
                        if u + AHEAD < N_EXP:
                            split_high(act, moe0 + u + AHEAD, i)
                        if u % 2 == 0 and 2 <= p <= EPAIR:
                            hidden_high(act, i, p - 2)
                        if u == ECH + 1:
                            hidden_high(act, i, EPAIR - 1)
                        if u % 2 == 0 and p < EPAIR:
                            act.wait_ge(e_up, ECH * i + u + 1)
                            if p >= 2:
                                act.wait_ge(e_gated, EPAIR * i + p - 1)
                            nc.scalar.activation(slE[0:CAP, p % 2, :], ps[p % 2][0:CAP, 0:256], ACT.Silu).then_inc(e_silu, 1)
                        if u == ECH + 2:
                            gathered_high(act, i + 1)
                            act.wait_ge(ohT_done, i + 1)
                            nc.scalar.activation(ohT[0:CAP, 0:2, :], ps[2][0:CAP, 0:256].rearrange("p (t c) -> p t c", t=2), ACT.Copy)
                            nc.scalar.activation(ohT[0:CAP, 2, 0:DEC], ps[2][0:CAP, 256:256 + DEC], ACT.Copy).then_inc(ohT_ready, 1)
                    act.wait_ge(split_free, split_index(moe0) + N_EXP * (i + 1))
                    nc.scalar.activation(yE[0:CAP, 0:512], ps[4][0:CAP, :], ACT.Copy)
                    nc.scalar.activation(yE[0:CAP, 512:D], ps[5][0:CAP, :], ACT.Copy).then_inc(y_ready, 1)

                def turned_view(p):
                    return ps[6 + p % 2][:, 0:2 * CAP].rearrange("p (c t) -> p c t", c=2)

                def hidden_high(act, i, p):
                    act.wait_ge(e_turned, EPAIR * i + p + 1)
                    nc.scalar.activation(gEh[:, 2 * p:2 * p + 2, :], turned_view(p), ACT.Copy).then_inc(e_high, 1)

                def hidden_low(dve, i, p):
                    dve.wait_ge(e_high, EPAIR * i + p + 1)
                    nc.vector.tensor_tensor(gEl[:, 2 * p:2 * p + 2, :], turned_view(p), gEh[:, 2 * p:2 * p + 2, :].bitcast(F32),
                                            ALU.subtract).then_inc(e_ready, 1)

                def gathered_view(h):
                    return ps[h][:, 0:4 * CAP].rearrange("p (k t) -> p k t", k=4)

                def gathered_high(act, i):
                    for h in range(2):
                        act.wait_ge(ga_done, 2 * i + h + 1)
                        nc.scalar.activation(xgh[:, 4 * h:4 * h + 4, :], gathered_view(h), ACT.Copy).then_inc(xg_high, 1)

                def gathered_low(dve, i):
                    for h in range(2):
                        dve.wait_ge(xg_high, 2 * i + h + 1)
                        nc.vector.tensor_tensor(xgl[:, 4 * h:4 * h + 4, :], gathered_view(h),
                                                xgh[:, 4 * h:4 * h + 4, :].bitcast(F32), ALU.subtract).then_inc(xg_ready, 1)

                def onehot(i):
                    for t in range(NT):
                        n = TILES[t][1]
                        ins = nc.vector.tensor_scalar(oh[0:n, t, :], iota[0:n, :], posr[0:n, t, bass.ds(i, 1)], None, ALU.is_equal)
                    ins.then_inc(oh_ready, 1)

                def expert_vector(dve, r, e):
                    i = r * NE + e
                    dve.wait_ge(stream_done, DEPTH * 2)
                    for u in range(AHEAD):
                        split_low(dve, moe0 + u, i)
                    onehot(i + 1)
                    for t in range(NT):
                        n = TILES[t][1]
                        ins = nc.vector.tensor_scalar(ohg[0:n, t, :], iota[0:n, :], posr[0:n, t, bass.ds(i, 1)],
                                                      gate[0:n, t, bass.ds(e, 1)], ALU.is_equal, ALU.mult)
                    ins.then_inc(ohg_ready, 1)
                    for u in range(N_EXP):
                        p = u // 2
                        if u + AHEAD < N_EXP:
                            split_low(dve, moe0 + u + AHEAD, i)
                        if u % 2 == 0 and 2 <= p <= EPAIR:
                            hidden_low(dve, i, p - 2)
                        if u == ECH + 1:
                            hidden_low(dve, i, EPAIR - 1)
                        if u % 2 and p < EPAIR:
                            dve.wait_ge(e_up, ECH * i + u + 1)
                            dve.wait_ge(e_silu, EPAIR * i + p + 1)
                            if p >= 2:
                                dve.wait_ge(e_turned, EPAIR * i + p - 1)
                            nc.vector.tensor_tensor(gt[0:CAP, p % 2, :], slE[0:CAP, p % 2, :], ps[2 + p % 2][0:CAP, 0:256],
                                                    ALU.mult).then_inc(e_gated, 1)
                        if u == ECH + 2:
                            gathered_low(dve, i + 1)
                    for t in range(NT):
                        n = TILES[t][1]
                        for c in range(2):
                            dve.wait_ge(sc_done, 6 * i + 2 * t + c + 1)
                            q = resid[0:n, t, 512 * c:512 * c + 512]
                            nc.vector.tensor_tensor(q, q, ps[6 + c][0:n, :], ALU.add).then_inc(sc_added, 1)

                def expert_loads(sp, r, e, lo):
                    i = r * NE + e
                    for j in range(lo, N_EXP):
                        sp.wait_ge(unit_used, moe0 + N_EXP * i + j - RING + 1)
                        w = [A[x][0, bass.ds(e, 1)].squeeze(0) if not isinstance(e, int) else A[x][0, e]
                             for x in ("moe_w1", "moe_w3", "moe_w2")]
                        dst, src = mlp_loads(moe0, j, *w, D_FFE)
                        sp.dma_start(dst, src).then_inc(slot_full[(moe0 + j) % RING], 16)

                def rounds(eng, body, peel=None):
                    if peel is not None:
                        peel()
                    with eng.Fori(0 if peel is None else 1, NE) as e:
                        body(0, e)
                    eng.wait_ge(flag_ready, 1)
                    more = eng.value_load(iu[0:1, 0:1], min_val=0, max_val=1)
                    with eng.If(more > 0):
                        with eng.Fori(1, ROUNDS) as r:
                            with eng.Fori(0, NE) as e:
                                body(r, e)

                @block.sync
                def _(sp):
                    sp.dma_start(router, A["moe_router"][0].rearrange("(k p) e -> p k e", p=P)).then_inc(lgt_in, 16)
                    rounds(sp, lambda r, e: expert_loads(sp, r, e, 0), lambda: expert_loads(sp, 0, 0, RING))

                @block.gpsimd
                def _(pool):
                    c = chain(pool, "pool")
                    for i, (t0, n) in enumerate(TILES):
                        c.link(nc.gpsimd.tensor_scalar(resid[0:n, i, :], htok[0:n, i, :], ALPHA, None, ALU.mult))
                    nc.gpsimd.memset(std[:], 1.0).then_inc(stream_done, 1)
                    keep(c, "pool")

                @block.tensor
                def _(pe):
                    pe.wait_ge(lgt_in, 16)
                    for i, (t0, n) in enumerate(TILES):
                        for k in range(KD):
                            ins = rel.mm(ps[0][0:n, NE * i:NE * i + NE], hT[:, k, t0:t0 + n], router[:, k, :],
                                         start=(k == 0), stop=(k == KD - 1))
                    ins.then_inc(rt_done, 1)
                    pe.wait_ge(sel_ready, 1)
                    for i, (t0, n) in enumerate(TILES):
                        for j in range(i):
                            nc.tensor.matmul(ps[1][0:n, NE * i:NE * i + NE], ones[:, 0:n], selm[:, j, :], start=(j == 0), stop=False)
                        ins = nc.tensor.matmul(ps[1][0:n, NE * i:NE * i + NE], before[0:n, 0:n], selm[0:n, i, :],
                                               start=(i == 0), stop=True)
                    for i, (t0, n) in enumerate(TILES):
                        ins = nc.tensor.matmul(ps[1][:, 32:32 + NE], ones[0:n, :], selm[0:n, i, :], start=(i == 0), stop=(i == NT - 1))
                    ins.then_inc(pos_done, 1)
                    pe.wait_ge(pos_ready, 1)
                    gather(pe, 0)
                    rounds(pe, lambda r, e: expert_tensor(pe, r, e))

                @block.scalar
                def _(act):
                    act.wait_ge(rt_top, 1)
                    nc.scalar.activation(rw[:, :, 1:2], rw[:, :, 0:1], ACT.Exp).then_inc(rt_exp, 1)
                    gathered_high(act, 0)
                    rounds(act, lambda r, e: expert_scalar(act, r, e))

                @block.vector
                def _(dve):
                    c = chain(dve, "dve")
                    V = nc.vector
                    c.link(V.memset(rlog, 0.0))
                    dve.wait_ge(rt_done, 1)
                    for i, (t0, n) in enumerate(TILES):
                        ins = V.tensor_copy(rlog[0:n, i, :], ps[0][0:n, NE * i:NE * i + NE])
                    c.link(ins)
                    for i in range(NT):
                        c.link(V.max(rtop[:, i, :], rlog[:, i, :]))
                        c.link(V.max_index(ridx[:, i, :].bitcast(U32), rtop[:, i, :], rlog[:, i, :]))
                    V.tensor_tensor(rw[:, :, 0:1], rtop[:, :, 1:2], rtop[:, :, 0:1], ALU.subtract).then_inc(rt_top, 1)
                    c.link(V.tensor_copy(rtop[:, :, 2:4], ridx[:, :, 0:2].bitcast(U32)))
                    dve.wait_ge(rt_exp, 1)
                    c.link(V.tensor_scalar(rw[:, :, 2:3], rw[:, :, 1:2], 1.0, None, ALU.add))
                    c.link(V.reciprocal(rw[:, :, 2:3], rw[:, :, 2:3]))
                    c.link(V.tensor_tensor(rw[:, :, 3:4], rw[:, :, 2:3], rw[:, :, 1:2], ALU.mult))
                    for i in range(NT):
                        for q in range(2):
                            c.link(V.tensor_scalar(rsel[:, i, NE * q:NE * q + NE], iota[:, 0:NE], rtop[:, i, 2 + q:3 + q], None,
                                                   ALU.is_equal))
                        c.link(V.tensor_tensor(selm[:, i, :], rsel[:, i, 0:NE], rsel[:, i, NE:2 * NE], ALU.add))
                        c.link(V.tensor_scalar(gate[:, i, :], rsel[:, i, 0:NE], rw[:, i, 2:3], None, ALU.mult))
                        ins = V.scalar_tensor_tensor(out=gate[:, i, :], in0=rsel[:, i, NE:2 * NE], scalar=rw[:, i, 3:4],
                                                     in1=gate[:, i, :], op0=ALU.mult, op1=ALU.add)
                        if i < NT - 1:
                            c.link(ins)
                    ins.then_inc(sel_ready, 1)
                    c.link(V.memset(posr, -1.0))
                    dve.wait_ge(pos_done, 1)
                    c.link(V.tensor_reduce(cmx[:, 0:1], ps[1][:, 32:32 + NE], AX.X, ALU.max))
                    c.link(V.tensor_scalar(cmx[:, 1:2], cmx[:, 0:1], float(CAP), None, ALU.is_gt))
                    V.tensor_copy(iu[:, 0:1], cmx[:, 1:2]).then_inc(flag_ready, 1)
                    for i, (t0, n) in enumerate(TILES):
                        c.link(V.scalar_tensor_tensor(out=posr[0:n, i, 0:NE], in0=ps[1][0:n, NE * i:NE * i + NE], scalar=1.0,
                                                      in1=selm[0:n, i, :], op0=ALU.add, op1=ALU.mult))
                        c.link(V.tensor_scalar(posr[0:n, i, 0:NE], posr[0:n, i, 0:NE], -1.0, None, ALU.add))
                        for r in range(1, ROUNDS):
                            c(V.tensor_scalar(posr[0:n, i, NE * r:NE * r + NE], posr[0:n, i, 0:NE], -float(CAP * r), None, ALU.add))
                    c.sync()
                    V.memset(cmx[:, 0:1], 0.0).then_inc(sc_added, 1)
                    V.memset(cnt, 0.0).then_inc(pos_ready, 1)
                    onehot(0)
                    gathered_low(dve, 0)
                    keep(c, "dve")
                    rounds(dve, lambda r, e: expert_vector(dve, r, e))

        norm(0, 0, A["ln_in_g"], A["ln_in_b"])
        calls = 1
        for l in range(DEPTH):
            if upto < 10 * l + 1:
                return
            project(l)
            attend(l)
            delta(l)
            if upto < 10 * l + 2:
                return
            merge(l)
            norm(calls, 1 + 2 * l, A["ln1_g"][l], A["ln1_b"][l], htok if l == 1 else None)
            if upto < 10 * l + 3:
                return
            dense_mlp() if l == 0 else moe()
            norm(calls + 1, 2 + 2 * l, A["ln2_g"][l], A["ln2_b"][l], final=(l == DEPTH - 1))
            calls += 2


_SHAPES = {
    "y_prompt": (1, SEQ, D), "y_sample": (1, DEC, D),
    "new_k_p": (DEPTH, 1, SEQ, A_KV, HD), "new_v_p": (DEPTH, 1, SEQ, A_KV, HD), "new_idx_k_p": (DEPTH, 1, SEQ, HD),
    "new_conv_p": (DEPTH, 1, CW - 1, CCH), "new_gdn_p": (DEPTH, 1, B_HEADS, BD, BD),
    "new_k_s": (DEPTH, 1, DEC, A_KV, HD), "new_v_s": (DEPTH, 1, DEC, A_KV, HD), "new_idx_k_s": (DEPTH, 1, DEC, HD),
    "new_conv_s": (DEPTH, 1, CW - 1, CCH), "new_gdn_s": (DEPTH, 1, B_HEADS, BD, BD),
}


_INS = ["x_prompt", "x_sample", "cache_k", "cache_v", "cache_idx_k", "state_conv", "state_gdn", "ln_in_g", "ln_in_b",
        "w_in", "conv_w", "a_log", "dt_bias", "gnorm_g", "w_oa", "w_ob", "w_out", "ln1_g", "ln1_b", "ln2_g", "ln2_b",
        "ffn_w1", "ffn_w3", "ffn_w2", "moe_router", "moe_w1", "moe_w3", "moe_w2"]


def kernel(**inputs):
    import numpy as np
    import concourse.bacc as bacc
    from concourse.bass_utils import run_bass_kernel_spmd

    nc = bacc.Bacc("TRN2", target_bir_lowering=False, num_devices=1)
    arrays, A, OUT = {}, {}, {}
    for name in _INS:
        a = np.ascontiguousarray(inputs[name])
        arrays[f"in_{name}"] = a
        A[name] = nc.dram_tensor(f"in_{name}", a.shape, mybir.dt.from_np(a.dtype), kind="ExternalInput").ap()
    for name, shape in _SHAPES.items():
        OUT[name] = nc.dram_tensor(f"out_{name}", shape, F32, kind="ExternalOutput").ap()
    program(nc, A, OUT)
    r = run_bass_kernel_spmd(nc, [arrays], core_ids=[0])
    return tuple(r.results[0][f"out_{name}"] for name in _SHAPES)
```

```python
from contextlib import ExitStack

import concourse.bass as bass
from concourse import mybir

F32 = mybir.dt.float32
F32R = mybir.dt.float32r
I32 = mybir.dt.int32
U32 = mybir.dt.uint32
ALU = mybir.AluOpType
ACT = mybir.ActivationFunctionType
AX = mybir.AxisListType

P = 128
D = 1024
KD = D // P
SEQ, DEC, PAST = 256, 32, 256
T = SEQ + DEC
TILES = [(0, 128), (128, 128), (256, DEC)]
NT = len(TILES)
DEPTH = 2
CHUNK = 64
A_HEADS, A_KV, HD = 8, 2, 64
IH = 8
B_HEADS, BD = 4, 128
CW = 4
CCH = 3 * B_HEADS * BD
CT = CCH // P
D_FF, D_FFE, NE = 2816, 3584, 8
ALPHA = (2 * DEPTH) ** 0.25
LN_EPS, RMS_EPS = 1e-5, 1e-6

O_QA = 0
O_KA = O_QA + A_HEADS * HD
O_VA = O_KA + A_KV * HD
O_QI = O_VA + A_KV * HD
O_KI = O_QI + IH * HD
O_WI = O_KI + HD
O_CV = O_WI + IH
O_AB = O_CV + CCH
O_Z = O_AB + 2 * B_HEADS
O_GA = O_Z + B_HEADS * BD
O_GB = O_GA + D

K_CACHE = SEQ
K_SMP = SEQ + PAST
NK = SEQ + PAST + DEC
KEYS = [(0, SEQ), (0, SEQ), (K_CACHE, PAST + DEC)]
NSEL = [min(256, s // 4) for _, s in KEYS]
VT = [[0, 1], [0, 1], [2, 3, 4]]
CI = (CW - 1) + SEQ + (CW - 1) + DEC
CO = CI - (CW - 1)
C_SMP = SEQ + CW - 1
CCOL = [0, 128, C_SMP]
NEG = -3.0e38
TAKEN = -3.4e38

RING, SLOT = 6, 2048
WS = 3
AHEAD = WS - 1
CAP = 128
ROUNDS = -(-T // CAP)


def program(nc, A, OUT, upto=99):
    ctx = ExitStack()
    with ctx:
        def sb(name, shape, dt=F32):
            return ctx.enter_context(nc.sbuf_tensor(name, shape, dt))

        def sem(name):
            return ctx.enter_context(nc.semaphore(name))

        ps = [ctx.enter_context(nc.psum_tensor(f"ps{b}", [P, 512], F32)) for b in range(8)]

        ring = sb("ring", [P, RING * SLOT])
        resid = sb("resid", [P, NT, D])
        hT = sb("hT", [P, KD, T])
        lnp = sb("lnp", [P, 10, KD])
        stats = sb("stats", [P, NT, 2, 6])
        mv = sb("mv", [P, NT, 2])
        std = sb("std", [P, NT])
        rstd = sb("rstd", [P, NT])
        ident = sb("ident", [P, P])
        ones = sb("ones", [P, P])
        cumU = sb("cumU", [P, P])
        blk = sb("blk", [P, P])
        d16 = sb("d16", [P, P])
        off16 = sb("off16", [P, P])
        negL = sb("negL", [P, P])
        negU = sb("negU", [P, P])
        before = sb("before", [P, P])
        iota = sb("iota", [P, CAP])
        itmp = sb("itmp", [P, 320], I32)
        adm = sb("adm", [P, 2, SEQ])
        ndist = sb("ndist", [P, NT, PAST + DEC])
        wsm = sb("wsm", [P, NT, 16])

        def layout(*tensors):
            with ExitStack() as mem:
                return [mem.enter_context(nc.sbuf_tensor(*t)) for t in (t if len(t) == 3 else (*t, F32) for t in tensors)]

        SHARED = (nc.sbuf_usable_end - nc.sbuf_base) // 4 - 64
        ARENA = 20000
        OAB0 = SHARED - 2 * 4 * T
        cT, zT, arena, slopes, distr, identr, away, _, oaT, obT = layout(
            ("cT", [P, CT, CO]),
            ("zT", [P, B_HEADS, T]), ("arena", [P, ARENA]),
            ("slopes", [P, A_HEADS, P], F32R),
            ("distr", [P, NT, PAST + DEC], F32R), ("identr", [P, P], F32R),
            ("away", [P, PAST + DEC], F32R),
            ("pad", [P, OAB0 - CT * CO - B_HEADS * T - ARENA - A_HEADS * P - (NT + 1) * (PAST + DEC) - P]), ("oaT", [P, 4, T]), ("obT", [P, 4, T]))
        wh, wl, oabh, oabl, mTh, mTl, mo_ = layout(
            ("wh", [P, WS, SLOT], F32R), ("wl", [P, WS, SLOT], F32R),
            ("oabh", [P, 8, T], F32R), ("oabl", [P, 8, T], F32R),
            ("mTh", [P, KD, T], F32R), ("mTl", [P, KD, T], F32R), ("mo_", [P, 2, 2 * T]))
        GATE0 = CT * CO + B_HEADS * T + ARENA
        assert 2 * WS * SLOT + 4 * KD * T + 4 * T <= GATE0 and GATE0 + 2 * KD * T <= OAB0
        _, tanhs = layout(("under", [P, GATE0]), ("tanhs", [P, 2 * KD, T]))
        _, hTh, hTl, slT, gfull, gTh, gTl = layout(
            ("parts", [P, 2 * WS * SLOT]), ("hTh", [P, KD, T], F32R), ("hTl", [P, KD, T], F32R),
            ("slT", [P, 2, T]), ("gfull", [P, 2, T]),
            ("gTh", [P, D_FF // P, T], F32R), ("gTl", [P, D_FF // P, T], F32R))
        assert 2 * WS * SLOT + (2 * KD + 4 + D_FF // P + 8) * T <= SHARED - 2 * D
        _, yT = layout(("splits", [P, 2 * WS * SLOT]), ("yT", [P, KD, T]))
        _, xgh, xgl, gEh, gEl, htok, htokh, oh, ohT, yh, yl, experts = layout(
            ("weights", [P, 2 * WS * SLOT]), ("xgh", [P, KD, CAP], F32R), ("xgl", [P, KD, CAP], F32R),
            ("gEh", [P, D_FFE // P, CAP], F32R), ("gEl", [P, D_FFE // P, CAP], F32R), ("htok", [P, NT, D]),
            ("htokh", [P, NT, D], F32R), ("oh", [P, NT, CAP], F32R), ("ohT", [P, NT, P], F32R),
            ("yh", [P, D], F32R), ("yl", [P, D], F32R), ("experts", [P, 1800]))
        _, htokl = layout(("above", [P, 2 * WS * SLOT + 2 * KD * CAP + 2 * (D_FFE // P) * CAP]), ("htokl", [P, NT, D], F32R))
        _, gb_all = layout(("below", [P, SHARED - 2 * D]), ("gb", [P, 2, D]))

        class Area:
            def __init__(self, where=None):
                self.at, self.where = 0, arena if where is None else where

            def __call__(self, *dims):
                n = 1
                for d in dims:
                    n *= d
                v = self.where[:, self.at:self.at + n]
                self.at += n
                assert self.at <= self.where.shape[1], (self.at, self.where.shape)
                if len(dims) == 2:
                    v = v.rearrange("p (a b) -> p a b", a=dims[0])
                if len(dims) == 3:
                    v = v.rearrange("p (a b c) -> p a b c", a=dims[0], b=dims[1])
                return v

        ar = Area()
        qaT = ar(4, T)
        kT = ar(NK)
        kiT = ar(NK)
        qiT = ar(4, T)
        vtok = ar(5, A_KV * HD)
        ATT0 = ar.at
        cin = ar(CT, CI)
        vT = ar(T)
        ktok = ar(2, A_KV * HD)
        kitok = ar(2, 2 * HD)
        crow = ar(CCH)
        cw = ar(CT, 8)
        last = ar(CT, 6)
        STORED0 = ARENA - CCH - NT * (A_KV + 1) * HD
        assert ar.at <= STORED0
        ar.at = STORED0
        lrow = ar(CCH)
        knew = ar(NT, A_KV * HD)
        inew = ar(NT, HD)

        units = []

        def slot(n, dims):
            s = (n % RING) * SLOT
            size = 1
            for d in dims:
                size *= d
            v = ring[:, s:s + size]
            return v.rearrange("p (a b) -> p a b", a=dims[0])

        def unit(*loads):
            n = len(units)
            units.append(loads)
            return n

        def rows(w):
            return w.rearrange("(k p) n -> p k n", p=P)

        def project_units(l):
            w = rows(A["w_in"][l])
            n0 = len(units)
            for k in (0, 4):
                v = slot(len(units), (4, 512)).rearrange("p k (c a x) -> p k c a x", a=2, x=HD)
                unit(*[(v[:, q, :, a, :], w[:, k + q, O_QA + 256 * a:O_QA + 256 * a + 256]
                        .rearrange("p (c x) -> p c x", x=HD)) for q in range(4) for a in range(2)])
            n = len(units)
            unit((slot(n, (8, 256)), w[:, :, O_KA:O_KA + 256]))
            for k in (0, 4):
                n = len(units)
                unit((slot(n, (4, 512)), w[:, k:k + 4, O_QI:O_QI + 512]))
            n = len(units)
            v = slot(n, (8, 80))
            unit((v[:, :, 0:72], w[:, :, O_KI:O_KI + 72]), (v[:, :, 72:80], w[:, :, O_AB:O_AB + 8]))
            for j in range(6):
                n = len(units)
                unit((slot(n, (8, 256)), w[:, :, O_CV + 256 * j:O_CV + 256 * j + 256]))
            for j in range(2):
                n = len(units)
                unit((slot(n, (8, 256)), w[:, :, O_Z + 256 * j:O_Z + 256 * j + 256]))
            assert n0 % RING < RING - 1 and (n0 + 3) % RING < RING - 1
            return n0

        def merge_units(l):
            w, oa, ob, wo = rows(A["w_in"][l]), rows(A["w_oa"][l]), rows(A["w_ob"][l]), rows(A["w_out"][l])
            n0 = len(units)
            for j in range(4):
                c = 256 * j
                n = len(units)
                unit((slot(n, (8, 256)), w[:, :, O_GA + c:O_GA + c + 256]))
                n = len(units)
                unit((slot(n, (8, 256)), w[:, :, O_GB + c:O_GB + c + 256]))
            for j in range(4):
                c = 256 * j
                n = len(units)
                v = slot(n, (8, 256))
                unit((v[:, 0:4, :], oa[:, :, c:c + 256]), (v[:, 4:8, :], ob[:, :, c:c + 256]))
            for j in range(4):
                n = len(units)
                unit((slot(n, (8, 256)), wo[:, :, 256 * j:256 * j + 256]))
            return n0

        def mlp_loads(n0, j, w1, w3, w2, ff):
            pairs = ff // 256
            if j < 2 * pairs:
                w = (w1, w3)[j % 2]
                c = 256 * (j // 2)
                return slot(n0 + j, (8, 256)), w.rearrange("(k p) n -> p k n", p=P)[:, :, c:c + 256]
            r = 256 * (j - 2 * pairs)
            return slot(n0 + j, (2, D)), w2[r:r + 256, :].rearrange("(k p) n -> p k n", p=P)

        N_PROJ, N_GATE, N_MERGE, N_FFN, N_EXP = 14, 8, 8, 3 * D_FF // 256, 3 * D_FFE // 256
        first = {}
        for l in range(DEPTH):
            first["project", l] = project_units(l)
            first["gate", l] = merge_units(l)
            first["merge", l] = first["gate", l] + N_GATE
            if l == 0:
                first["mlp", l] = len(units)
                for j in range(N_FFN):
                    unit(mlp_loads(first["mlp", 0], j, A["ffn_w1"][0], A["ffn_w3"][0], A["ffn_w2"][0], D_FF))
        moe0 = first["moe"] = len(units)
        for j in range(N_EXP):
            unit(mlp_loads(moe0, j, A["moe_w1"][0, 0], A["moe_w3"][0, 0], A["moe_w2"][0, 0], D_FFE))
        assert N_EXP % RING == 0

        slot_full = [sem(f"slot_full{s}") for s in range(RING)]
        unit_used = sem("unit_used")
        full_at = []
        count = [0] * RING
        for n, loads in enumerate(units):
            count[n % RING] += 16 * len(loads)
            full_at.append(count[n % RING])
        PER_EXPERT = 16 * N_EXP // RING

        loaded = [0]

        def load_units(sp, used):
            hi = min(used + RING, len(units))
            lo, loaded[0] = loaded[0], hi
            for n in range(lo, hi):
                if n >= RING:
                    sp.wait_ge(unit_used, n - RING + 1)
                for dst, src in units[n]:
                    sp.dma_start(dst, src).then_inc(slot_full[n % RING], 16)

        def have(pe, n, experts=0):
            pe.wait_ge(slot_full[n % RING], experts * PER_EXPERT + full_at[n])

        class Release:
            def __init__(self):
                self.due = None

            def mm(self, *a, **k):
                ins = nc.tensor.matmul(*a, **k)
                if self.due:
                    ins.then_inc(self.due, 1)
                    self.due = None
                return ins
        rel = Release()

        hi_ready, split_free = sem("hi_ready"), sem("split_free")

        def split_index(n):
            return sum(1 for m in range(n) if is_split(m))

        def is_split(m):
            return m >= moe0 or any(first[w, l] <= m < first[w, l] + c
                                    for w, l, c in (("merge", 0, N_MERGE), ("merge", 1, N_MERGE), ("mlp", 0, N_FFN)))

        def split_high(act, n, experts=0):
            k = split_index(n)
            have(act, n, experts)
            if k >= WS:
                act.wait_ge(split_free, k - WS + 1 + N_EXP * experts)
            s = (n % RING) * SLOT
            nc.scalar.activation(wh[:, k % WS, :], ring[:, s:s + SLOT], ACT.Copy).then_inc(hi_ready, 1)

        def split_low(dve, n, experts=0):
            k = split_index(n)
            dve.wait_ge(hi_ready, k + 1 + N_EXP * experts)
            s = (n % RING) * SLOT
            nc.vector.tensor_tensor(wl[:, k % WS, :], ring[:, s:s + SLOT], wh[:, k % WS, :].bitcast(F32), ALU.subtract
                                    ).then_inc(unit_used, 1)

        def halves(n, dims):
            k = split_index(n) % WS
            return [w[:, k, :].rearrange("p (a b) -> p a b", a=dims[0]) for w in (wh, wl)]

        def have_split(pe, n, experts=0):
            pe.wait_ge(unit_used, n + 1 + N_EXP * experts)

        def product(out, terms):
            for k, (a, b) in enumerate(terms):
                for q, (x, y) in enumerate(((a[0], b[0]), (a[0], b[1]), (a[1], b[0]))):
                    ins = rel.mm(out, x, y, start=(k == 0 and q == 0), stop=(k == len(terms) - 1 and q == 2))
            return ins

        x_high, x_low = sem("x_high"), sem("x_low")

        def inputs_high(act, at, pairs):
            for j, (x, h, _) in enumerate(pairs):
                nc.scalar.activation(h, x, ACT.Copy).then_inc(x_high, 1)

        def inputs_low(dve, at, pairs):
            for j, (x, h, l) in enumerate(pairs):
                dve.wait_ge(x_high, at + j + 1)
                nc.vector.tensor_tensor(l, x, h.bitcast(F32), ALU.subtract).then_inc(x_low, 1)

        class Chain:
            def __init__(self, eng, s):
                self.eng, self.s, self.n, self.base = eng, s, 0, 0

            def __call__(self, ins):
                ins.then_inc(self.s, 1)
                self.n += 1

            def sync(self):
                self.eng.wait_ge(self.s, self.base + self.n)

            def link(self, ins):
                self(ins)
                self.sync()

        dve_step, act_step, pool_step = sem("dve_step"), sem("act_step"), sem("pool_step")
        steps = {"dve": 0, "act": 0, "pool": 0}

        def chain(eng, which):
            c = Chain(eng, {"dve": dve_step, "act": act_step, "pool": pool_step}[which])
            c.n = steps[which]
            return c

        def keep(c, which):
            steps[which] = c.n

        x_in, ln_in = sem("x_in"), sem("ln_in")
        const_ready, ln_turned = sem("const_ready"), sem("ln_turned")
        lnrow = arena[0:80, 0:P]
        with nc.Block() as block:
            @block.sync
            def _(sp):
                sp.dma_start(resid[:, 0:2, :], A["x_prompt"][0].rearrange("(i p) d -> p i d", p=P)).then_inc(x_in, 16)
                sp.dma_start(resid[0:DEC, 2, :], A["x_sample"][0]).then_inc(x_in, 16)
                vec = [A["ln_in_g"], A["ln_in_b"]]
                for l in range(DEPTH):
                    vec += [A["ln1_g"][l], A["ln1_b"][l], A["ln2_g"][l], A["ln2_b"][l]]
                for j, v in enumerate(vec):
                    sp.dma_start(arena[KD * j:KD * j + KD, 0:P], v.rearrange("(k p) -> k p", p=P)).then_inc(ln_in, 16)
                load_units(sp, 0)

            @block.gpsimd
            def _(pool):
                c = chain(pool, "pool")
                c.link(nc.gpsimd.memset(ident[:], 0.0))
                c.link(nc.gpsimd.affine_select(out=ident[:], in_=ident[:], compare_op=ALU.not_equal, fill=1.0, base=0,
                                          pattern=[[-1, P]], channel_multiplier=1))
                c.link(nc.gpsimd.memset(mv[:], 1.0))
                c.link(nc.gpsimd.memset(wsm[:], 0.0))
                nc.gpsimd.memset(std[:], 1.0).then_inc(const_ready, 1)
                keep(c, "pool")

            @block.tensor
            def _(pe):
                pe.wait_ge(const_ready, 1)
                pe.wait_ge(ln_in, 160)
                nc.tensor.transpose(ps[0][:, 0:80], lnrow, ident[0:80, 0:80]).then_inc(ln_turned, 1)

            @block.vector
            def _(dve):
                dve.wait_ge(ln_turned, 1)
                dve.wait_ge(x_in, 32)
                c = chain(dve, "dve")
                c.link(nc.vector.tensor_copy(lnp[:], ps[0][:, 0:80].rearrange("p (j k) -> p j k", k=KD)))
                keep(c, "dve")

        masks_ready = sem("masks_ready")

        def masks(pool):
            c = chain(pool, "pool")
            c.link(nc.gpsimd.memset(ones[:], 1.0))
            c.link(nc.gpsimd.memset(cumU[:], 0.0))
            c.link(nc.gpsimd.memset(blk[:], 0.0))
            c.link(nc.gpsimd.memset(negL[:], 0.0))
            c.link(nc.gpsimd.memset(negU[:], 0.0))
            c.link(nc.gpsimd.memset(before[:], 1.0))
            c.link(nc.gpsimd.memset(adm[:], 0.0))
            c.link(nc.gpsimd.memset(d16[:], 0.0))
            c.sync()
            for a in range(0, P, CHUNK):
                s = slice(a, a + CHUNK)
                c.link(nc.gpsimd.memset(cumU[s, s], 1.0))
                c.link(nc.gpsimd.memset(blk[s, s], 1.0))
            for i in range(2):
                for half in range(2):
                    k0 = (2 * i + half + 1) * CHUNK
                    if k0 < SEQ:
                        c.link(nc.gpsimd.memset(adm[half * CHUNK:half * CHUNK + CHUNK, i, k0:SEQ], NEG))
            c.link(nc.gpsimd.affine_select(out=before[:], in_=before[:], compare_op=ALU.is_gt, fill=0.0, base=0,
                                      pattern=[[1, P]], channel_multiplier=-1))
            c.sync()
            c.link(nc.gpsimd.memset(d16[:], 1.0))
            d16v = d16[:].rearrange("p (b c) -> p b c", c=16)
            c.link(nc.gpsimd.affine_select(out=d16v, in_=d16v, compare_op=ALU.is_ge, fill=0.0, base=0,
                                           pattern=[[-16, 8], [0, 16]], channel_multiplier=1))
            c.link(nc.gpsimd.affine_select(out=d16v, in_=d16v, compare_op=ALU.is_ge, fill=0.0, base=15,
                                           pattern=[[16, 8], [0, 16]], channel_multiplier=-1))
            c.link(nc.gpsimd.affine_select(out=d16[:], in_=d16[:], compare_op=ALU.is_gt, fill=0.0, base=0,
                                           pattern=[[-1, P]], channel_multiplier=1))
            c.link(nc.gpsimd.affine_select(out=cumU[:], in_=cumU[:], compare_op=ALU.is_ge, fill=0.0, base=0,
                                           pattern=[[1, P]], channel_multiplier=-1))
            c.link(nc.gpsimd.affine_select(out=off16[:], in_=blk[:], compare_op=ALU.is_gt, fill=0.0, base=0,
                                           pattern=[[-1, P]], channel_multiplier=1))
            c.link(nc.gpsimd.tensor_tensor(off16[:], off16[:], d16[:], ALU.subtract))
            c.link(nc.gpsimd.affine_select(out=negL[:], in_=blk[:], compare_op=ALU.is_ge, fill=0.0, base=0,
                                           pattern=[[-1, P]], channel_multiplier=1))
            c.link(nc.gpsimd.tensor_scalar(negL[:], negL[:], 1.0, 1e30, ALU.subtract, ALU.mult))
            c.link(nc.gpsimd.tensor_scalar(negU[:], cumU[:], 1.0, 1e30, ALU.subtract, ALU.mult))
            c.link(nc.gpsimd.iota(itmp[:, 0:CAP], pattern=[[1, CAP]], base=0, channel_multiplier=0))
            c.link(nc.gpsimd.tensor_copy(iota[:], itmp[:, 0:CAP]))
            for i in range(NT):
                c.link(nc.gpsimd.iota(itmp[:, 0:PAST + DEC], pattern=[[1, PAST + DEC]], base=-TILES[i][0],
                                      channel_multiplier=-1))
                c.link(nc.gpsimd.tensor_copy(ndist[:, i, :], itmp[:, 0:PAST + DEC]))
            nc.gpsimd.memset(std[:], 1.0).then_inc(masks_ready, 1)
            keep(c, "pool")

        gb_in = sem("gb_in")
        var_ready, std_ready, hat_ready = sem("var_ready"), sem("std_ready"), sem("hat_ready")
        nrm_turned, stream_done, out_stored = sem("nrm_turned"), sem("stream_done"), sem("out_stored")

        def norm(call, j, g_vec, b_vec, keep_h=None, final=False, split_next=None):
            gb = gb_all
            whole = final or keep_h is not None
            src = resid if keep_h is None else keep_h
            with nc.Block() as block:
                @block.sync
                def _(sp):
                    sp.dma_start(gb[:, 0, :], g_vec.partition_broadcast(P)).then_inc(gb_in, 16)
                    sp.dma_start(gb[:, 1, :], b_vec.partition_broadcast(P)).then_inc(gb_in, 16)
                    if final:
                        for i in range(2):
                            sp.wait_ge(hat_ready, NT * call + i + 1)
                            sp.dma_start(OUT["y_prompt"][0, P * i:P * i + P, :], resid[:, i, :]).then_inc(out_stored, 16)
                        sp.wait_ge(hat_ready, NT * (call + 1))
                        sp.dma_start(OUT["y_sample"][0], resid[0:DEC, 2, :]).then_inc(out_stored, 16)
                        sp.wait_ge(out_stored, 48)

                @block.vector
                def _(dve):
                    c = chain(dve, "dve")
                    for i, (t0, n) in enumerate(TILES):
                        for a in range(2):
                            c(nc.vector.bn_stats(stats[0:n, i, a, :], resid[0:n, i, 512 * a:512 * a + 512]))
                    for i, (t0, n) in enumerate(TILES):
                        c.sync() if i == 0 else None
                        c(nc.vector.bn_aggr(mv[0:n, i, :], stats[0:n, i, :, :].rearrange("p a b -> p (a b)")))
                    c.sync()
                    nc.vector.tensor_scalar(rstd[:], mv[:, :, 1], LN_EPS, None, ALU.add).then_inc(var_ready, 1)
                    if whole:
                        dve.wait_ge(gb_in, 32 * (call + 1))
                        for i, (t0, n) in enumerate(TILES):
                            c(nc.vector.scalar_tensor_tensor(out=src[0:n, i, :], in0=resid[0:n, i, :], scalar=mv[0:n, i, 0:1],
                                                             in1=gb[0:n, 0, :], op0=ALU.subtract, op1=ALU.mult))
                    dve.wait_ge(std_ready, call + 1)
                    c.link(nc.vector.reciprocal(rstd[:], std[:]))
                    for i, (t0, n) in enumerate(TILES):
                        if whole:
                            ins = nc.vector.scalar_tensor_tensor(out=src[0:n, i, :], in0=src[0:n, i, :], scalar=rstd[0:n, i:i + 1],
                                                                 in1=gb[0:n, 1, :], op0=ALU.mult, op1=ALU.add)
                        else:
                            ins = nc.vector.tensor_scalar(resid[0:n, i, :], resid[0:n, i, :], mv[0:n, i, 0:1],
                                                          rstd[0:n, i:i + 1], ALU.subtract, ALU.mult)
                        ins.then_inc(hat_ready, 1)
                    if split_next is not None:
                        split_low(dve, split_next)
                    for k in range(1, 0 if final else KD, 2):
                        dve.wait_ge(nrm_turned, KD * call + k + 1)
                        if whole:
                            nc.vector.tensor_copy(hT[:, k, :], ps[k][:, 0:T])
                        else:
                            nc.vector.tensor_scalar(hT[:, k, :], ps[k][:, 0:T], lnp[:, 2 * j, k:k + 1],
                                                    lnp[:, 2 * j + 1, k:k + 1], ALU.mult, ALU.add)
                    if split_next is not None:
                        split_low(dve, split_next + 1)
                    keep(c, "dve")

                @block.scalar
                def _(act):
                    if split_next is not None:
                        split_high(act, split_next)
                        split_high(act, split_next + 1)
                    act.wait_ge(var_ready, call + 1)
                    nc.scalar.activation(std[:], rstd[:], ACT.Sqrt).then_inc(std_ready, 1)
                    for k in range(0, 0 if final else KD, 2):
                        act.wait_ge(nrm_turned, KD * call + k + 1)
                        if whole:
                            nc.scalar.activation(hT[:, k, :], ps[k][:, 0:T], ACT.Copy)
                        else:
                            nc.scalar.activation(hT[:, k, :], ps[k][:, 0:T], ACT.Identity,
                                                 bias=lnp[:, 2 * j + 1, k:k + 1], scale=lnp[:, 2 * j, k:k + 1])

                @block.tensor
                def _(pe):
                    for k in range(0 if final else KD):
                        for i, (t0, n) in enumerate(TILES):
                            if k == 0:
                                pe.wait_ge(hat_ready, NT * call + i + 1)
                            ins = nc.tensor.transpose(ps[k][:, t0:t0 + n], src[0:n, i, 128 * k:128 * k + 128], ident[0:n, 0:n])
                        ins.then_inc(nrm_turned, 1)

        def finish_stream(pool, call):
            c = chain(pool, "pool")
            pool.wait_ge(gb_in, 32 * (call + 1))
            for i, (t0, n) in enumerate(TILES):
                r = resid[0:n, i, :]
                c.link(nc.gpsimd.tensor_tensor(r, r, gb_all[0:n, 0, :], ALU.mult))
                c.link(nc.gpsimd.tensor_tensor(r, r, gb_all[0:n, 1, :], ALU.add))
                c.link(nc.gpsimd.tensor_scalar(r, r, ALPHA, None, ALU.mult))
            nc.gpsimd.memset(std[:], 1.0).then_inc(stream_done, 1)
            keep(c, "pool")

        mix_in, pre_turned, pre_evac = sem("mix_in"), sem("pre_turned"), sem("pre_evac")
        pj_done, pj_evac, conv_ready, silu_ready = sem("pj_done"), sem("pj_evac"), sem("conv_ready"), sem("silu_ready")
        post_turned, post_evac, new_stored, last_ready = sem("post_turned"), sem("post_evac"), sem("new_stored"), sem("last_ready")
        N_CH = 28

        def project(l):
            u0 = first["project", l]
            with nc.Block() as block:
                @block.sync
                def _(sp):
                    load_units(sp, u0 + N_PROJ)
                    sp.wait_ge(post_evac, 6 * (l + 1))
                    for name, src, w in (("k", knew, 2 * HD), ("v", None, 2 * HD), ("idx_k", inew, HD)):
                        op, os = OUT[f"new_{name}_p"][l, 0], OUT[f"new_{name}_s"][l, 0]
                        if name != "idx_k":
                            op, os = op.rearrange("t g d -> t (g d)"), os.rearrange("t g d -> t (g d)")
                        main = vtok[:, 0:2, :] if src is None else src[:, 0:2, :]
                        tail = vtok[0:DEC, 4, :] if src is None else src[0:DEC, 2, :]
                        sp.dma_start(op.rearrange("(i p) c -> p i c", p=P), main).then_inc(new_stored, 16)
                        sp.dma_start(os, tail).then_inc(new_stored, 16)
                    sp.dma_start(OUT["new_conv_p"][l, 0], lrow[0:3, :]).then_inc(new_stored, 16)
                    sp.dma_start(OUT["new_conv_s"][l, 0], lrow[3:6, :]).then_inc(new_stored, 16)

                @block.scalar
                def _(act):
                    act.dma_start(crow[0:CW, :], A["conv_w"][l]).then_inc(mix_in, 16)
                    act.dma_start(crow[CW:CW + 3, :], A["state_conv"][l, 0]).then_inc(mix_in, 16)
                    act.dma_start(ktok, A["cache_k"][l, 0].rearrange("(i p) g d -> p i (g d)", p=P)).then_inc(mix_in, 16)
                    act.dma_start(vtok[:, 2:4, :], A["cache_v"][l, 0].rearrange("(i p) g d -> p i (g d)", p=P)).then_inc(mix_in, 16)
                    for a in range(2):
                        act.dma_start(kitok[:, :, HD * a:HD * a + HD], A["cache_idx_k"][l, 0].rearrange("(i p) d -> p i d", p=P)
                                      ).then_inc(mix_in, 16)

                    def split(dst, src, at, smp, func=ACT.Copy):
                        nc.scalar.activation(dst[:, at:at + SEQ], src[:, 0:SEQ], func)
                        return nc.scalar.activation(dst[:, smp:smp + DEC], src[:, SEQ:T], func)

                    def silu(j):
                        act.wait_ge(conv_ready, CT * l + j + 1)
                        nc.scalar.activation(cT[:, j, :], cT[:, j, :], ACT.Silu).then_inc(silu_ready, 1)
                    for m in range(N_CH):
                        act.wait_ge(pj_done, N_CH * l + m + 1)
                        src = ps[m % 4][:, 0:T]
                        if m < 4:
                            ins = nc.scalar.activation(qaT[:, m, :], src, ACT.Copy, scale=HD ** -0.5)
                        elif m == 4:
                            ins = split(kT, src, 0, K_SMP)
                        elif m == 5:
                            ins = nc.scalar.activation(vT, src, ACT.Copy)
                        elif m < 10:
                            ins = nc.scalar.activation(qiT[:, m - 6, :], src, ACT.Copy)
                        elif m == 10:
                            ins = split(kiT, src, 0, K_SMP)
                        elif m == 11:
                            for i, (t0, n) in enumerate(TILES):
                                ins = nc.scalar.activation(wsm[0:n, i, :], ps[m % 4][0:n, 16 * i:16 * i + 16], ACT.Copy)
                        elif m < 24:
                            j = m - 12
                            ins = split(cin[:, j, :], src, CW - 1, 2 * (CW - 1) + SEQ)
                        else:
                            ins = nc.scalar.activation(zT[:, m - 24, :], src, ACT.Silu)
                        ins.then_inc(pj_evac, 1)
                        if m >= 16:
                            silu(m - 16)

                @block.tensor
                def _(pe):
                    def product(m, lhs, unit_of, last_use):
                        if m >= 4:
                            pe.wait_ge(pj_evac, N_CH * l + m - 3)
                        for k in range(KD):
                            if unit_of(k) is not None:
                                have(pe, unit_of(k))
                            ins = rel.mm(ps[m % 4][:, 0:T], lhs(k), hT[:, k, :], start=(k == 0), stop=(k == KD - 1))
                            if last_use and k == 3 and last_use == "pair":
                                rel.due = unit_used
                        ins.then_inc(pj_done, 1)
                        if last_use:
                            rel.due = unit_used

                    def pairview(n):
                        s = (n % RING) * SLOT
                        return ring[:, s:s + 2 * SLOT].rearrange("p (k c) -> p k c", c=512)
                    qw = pairview(u0)
                    for c in range(4):
                        product(c, lambda k: qw[:, k, P * c:P * c + P], lambda k: u0 + k // 4 if c == 0 and k % 4 == 0 else None, "pair" if c == 3 else "")
                    pe.wait_ge(mix_in, 96 * (l + 1))
                    for j in range(CT):
                        ins = nc.tensor.transpose(ps[4][:, 8 * j:8 * j + 7], crow[0:7, P * j:P * j + P], ident[0:7, 0:7])
                    for i in range(2):
                        nc.tensor.transpose(ps[5][:, P * i:P * i + P], ktok[:, i, :], ident[:])
                    for i in range(2):
                        ins = nc.tensor.transpose(ps[5][:, 256 + P * i:256 + P * i + P], kitok[:, i, :], ident[:])
                    ins.then_inc(pre_turned, 1)
                    kv = slot(u0 + 2, (8, 256))
                    for c in range(2):
                        product(4 + c, lambda k: kv[:, k, P * c:P * c + P], lambda k: u0 + 2 if k == 0 else None, c == 1)
                    iw = pairview(u0 + 3)
                    for c in range(4):
                        product(6 + c, lambda k: iw[:, k, P * c:P * c + P],
                                lambda k: u0 + 3 + k // 4 if c == 0 and k % 4 == 0 else None, "pair" if c == 3 else "")
                    sw = slot(u0 + 5, (8, 80))
                    pe.wait_ge(pj_evac, N_CH * l + 10 - 3)
                    have(pe, u0 + 5)
                    for half in range(2):
                        for k in range(KD):
                            ins = rel.mm(ps[10 % 4][64 * half:64 * half + 64, 0:T], sw[:, k, 0:HD], hT[:, k, :],
                                         start=(k == 0), stop=(k == KD - 1))
                    ins.then_inc(pj_done, 1)
                    pe.wait_ge(pj_evac, N_CH * l + 11 - 3)
                    for i, (t0, n) in enumerate(TILES):
                        for k in range(KD):
                            ins = rel.mm(ps[11 % 4][0:n, 16 * i:16 * i + 16], hT[:, k, t0:t0 + n], sw[:, k, HD:80],
                                         start=(k == 0), stop=(k == KD - 1))
                    ins.then_inc(pj_done, 1)
                    rel.due = unit_used
                    for j in range(8):
                        n = u0 + 6 + j
                        w = slot(n, (8, 256))
                        for c in range(2):
                            product(12 + 2 * j + c, lambda k: w[:, k, P * c:P * c + P], lambda k: n if k == 0 else None, c == 1)
                    for i, (t0, n) in enumerate(TILES):
                        ins = rel.mm(ps[5][0:n, P * i:P * i + P], vT[:, t0:t0 + n], ident[:], is_transpose=True,
                                     start=True, stop=True)
                    ins.then_inc(post_turned, 1)
                    for i, (t0, n) in enumerate(TILES):
                        k0 = t0 if i < 2 else K_SMP
                        ins = nc.tensor.transpose(ps[6][0:n, P * i:P * i + P], kT[:, k0:k0 + n], ident[:])
                    ins.then_inc(post_turned, 1)
                    for i, (t0, n) in enumerate(TILES):
                        k0 = t0 if i < 2 else K_SMP
                        ins = nc.tensor.transpose(ps[7][0:n, HD * i:HD * i + HD], kiT[0:HD, k0:k0 + n], ident[0:HD, 0:HD])
                    ins.then_inc(post_turned, 1)
                    pe.wait_ge(last_ready, l + 1)
                    pe.wait_ge(pj_evac, N_CH * l + 24)
                    for g, b in enumerate((4, 0, 1)):
                        if b < 4:
                            pe.wait_ge(pj_evac, N_CH * l + 25 + b)
                        for j in range(4):
                            ins = nc.tensor.transpose(ps[b][0:6, P * j:P * j + P], last[:, 4 * g + j, :], ident[:])
                        ins.then_inc(post_turned, 1)

                @block.gpsimd
                def _(pool):
                    if l == 0:
                        masks(pool)
                    finish_stream(pool, 2 * l)

                @block.vector
                def _(dve):
                    c = chain(dve, "dve")
                    nc.vector.memset(cin[:, :, 0:3], 0.0).then_inc(pre_evac, 1)
                    dve.wait_ge(pre_turned, l + 1)
                    cwv = ps[4][:, 0:8 * CT].rearrange("p (j a) -> p j a", a=8)
                    c(nc.vector.tensor_copy(cw[:, :, 0:7], cwv[:, :, 0:7]))
                    nc.vector.tensor_copy(cin[:, :, CW - 1 + SEQ:2 * (CW - 1) + SEQ], cwv[:, :, CW:CW + 3]).then_inc(pre_evac, 1)
                    nc.vector.tensor_copy(kT[:, K_CACHE:K_SMP], ps[5][:, 0:256]).then_inc(pre_evac, 1)
                    nc.vector.tensor_copy(kiT[:, K_CACHE:K_SMP], ps[5][:, 256:512]).then_inc(pre_evac, 1)
                    dve.wait_ge(pre_evac, 4 * (l + 1))
                    c.sync()
                    for j in range(CT):
                        dve.wait_ge(pj_evac, N_CH * l + 12 + j + 1)
                        for a in range(CW):
                            tap = cw[:, j, a:a + 1]
                            src = cin[:, j, a:a + CO]
                            if a == 0:
                                c.link(nc.vector.tensor_scalar(cT[:, j, :], src, tap, None, ALU.mult))
                            else:
                                ins = nc.vector.scalar_tensor_tensor(out=cT[:, j, :], in0=src, scalar=tap, in1=cT[:, j, :],
                                                                     op0=ALU.mult, op1=ALU.add)
                                if a < CW - 1:
                                    c.link(ins)
                                else:
                                    ins.then_inc(conv_ready, 1)
                        nc.vector.tensor_copy(last[:, j, 0:3], cin[:, j, SEQ:SEQ + 3])
                        ins = nc.vector.tensor_copy(last[:, j, 3:6], cin[:, j, CI - 3:CI])
                    ins.then_inc(last_ready, 1)
                    dve.wait_ge(post_turned, 6 * l + 1)
                    nc.vector.tensor_copy(vtok[:, 0:2, :], ps[5][:, 0:256].rearrange("p (i c) -> p i c", i=2))
                    nc.vector.tensor_copy(vtok[0:DEC, 4, :], ps[5][0:DEC, 256:384]).then_inc(post_evac, 1)
                    dve.wait_ge(post_turned, 6 * l + 2)
                    nc.vector.tensor_copy(knew[:, 0:2, :], ps[6][:, 0:256].rearrange("p (i c) -> p i c", i=2))
                    nc.vector.tensor_copy(knew[0:DEC, 2, :], ps[6][0:DEC, 256:384]).then_inc(post_evac, 1)
                    dve.wait_ge(post_turned, 6 * l + 3)
                    nc.vector.tensor_copy(inew[:, 0:2, :], ps[7][:, 0:128].rearrange("p (i c) -> p i c", i=2))
                    nc.vector.tensor_copy(inew[0:DEC, 2, :], ps[7][0:DEC, 128:192]).then_inc(post_evac, 1)
                    for g, b in enumerate((4, 0, 1)):
                        dve.wait_ge(post_turned, 6 * l + 4 + g)
                        nc.vector.tensor_copy(lrow[0:6, 512 * g:512 * g + 512], ps[b][0:6, :]).then_inc(post_evac, 1)
                    if l == 0:
                        dve.wait_ge(masks_ready, 1)
                        c.link(nc.vector.scalar_tensor_tensor(out=ndist[:], in0=ndist[:], scalar=-1.0, in1=ndist[:],
                                                              op0=ALU.mult, op1=ALU.min))
                    keep(c, "dve")

        gate_done, gate_read = sem("gate_done"), sem("gate_read")
        GATES_ATT, GATES_FIRST, GATES_REC = 2, 4, 2 * KD - 5

        def gate_bank(q):
            return ps[4 + q if q < GATES_ATT else (6 if q < GATES_REC else 2) + q % 2]

        def gate_products(pe, l, z0, z1):
            for z in range(z0, z1):
                q, k = z // KD, z % KD
                n = first["gate", l] + q // 2
                if k == 0 and q % 2 == 0:
                    have(pe, n)
                if k == 0 and q >= GATES_ATT:
                    pe.wait_ge(gate_read, 2 * KD * l + q - 1)
                ins = rel.mm(gate_bank(q)[:, 0:T], slot(n, (8, 256))[:, k, P * (q % 2):P * (q % 2) + P], hT[:, k, :],
                             start=(k == 0), stop=(k == KD - 1))
                if k == KD - 1:
                    if q < 2 * KD - 1:
                        ins.then_inc(gate_done, 1)
                        if q % 2:
                            rel.due = unit_used
                    else:
                        ins.then_inc(unit_used, 1)

        def gates_out(act, l, q0, q1):
            for q in range(q0, q1):
                if q < 2 * KD - 1:
                    act.wait_ge(gate_done, (2 * KD - 1) * l + q + 1)
                else:
                    act.wait_ge(unit_used, first["gate", l] + N_GATE)
                nc.scalar.activation(tanhs[:, (q + KD) % (2 * KD), :], gate_bank(q)[:, 0:T], ACT.Tanh, scale=0.5
                                     ).then_inc(gate_read, 1)

        it_done, it_read, score_ready, pen_ready, away_ready = (sem("it_done"), sem("it_read"), sem("score_ready"),
                                                                sem("pen_ready"), sem("away_ready"))
        lg_done, mx_ready, exp_done = sem("lg_done"), sem("mx_ready"), sem("exp_done")
        v_done, orow_ready, o_turned, oa_ready = sem("v_done"), sem("orow_ready"), sem("o_turned"), sem("oa_ready")
        at_ = Area()
        at_.at = ATT0
        SMAX = PAST + DEC
        relu = at_(2 * IH, SMAX)
        prob = at_(A_HEADS, SMAX)
        probT = at_(3, A_HEADS * P)
        score = at_(SMAX)
        orow = at_(A_HEADS, HD)
        top8 = at_(8)
        nmx = at_(A_HEADS)
        den = at_(A_HEADS)
        rden = at_(A_HEADS)
        wis = at_(NT, IH)
        assert at_.at <= STORED0
        TURNS = []
        for kind, i in (("I", 0), ("I", 1), ("T", 0), ("I", 2), ("T", 1), ("T", 2)):
            TURNS += [(kind, i, g) for g in range(IH if kind == "I" else 2 * len(VT[i]))]
        NTURN = len(TURNS)

        def attend(l):
            def turn_of(kind, i, g):
                return TURNS.index((kind, i, g))
            with nc.Block() as block:
                @block.sync
                def _(sp):
                    load_units(sp, first["gate", l] + GATES_ATT // 2 - 1)
                    sp.wait_ge(new_stored, 160 * l + 128)

                @block.gpsimd
                def _(pool):
                    c = chain(pool, "pool")
                    c.link(nc.gpsimd.tensor_copy(identr[:], ident[:]))
                    for h in range(A_HEADS):
                        c.link(nc.gpsimd.tensor_scalar(slopes[:, h, :], ident[:], 2.0 ** -(h + 1), None, ALU.mult))
                    nc.gpsimd.tensor_copy(distr[:], ndist[:]).then_inc(pen_ready, 1)
                    keep(c, "pool")

                @block.tensor
                def _(pe):
                    def room(k):
                        if k >= 3:
                            pe.wait_ge(it_read, l * NTURN + k - 2)

                    def indexer(i):
                        (t0, n), (k0, s) = TILES[i], KEYS[i]
                        for h in range(IH):
                            k = turn_of("I", i, h)
                            room(k)
                            r = slice(HD * (h % 2), HD * (h % 2) + HD)
                            nc.tensor.matmul(ps[k % 3][0:n, 0:s], qiT[r, h // 2, t0:t0 + n], kiT[r, k0:k0 + s],
                                             start=True, stop=True).then_inc(it_done, 1)

                    def logits(i):
                        (t0, n), (k0, s) = TILES[i], KEYS[i]
                        for h in range(A_HEADS):
                            if A_HEADS * i + h >= 4:
                                pe.wait_ge(exp_done, A_HEADS * (l * NT + i) + h - 3)
                            b = ps[4 + h % 4][0:n, 0:s]
                            r = slice(HD * (h // 4), HD * (h // 4) + HD)
                            nc.tensor.matmul(b, qaT[r, h % 4, t0:t0 + n], kT[r, k0:k0 + s], start=True, stop=False)
                            if i == 0 and h == 0:
                                pe.wait_ge(pen_ready, l + 1)
                            nc.tensor.matmul(b, slopes[0:n, h, 0:n], distr[0:n, i, 0:s], start=False, stop=False)
                            if h == 0:
                                pe.wait_ge(away_ready, l * NT + i + 1)
                            nc.tensor.matmul(b, identr[0:n, 0:n], away[0:n, 0:s], start=False, stop=True).then_inc(lg_done, 1)

                    def turn(i):
                        (t0, n), (k0, s) = TILES[i], KEYS[i]
                        pe.wait_ge(exp_done, A_HEADS * (l * NT + i + 1))
                        for g in range(2 * len(VT[i])):
                            ck, j = g // 2, g % 2
                            kc = min(P, s - P * ck)
                            k = turn_of("T", i, g)
                            room(k)
                            for q in range(4):
                                ins = nc.tensor.transpose(ps[k % 3][0:kc, n * q:n * q + n],
                                                          prob[0:n, 4 * j + q, P * ck:P * ck + kc], ident[0:n, 0:n])
                            ins.then_inc(it_done, 1)

                    def values(i):
                        (t0, n), (k0, s) = TILES[i], KEYS[i]
                        pe.wait_ge(it_read, l * NTURN + turn_of("T", i, 2 * len(VT[i]) - 1) + 1)
                        if i:
                            pe.wait_ge(oa_ready, l * NT + i)
                        for h in range(A_HEADS):
                            for ck, vt in enumerate(VT[i]):
                                kc = min(P, s - P * ck)
                                ins = nc.tensor.matmul(ps[3][0:n, HD * h:HD * h + HD], probT[0:kc, ck, n * h:n * h + n],
                                                       vtok[0:kc, vt, HD * (h // 4):HD * (h // 4) + HD], start=(ck == 0),
                                                       stop=(ck == len(VT[i]) - 1))
                        ins.then_inc(v_done, 1)

                    def turn_out(i):
                        n = TILES[i][1]
                        pe.wait_ge(orow_ready, l * NT + i + 1)
                        for c in range(4):
                            ins = nc.tensor.transpose(ps[3][:, P * c:P * c + n], orow[0:n, 2 * c:2 * c + 2, :]
                                                      .rearrange("p a d -> p (a d)"), ident[0:n, 0:n])
                        ins.then_inc(o_turned, 1)

                    indexer(0)
                    indexer(1)
                    gate_products(pe, l, 0, KD * GATES_ATT)
                    pe.wait_ge(gate_read, 2 * KD * l + GATES_ATT)
                    logits(0)
                    turn(0)
                    indexer(2)
                    values(0)
                    logits(1)
                    turn_out(0)
                    turn(1)
                    values(1)
                    logits(2)
                    turn_out(1)
                    turn(2)
                    values(2)
                    turn_out(2)

                @block.scalar
                def _(act):
                    def relus(i):
                        (t0, n), (k0, s) = TILES[i], KEYS[i]
                        if i == 2:
                            act.wait_ge(score_ready, l * NT + 1)
                        for h in range(IH):
                            k = turn_of("I", i, h)
                            act.wait_ge(it_done, l * NTURN + k + 1)
                            nc.scalar.activation(relu[0:n, IH * (i % 2) + h, 0:s], ps[k % 3][0:n, 0:s], ACT.Relu
                                                 ).then_inc(it_read, 1)

                    def exps(i):
                        (t0, n), (k0, s) = TILES[i], KEYS[i]
                        for h in range(A_HEADS):
                            act.wait_ge(mx_ready, A_HEADS * (l * NT + i) + h + 1)
                            nc.scalar.activation(prob[0:n, h, 0:s], ps[4 + h % 4][0:n, 0:s], ACT.Exp, bias=nmx[0:n, h:h + 1],
                                                 accum_out=den[0:n, h:h + 1]).then_inc(exp_done, 1)

                    def turned(i):
                        (t0, n), (k0, s) = TILES[i], KEYS[i]
                        for g in range(2 * len(VT[i])):
                            ck, j = g // 2, g % 2
                            kc = min(P, s - P * ck)
                            k = turn_of("T", i, g)
                            act.wait_ge(it_done, l * NTURN + k + 1)
                            nc.scalar.activation(probT[0:kc, ck, 4 * j * n:4 * j * n + 4 * n], ps[k % 3][0:kc, 0:4 * n],
                                                 ACT.Copy).then_inc(it_read, 1)

                    def outs(i):
                        t0, n = TILES[i]
                        act.wait_ge(o_turned, l * NT + i + 1)
                        nc.scalar.activation(oaT[:, :, t0:t0 + n], ps[3][:, :].rearrange("p (c t) -> p c t", c=4)[:, :, 0:n],
                                             ACT.Copy).then_inc(oa_ready, 1)
                    relus(0)
                    relus(1)
                    gates_out(act, l, 0, GATES_ATT)
                    exps(0)
                    turned(0)
                    relus(2)
                    exps(1)
                    outs(0)
                    turned(1)
                    exps(2)
                    outs(1)
                    turned(2)
                    outs(2)

                @block.vector
                def _(dve):
                    c = chain(dve, "dve")
                    c.link(nc.vector.tensor_scalar(wis, wsm[:, :, 0:IH], HD ** -0.5, None, ALU.mult))

                    def choose(i):
                        (t0, n), (k0, s) = TILES[i], KEYS[i]
                        sc = score[0:n, 0:s]
                        for h in range(IH):
                            dve.wait_ge(it_read, l * NTURN + turn_of("I", i, h) + 1)
                            w = wis[0:n, i, h:h + 1]
                            x = relu[0:n, IH * (i % 2) + h, 0:s]
                            if h == 0:
                                c.link(nc.vector.tensor_scalar(sc, x, w, None, ALU.mult))
                            else:
                                ins = nc.vector.scalar_tensor_tensor(out=sc, in0=x, scalar=w, in1=sc,
                                                                     op0=ALU.mult, op1=ALU.add)
                                if h < IH - 1:
                                    c.link(ins)
                                else:
                                    ins.then_inc(score_ready, 1)
                        dve.wait_ge(score_ready, l * NT + i + 1)
                        if i < 2:
                            c.link(nc.vector.tensor_tensor(sc, sc, adm[0:n, i, 0:s], ALU.add))
                        assert NSEL[i] % 8 == 0
                        for _ in range(NSEL[i] // 8):
                            c.link(nc.vector.max(top8[0:n], sc))
                            c.link(nc.vector.match_replace(out=sc, in_to_replace=top8[0:n], in_values=sc, imm_value=TAKEN))
                        nc.vector.tensor_scalar(away[0:n, 0:s], sc, TAKEN, -1e30, ALU.not_equal, ALU.mult).then_inc(away_ready, 1)

                    def maxima(i):
                        (t0, n), (k0, s) = TILES[i], KEYS[i]
                        for h in range(A_HEADS):
                            dve.wait_ge(lg_done, A_HEADS * (l * NT + i) + h + 1)
                            nc.vector.tensor_reduce(nmx[0:n, h:h + 1], ps[4 + h % 4][0:n, 0:s], AX.X, ALU.max, negate=True
                                                    ).then_inc(mx_ready, 1)

                    def normalise(i):
                        n = TILES[i][1]
                        dve.wait_ge(v_done, l * NT + i + 1)
                        c.link(nc.vector.reciprocal(rden[0:n], den[0:n]))
                        nc.vector.tensor_tensor(orow[0:n], ps[3][0:n, :].rearrange("p (h d) -> p h d", h=A_HEADS),
                                                rden[0:n].unsqueeze(2).to_broadcast([n, A_HEADS, HD]), ALU.mult
                                                ).then_inc(orow_ready, 1)
                    choose(0)
                    maxima(0)
                    choose(1)
                    normalise(0)
                    maxima(1)
                    choose(2)
                    normalise(1)
                    maxima(2)
                    normalise(2)
                    keep(c, "dve")

        PREP = ["norm", "qk", "v", "grow", "qT", "kT", "qdT", "KK", "QKT", "MdT", "MoT", "P2", "P2T", "X1", "P4", "P4T",
                "X2", "P8", "X3", "X3T", "B", "BT", "Y1", "B2", "TT", "u", "wT"]
        BY_DVE = {"norm", "qk", "v", "grow", "KK", "QKT", "X1", "X2", "X3", "Y1", "TT"}
        RN = {r: k for k, r in enumerate(PREP)}
        DV = [r for r in PREP if r in BY_DVE]
        AC = [r for r in PREP if r not in BY_DVE]
        dl_in, sq_ready, g_ready = sem("dl_in"), sem("sq_ready"), sem("g_ready")
        prep_done, prep_dve, prep_act = sem("prep_done"), sem("prep_dve"), sem("prep_act")
        sm_dve, sm_act, egl_done, egl_ready = sem("sm_dve"), sem("sm_act"), sem("egl_done"), sem("egl_ready")
        dec_in, dec_ready, x_ready = sem("dec_in"), sem("dec_ready"), sem("x_ready")
        ws_done, vnew_ready, o_done, o_ready = sem("ws_done"), sem("vnew_ready"), sem("o_done"), sem("o_ready")
        ds_done, s_ready, on_ready, ot_done, ob_ready = (sem("ds_done"), sem("s_ready"), sem("on_ready"), sem("ot_done"),
                                                         sem("ob_ready"))
        ssq_ready, rn_ready = sem("ssq_ready"), sem("rn_ready")
        H4 = B_HEADS
        da = Area()
        sq = da(2 * H4, CO)
        SQ_END = da.at
        da.at = 0
        USES = [("q", "Md", "P4T", "XT", "vnew"), ("k", "Mo", "X", "TT"), ("qd", "MdT", "u"),
                ("gtri", "qT", "PT", "P8", "B2", "on"), ("kT", "P", "BT", "o"), ("E", "MoT", "wT"), ("ET", "P4", "B"),
                ("QKT",), ("qdT",), ("kbG",), ("kt",), ("vb",)]
        WIDE = {"q", "k", "qd", "u", "vnew", "o", "on", "kbG", "kt", "vb"}
        tl = []
        for i in range(NT):
            n = TILES[i][1]
            d = {}
            for names in USES:
                at = da.at
                da.at += H4 * (BD if WIDE & set(names) else n)
                for x in names:
                    w = BD if x in WIDE else n
                    d[x] = arena[:, at:at + H4 * w].rearrange("p (h x) -> p h x", h=H4)
            tl.append(d)
        osq = da(H4, BD)
        da.at = max(da.at, SQ_END)
        state = da(2, H4 * BD).rearrange("p s (h v) -> p s h v", h=H4)
        prm = da(2, H4)
        gn = da(2)
        sp_ = da(3, NT * H4).rearrange("p a (i h) -> p a i h", i=NT)
        gv = da(NT, H4)
        nG = da(NT, H4)
        nbeta = da(NT, H4)
        nrm16 = da(NT, 16)
        sc = da(NT, 6 * H4).rearrange("p i (a h) -> p i a h", a=6)
        eg = da(5, H4)
        rr = da(NT, H4)
        SC_Q, SC_QD, SC_K, SC_KBG, SC_KT, SC_VB = range(6)
        SEQS = [(0, 0, 0, 0), (2, 0, 1, 4), (0, 64, 0, 1), (1, 0, 0, 2), (1, 64, 0, 3)]

        def delta(l):
            NR = len(PREP)
            sb_ = l * NT

            def at_round(r, i):
                return (l * NR + RN[r]) * NT + i + 1

            def evac_of(r, i):
                if r in BY_DVE:
                    return prep_dve, (l * len(DV) + DV.index(r)) * NT + i + 1
                return prep_act, (l * len(AC) + AC.index(r)) * NT + i + 1

            def bank(r, i):
                return ps[2 * i + RN[r] % 2]

            def gates_by(k):
                return KD * GATES_FIRST + KD * (GATES_REC - GATES_FIRST) * k // (NR - 2)


            def v4(ap, n, w):
                return ap[0:n, 0:H4 * w].rearrange("p (h x) -> p h x", h=H4)

            with nc.Block() as block:
                @block.sync
                def _(sp):
                    sp.dma_start(prm[:, 0, :], A["a_log"][l].partition_broadcast(P)).then_inc(dl_in, 16)
                    sp.dma_start(prm[:, 1, :], A["dt_bias"][l].partition_broadcast(P)).then_inc(dl_in, 16)
                    sp.dma_start(gn[:, 0:1], A["gnorm_g"][l].rearrange("(p a) -> p a", a=1)).then_inc(dl_in, 16)
                    sp.dma_start(state[:, 1, :, :], A["state_gdn"][l, 0].rearrange("h k v -> k h v")).then_inc(dl_in, 16)
                    load_units(sp, first["gate", l] + N_GATE)
                    sp.wait_ge(s_ready, len(SEQS) * (l + 1))
                    sp.dma_start(OUT["new_gdn_p"][l, 0].rearrange("h k v -> k h v"), state[:, 0, :, :]).then_inc(new_stored, 16)
                    sp.dma_start(OUT["new_gdn_s"][l, 0].rearrange("h k v -> k h v"), state[:, 1, :, :]).then_inc(new_stored, 16)
                    sp.wait_ge(new_stored, 160 * (l + 1))

                @block.gpsimd
                def _(pool):
                    nc.gpsimd.tensor_tensor(sq, cT[:, 0:2 * H4, :], cT[:, 0:2 * H4, :], ALU.mult).then_inc(sq_ready, 1)

                @block.tensor
                def _(pe):
                    def need(r, i):
                        s, v = evac_of(r, i)
                        pe.wait_ge(s, v)
                    gate_products(pe, l, KD * GATES_ATT, KD * GATES_FIRST)
                    pe.wait_ge(gate_read, 2 * KD * l + GATES_FIRST)
                    pe.wait_ge(sq_ready, l + 1)
                    pe.wait_ge(g_ready, l + 1)
                    for i, (t0, n) in enumerate(TILES):
                        b = ps[6]
                        if i:
                            need("norm", i - 1)
                        for h in range(2 * H4):
                            nc.tensor.matmul(b[0:n, 16 * i + h:16 * i + h + 1], sq[:, h, CCOL[i]:CCOL[i] + n], ones[:, 0:1],
                                             start=True, stop=True)
                        nc.tensor.matmul(b[0:n, 16 * i + 8:16 * i + 12], cumU[0:n, 0:n], gv[0:n, i, :], start=True, stop=True)
                        nc.tensor.matmul(b[0:n, 16 * i + 12:16 * i + 16], blk[0:n, 0:n], gv[0:n, i, :], start=True,
                                         stop=True).then_inc(prep_done, 1)
                    for (i, r0, s, ch) in SEQS:
                        n = TILES[i][1]
                        ins = nc.tensor.matmul(ps[7][:, H4 * ch:H4 * ch + H4], blk[0:n, r0:r0 + 1].to_broadcast([n, P]),
                                               gv[0:n, i, :], start=True, stop=True)
                    ins.then_inc(egl_done, 1)

                    def turns(r, src, w_in, w_out):
                        def f(i, n, h, b):
                            ri, wi_ = (n if w_in is None else w_in), (n if w_out is None else w_out)
                            return nc.tensor.transpose(v4(b, wi_, ri)[:, h, :], src(i, h), ident[0:ri, 0:ri])
                        return f

                    def mul(lhs, rhs, w=None):
                        def f(i, n, h, b):
                            ww = n if w is None else w
                            d = tl[i]
                            return nc.tensor.matmul(v4(b, n, ww)[:, h, :], d[lhs][0:n, h, :], d[rhs][0:n, h, :],
                                                    start=True, stop=True)
                        return f

                    def deep(lhs, rhs):
                        def f(i, n, h, b):
                            d = tl[i]
                            return nc.tensor.matmul(v4(b, n, n)[:, h, :], d[lhs][:, h, :], d[rhs][:, h, :],
                                                    start=True, stop=True)
                        return f

                    def tok(c0):
                        def f(i, n, h, b):
                            return nc.tensor.transpose(v4(b, n, BD)[:, h, :], cT[:, c0 + h, CCOL[i]:CCOL[i] + n], ident[:])
                        return f

                    for i, (t0, n) in enumerate(TILES):
                        for h in range(H4):
                            tok(0)(i, n, h, ps[2 * i])
                        for h in range(H4):
                            ins = tok(H4)(i, n, h, ps[2 * i + 1])
                        ins.then_inc(prep_done, 1)
                    T3 = {
                        "v": (tok(2 * H4), ["qk"]),
                        "grow": (lambda i, n, h, b: nc.tensor.matmul(
                            v4(b, n, n)[:, h, :], ones[0:n, 0:n], tl[i]["gtri"][0:n, h, :], start=True, stop=True), ["qk"]),
                        "qT": (lambda i, n, h, b: nc.tensor.transpose(
                            v4(b, BD, n)[:, h, :], tl[i]["q"][0:n, h, :], ident[0:n, 0:n]), ["v"]),
                        "kT": (lambda i, n, h, b: nc.tensor.transpose(
                            v4(b, BD, n)[:, h, :], tl[i]["k"][0:n, h, :], ident[0:n, 0:n]), ["grow"]),
                        "qdT": (lambda i, n, h, b: nc.tensor.transpose(
                            v4(b, BD, n)[:, h, :], tl[i]["qd"][0:n, h, :], ident[0:n, 0:n]), ["qT"]),
                        "KK": (deep("kT", "kT"), ["kT"]),
                        "QKT": (deep("kT", "qT"), ["qdT"]),
                        "MdT": (lambda i, n, h, b: nc.tensor.transpose(
                            v4(b, n, n)[:, h, :], tl[i]["Md"][0:n, h, :], ident[0:n, 0:n]), ["KK"]),
                        "MoT": (lambda i, n, h, b: nc.tensor.transpose(
                            v4(b, n, n)[:, h, :], tl[i]["Mo"][0:n, h, :], ident[0:n, 0:n]), ["QKT"]),
                        "P2": (mul("MdT", "Md"), ["MdT"]),
                        "P2T": (mul("Md", "MdT"), ["MoT"]),
                        "X1": (mul("P", "X"), ["P2"]),
                        "P4": (mul("PT", "P"), ["P2T"]),
                        "P4T": (mul("P", "PT"), ["X1"]),
                        "X2": (mul("P4", "X"), ["P4"]),
                        "P8": (mul("P4T", "P4"), ["P4T"]),
                        "X3": (mul("P8", "X"), ["X2", "P8"]),
                        "X3T": (lambda i, n, h, b: nc.tensor.transpose(
                            v4(b, n, n)[:, h, :], tl[i]["X"][0:n, h, :], ident[0:n, 0:n]), ["X3"]),
                        "B": (mul("MoT", "XT"), ["X3T"]),
                        "BT": (mul("XT", "MoT"), ["X3T"]),
                        "Y1": (mul("B", "X"), ["B"]),
                        "B2": (mul("BT", "B"), ["BT"]),
                        "TT": (mul("B2", "X"), ["B2", "Y1"]),
                        "u": (mul("TT", "vb", BD), ["TT"]),
                        "wT": (lambda i, n, h, b: nc.tensor.matmul(
                            v4(b, BD, n)[:, h, :], tl[i]["kbG"][0:n, h, :], tl[i]["TT"][0:n, h, :], start=True, stop=True),
                            ["TT"]),
                    }
                    for r in PREP[2:]:
                        f, needs = T3[r]
                        for i, (t0, n) in enumerate(TILES):
                            prev = PREP[RN[r] - 2]
                            if RN[r] - 2 >= 1:
                                need(prev, i)
                            for x in needs:
                                need(x, i)
                            if r == "grow":
                                pe.wait_ge(dec_in, sb_ + i + 1)
                            if r == "X1":
                                pe.wait_ge(x_ready, sb_ + i + 1)
                            for h in range(H4):
                                ins = f(i, n, h, bank(r, i))
                            ins.then_inc(prep_done, 1)
                        gate_products(pe, l, gates_by(RN[r] - 2), gates_by(RN[r] - 1))
                    pe.wait_ge(gate_read, 2 * KD * l + GATES_REC)
                    need("u", 1)
                    need("wT", 1)

                    for q, (i, r0, s, ch) in enumerate(SEQS):
                        n = min(CHUNK, TILES[i][1])
                        R = slice(r0, r0 + n)
                        d = tl[i]
                        g = len(SEQS) * l + q
                        need("u", i)
                        need("wT", i)
                        if q == 0:
                            pe.wait_ge(egl_ready, l + 1)
                        elif q == 1:
                            pe.wait_ge(dl_in, 64 * (l + 1))
                        else:
                            pe.wait_ge(s_ready, g)
                        if q:
                            pe.wait_ge(vnew_ready, g)
                        A_, B_, C_ = ps[6], ps[7], ps[0]
                        for h in range(H4):
                            ins = nc.tensor.matmul(A_[R, BD * h:BD * h + BD], d["wT"][:, h, R], state[:, s, h, :],
                                                   start=True, stop=True)
                        ins.then_inc(ws_done, 1)
                        z = KD * (GATES_REC + q)
                        gate_products(pe, l, z, z + 3)
                        pe.wait_ge(vnew_ready, g + 1)
                        if q:
                            pe.wait_ge(o_ready, g)
                            pe.wait_ge(s_ready, g)
                        for h in range(H4):
                            ins = nc.tensor.matmul(C_[:, BD * h:BD * h + BD], d["kt"][R, h, :], d["vnew"][R, h, :],
                                                   start=True, stop=True)
                        ins.then_inc(ds_done, 1)
                        for h in range(H4):
                            nc.tensor.matmul(B_[R, BD * h:BD * h + BD], d["qdT"][:, h, R], state[:, s, h, :],
                                             start=True, stop=False)
                            ins = nc.tensor.matmul(B_[R, BD * h:BD * h + BD], d["QKT"][R, h, R], d["vnew"][R, h, :],
                                                   start=False, stop=True)
                        ins.then_inc(o_done, 1)
                        gate_products(pe, l, z + 3, z + KD)
                    pe.wait_ge(gate_read, 2 * KD * (l + 1))
                    for i, (t0, n) in enumerate(TILES):
                        pe.wait_ge(on_ready, sb_ + i + 1)
                        for h in range(H4):
                            ins = nc.tensor.transpose(v4(ps[1 + i], BD, n)[:, h, :], tl[i]["on"][0:n, h, :], ident[0:n, 0:n])
                        ins.then_inc(ot_done, 1)

                @block.scalar
                def _(act):
                    c = chain(act, "act")
                    act.wait_ge(dl_in, 64 * (l + 1))
                    c.link(nc.scalar.activation(prm[:, 0, :], prm[:, 0, :], ACT.Exp))
                    act.wait_ge(sm_dve, 2 * l + 1)
                    c.link(nc.scalar.activation(sp_[:, 1, :, :], sp_[:, 1, :, :], ACT.Exp))
                    c.link(nc.scalar.activation(sp_[:, 1, :, :], sp_[:, 1, :, :], ACT.Ln, bias=1.0))
                    nc.scalar.activation(sp_[:, 2, :, :], wsm[:, :, 12:16], ACT.Exp, scale=-1.0).then_inc(sm_act, 1)
                    gates_out(act, l, GATES_ATT, GATES_FIRST)
                    act.wait_ge(sm_dve, 2 * l + 2)
                    c.link(nc.scalar.activation(nrm16[:, :, 0:8], nrm16[:, :, 0:8], ACT.Ln))
                    c.link(nc.scalar.activation(nrm16[:, :, 0:8], nrm16[:, :, 0:8], ACT.Exp, scale=-0.5))
                    c.link(nc.scalar.activation(nrm16[:, :, 12:16], nrm16[:, :, 12:16], ACT.Exp))
                    c.link(nc.scalar.activation(sp_[:, 0, :, :], nrm16[:, :, 8:12], ACT.Exp))
                    act.wait_ge(egl_done, l + 1)
                    nc.scalar.activation(eg.rearrange("p a h -> p (a h)"), ps[7][:, 0:20], ACT.Exp).then_inc(sm_act, 1)

                    def copies(r, dst, scale=1.0):
                        for i, (t0, n) in enumerate(TILES):
                            act.wait_ge(prep_done, at_round(r, i))
                            dd = tl[i][dst]
                            rows_ = BD if r in ("qT", "kT", "qdT", "wT") else n
                            w = BD if r == "u" else n
                            nc.scalar.activation(dd[0:rows_], v4(bank(r, i), rows_, w), ACT.Copy, scale=scale
                                                 ).then_inc(prep_act, 1)
                    out = GATES_FIRST
                    for r in AC:
                        gates_out(act, l, out, gates_by(RN[r] - 2) // KD)
                        out = gates_by(RN[r] - 2) // KD
                        if r == "kT":
                            for i, (t0, n) in enumerate(TILES):
                                act.wait_ge(prep_dve, evac_of("grow", i)[1])
                                for h in range(H4):
                                    nc.scalar.activation(tl[i]["E"][0:n, h, :], tl[i]["E"][0:n, h, :], ACT.Exp,
                                                         bias=nrm16[0:n, i, 8 + h:9 + h])
                                    ins = nc.scalar.activation(tl[i]["ET"][0:n, h, :], tl[i]["ET"][0:n, h, :], ACT.Exp,
                                                               bias=nG[0:n, i, h:h + 1])
                                ins.then_inc(dec_ready, 1)
                        copies(r, {"P2": "P", "P2T": "PT", "X3T": "XT"}.get(r, r), -1.0 if r == "wT" else 1.0)
                    gates_out(act, l, out, GATES_REC)
                    for q, (i, r0, s, ch) in enumerate(SEQS):
                        n = min(CHUNK, TILES[i][1])
                        g = len(SEQS) * l + q
                        act.wait_ge(o_done, g + 1)
                        nc.scalar.activation(tl[i]["o"][r0:r0 + n], v4(ps[7][r0:r0 + n], n, BD), ACT.Copy).then_inc(o_ready, 1)
                        gates_out(act, l, GATES_REC + q, GATES_REC + q + 1)
                    act.wait_ge(ssq_ready, l + 1)
                    c.link(nc.scalar.activation(rr, rr, ACT.Ln))
                    nc.scalar.activation(rr, rr, ACT.Exp, scale=-0.5).then_inc(rn_ready, 1)
                    keep(c, "act")

                @block.vector
                def _(dve):
                    c = chain(dve, "dve")
                    V = nc.vector
                    c(V.memset(rr, 1.0))
                    c(V.memset(nrm16, 1.0))
                    dve.wait_ge(dl_in, 64 * (l + 1))
                    for i in range(NT):
                        ins = V.tensor_tensor(sp_[:, 0, i, :], wsm[:, i, 8:12], prm[:, 1, :], ALU.add)
                    c.link(ins)
                    c.link(V.scalar_tensor_tensor(out=sp_[:, 1, :, :], in0=sp_[:, 0, :, :], scalar=-1.0, in1=sp_[:, 0, :, :],
                                                  op0=ALU.mult, op1=ALU.min))
                    V.tensor_scalar(sp_[:, 0, :, :], sp_[:, 0, :, :], 0.0, None, ALU.max).then_inc(sm_dve, 1)
                    dve.wait_ge(sm_act, 2 * l + 1)
                    c.link(V.tensor_tensor(sp_[:, 0, :, :], sp_[:, 0, :, :], sp_[:, 1, :, :], ALU.add))
                    for i in range(NT):
                        ins = V.scalar_tensor_tensor(out=gv[:, i, :], in0=sp_[:, 0, i, :], scalar=-1.0, in1=prm[:, 0, :],
                                                     op0=ALU.mult, op1=ALU.mult)
                    ins.then_inc(g_ready, 1)
                    c.link(V.tensor_scalar(sp_[:, 2, :, :], sp_[:, 2, :, :], 1.0, None, ALU.add))
                    c.link(V.reciprocal(sp_[:, 2, :, :], sp_[:, 2, :, :]))
                    c.link(V.tensor_scalar(nbeta, sp_[:, 2, :, :], -1.0, None, ALU.mult))
                    for i, (t0, n) in enumerate(TILES):
                        dve.wait_ge(prep_done, at_round("norm", i))
                        c.link(V.tensor_copy(nrm16[0:n, i, :], ps[6][0:n, 16 * i:16 * i + 16]))
                        V.tensor_scalar(nG[0:n, i, :], nrm16[0:n, i, 8:12], -1.0, None, ALU.mult).then_inc(prep_dve, 1)
                    dve.wait_ge(prep_dve, evac_of("norm", NT - 1)[1])
                    c.link(V.tensor_tensor(nrm16[:, :, 12:16], nrm16[:, :, 12:16], nrm16[:, :, 8:12], ALU.subtract))
                    V.tensor_scalar(nrm16[:, :, 0:8], nrm16[:, :, 0:8], RMS_EPS, None, ALU.add).then_inc(sm_dve, 1)
                    dve.wait_ge(sm_act, 2 * l + 2)
                    rq, rk, eT, eG, beta = (nrm16[:, :, 0:4], nrm16[:, :, 4:8], nrm16[:, :, 12:16], sp_[:, 0, :, :],
                                            sp_[:, 2, :, :])
                    c.link(V.tensor_scalar(sc[:, :, SC_Q, :], rq, BD ** -0.5, None, ALU.mult))
                    c.link(V.tensor_tensor(sc[:, :, SC_QD, :], sc[:, :, SC_Q, :], eG, ALU.mult))
                    c.link(V.tensor_copy(sc[:, :, SC_K, :], rk))
                    c.link(V.tensor_tensor(sc[:, :, SC_KT, :], rk, eT, ALU.mult))
                    c.link(V.tensor_copy(sc[:, :, SC_VB, :], beta))
                    c.link(V.tensor_tensor(sc[:, :, SC_KBG, :], rk, eG, ALU.mult))
                    c.link(V.tensor_tensor(sc[:, :, SC_KBG, :], sc[:, :, SC_KBG, :], beta, ALU.mult))
                    dve.wait_ge(sm_act, 2 * l + 2)
                    V.memset(state[:, 0, :, :], 0.0).then_inc(egl_ready, 1)

                    def scaled(dst, src, i, n, which):
                        f = sc[0:n, i, which, :].unsqueeze(2).to_broadcast([n, H4, BD])
                        return V.tensor_tensor(dst[0:n], v4(src, n, BD), f, ALU.mult)
                    for i, (t0, n) in enumerate(TILES):
                        d = tl[i]
                        dve.wait_ge(prep_done, at_round("qk", i))
                        c(scaled(d["q"], ps[2 * i], i, n, SC_Q))
                        c(scaled(d["qd"], ps[2 * i], i, n, SC_QD))
                        c(scaled(d["k"], ps[2 * i + 1], i, n, SC_K))
                        c(scaled(d["kbG"], ps[2 * i + 1], i, n, SC_KBG))
                        for h in range(H4):
                            ins = V.tensor_scalar(d["gtri"][0:n, h, :], cumU[0:n, 0:n], gv[0:n, i, h:h + 1], None, ALU.mult)
                        ins.then_inc(dec_in, 1)
                        scaled(d["kt"], ps[2 * i + 1], i, n, SC_KT).then_inc(prep_dve, 1)
                    for i, (t0, n) in enumerate(TILES):
                        dve.wait_ge(prep_done, at_round("v", i))
                        scaled(tl[i]["vb"], bank("v", i), i, n, SC_VB).then_inc(prep_dve, 1)

                    def allh(m, n):
                        return m[0:n, 0:n].unsqueeze(1).to_broadcast([n, H4, n])
                    for i, (t0, n) in enumerate(TILES):
                        d = tl[i]
                        dve.wait_ge(prep_done, at_round("grow", i))
                        gr = v4(bank("grow", i), n, n)
                        for h in range(H4):
                            V.scalar_tensor_tensor(out=d["E"][0:n, h, :], in0=gr[:, h, :], scalar=-1.0, in1=negL[0:n, 0:n],
                                                   op0=ALU.mult, op1=ALU.add)
                        V.tensor_tensor(d["ET"][0:n], gr, allh(negU, n), ALU.add).then_inc(prep_dve, 1)
                    for i, (t0, n) in enumerate(TILES):
                        d = tl[i]
                        dve.wait_ge(prep_done, at_round("KK", i))
                        dve.wait_ge(dec_ready, sb_ + i + 1)
                        dve.wait_ge(prep_act, evac_of("qdT", i)[1])
                        kk = v4(bank("KK", i), n, n)
                        for h in range(H4):
                            ins = V.scalar_tensor_tensor(out=d["E"][0:n, h, :], in0=kk[:, h, :], scalar=nbeta[0:n, i, h:h + 1],
                                                         in1=d["E"][0:n, h, :], op0=ALU.mult, op1=ALU.mult)
                        c.link(ins)
                        V.tensor_tensor(d["Mo"][0:n], d["E"][0:n], allh(off16, n), ALU.mult)
                        V.tensor_tensor(d["Md"][0:n], d["E"][0:n], allh(d16, n), ALU.mult).then_inc(prep_dve, 1)
                    for i, (t0, n) in enumerate(TILES):
                        d = tl[i]
                        dve.wait_ge(prep_done, at_round("QKT", i))
                        V.tensor_tensor(d["QKT"][0:n], v4(bank("QKT", i), n, n), d["ET"][0:n], ALU.mult).then_inc(prep_dve, 1)
                    for i, (t0, n) in enumerate(TILES):
                        d = tl[i]
                        dve.wait_ge(prep_act, evac_of("MoT", i)[1])
                        V.tensor_tensor(d["X"][0:n], d["MdT"][0:n], allh(ident, n), ALU.add).then_inc(x_ready, 1)
                    for r in ("X1", "X2", "X3", "Y1", "TT"):
                        for i, (t0, n) in enumerate(TILES):
                            d = tl[i]
                            dve.wait_ge(prep_done, at_round(r, i))
                            if r == "X1":
                                dve.wait_ge(x_ready, sb_ + i + 1)
                            else:
                                prev = {"X2": "X1", "X3": "X2", "Y1": "X3", "TT": "Y1"}[r]
                                dve.wait_ge(prep_dve, evac_of(prev, i)[1])
                            V.tensor_tensor(d["X"][0:n], d["X"][0:n], v4(bank(r, i), n, n), ALU.add).then_inc(prep_dve, 1)

                    for q, (i, r0, s, ch) in enumerate(SEQS):
                        n = min(CHUNK, TILES[i][1])
                        R = slice(r0, r0 + n)
                        d = tl[i]
                        g = len(SEQS) * l + q
                        dve.wait_ge(ws_done, g + 1)
                        dve.wait_ge(prep_act, evac_of("u", i)[1])
                        V.tensor_tensor(d["vnew"][R], v4(ps[6][R], n, BD), d["u"][R], ALU.add).then_inc(vnew_ready, 1)
                        dve.wait_ge(ds_done, g + 1)
                        dve.wait_ge(o_done, g + 1)
                        for h in range(H4):
                            ins = V.scalar_tensor_tensor(out=state[:, s, h, :], in0=state[:, s, h, :], scalar=eg[:, ch, h:h + 1],
                                                         in1=ps[0][:, BD * h:BD * h + BD], op0=ALU.mult, op1=ALU.add)
                        ins.then_inc(s_ready, 1)
                    dve.wait_ge(o_ready, len(SEQS) * (l + 1))
                    for i, (t0, n) in enumerate(TILES):
                        c.link(V.tensor_tensor(osq[0:n], tl[i]["o"][0:n], tl[i]["o"][0:n], ALU.mult))
                        c.link(V.tensor_reduce(rr[0:n, i, :], osq[0:n], AX.X, ALU.add))
                    V.tensor_scalar(rr, rr, 1.0 / BD, RMS_EPS, ALU.mult, ALU.add).then_inc(ssq_ready, 1)
                    dve.wait_ge(rn_ready, l + 1)
                    for i, (t0, n) in enumerate(TILES):
                        f = rr[0:n, i, :].unsqueeze(2).to_broadcast([n, H4, BD])
                        V.tensor_tensor(tl[i]["on"][0:n], tl[i]["o"][0:n], f, ALU.mult).then_inc(on_ready, 1)
                    for i, (t0, n) in enumerate(TILES):
                        dve.wait_ge(ot_done, sb_ + i + 1)
                        V.scalar_tensor_tensor(out=obT[:, :, t0:t0 + n], in0=v4(ps[1 + i], BD, n), scalar=gn[:, 0:1],
                                               in1=zT[:, :, t0:t0 + n], op0=ALU.mult, op1=ALU.mult).then_inc(ob_ready, 1)
                    keep(c, "dve")

        m_full, m_hi = sem("m_full"), sem("m_hi")
        mg_done, mg_read, m_ready, mo_done, mo_added = (sem("mg_done"), sem("mg_read"),
                                                                 sem("m_ready"), sem("mo_done"), sem("mo_added"))
        def merge(l):
            u0 = first["merge", l]
            inputs = [(oaT[:], oabh[:, 0:4, :], oabl[:, 0:4, :]), (obT[:], oabh[:, 4:8, :], oabl[:, 4:8, :])]
            at = (0, 2 + 2)[l]
            with nc.Block() as block:
                @block.sync
                def _(sp):
                    load_units(sp, u0 + N_MERGE)

                @block.tensor
                def _(pe):
                    for j in range(KD // 2):
                        n = u0 + j
                        w = halves(n, (8, 256))
                        have_split(pe, n)
                        if j >= 2:
                            pe.wait_ge(mg_read, KD * l + 2 * (j - 1))
                        for g in range(2):
                            if j == 0:
                                pe.wait_ge(x_low, at + g + 1)
                            for c in range(2):
                                product(ps[4 * (j % 2) + 2 * g + c][:, 0:T],
                                        [([v[:, 4 * g + k, P * c:P * c + P] for v in w], [v[:, 4 * g + k, :] for v in (oabh, oabl)])
                                         for k in range(4)]).then_inc(mg_done, 1)
                        rel.due = split_free
                    pe.wait_ge(mg_read, KD * (l + 1))
                    for j in range(4):
                        n = u0 + 4 + j
                        w = halves(n, (8, 256))
                        have_split(pe, n)
                        if j == 0:
                            pe.wait_ge(m_ready, KD * (l + 1))
                        for i, (t0, m) in enumerate(TILES):
                            g = NT * j + i
                            if g >= 8:
                                pe.wait_ge(mo_added, 4 * NT * l + g - 7)
                            product(ps[g % 8][0:m, 0:256], [([v[:, k, t0:t0 + m] for v in (mTh, mTl)], [v[:, k, :] for v in w])
                                                            for k in range(KD)]).then_inc(mo_done, 1)
                        rel.due = split_free

                @block.scalar
                def _(act):
                    inputs_high(act, at, inputs[0:1])
                    split_high(act, u0)
                    inputs_high(act, at + 1, inputs[1:])
                    split_high(act, u0 + 1)
                    for j in range(N_MERGE - AHEAD):
                        split_high(act, u0 + j + AHEAD)
                        for c in range(2 if j < KD // 2 else 0):
                            act.wait_ge(m_full, KD * l + 2 * j + c + 1)
                            nc.scalar.activation(mTh[:, 2 * j + c, :], mo_[:, c, 0:T], ACT.Copy).then_inc(m_hi, 1)

                @block.vector
                def _(dve):
                    inputs_low(dve, at, inputs[0:1])
                    split_low(dve, u0)
                    inputs_low(dve, at + 1, inputs[1:])
                    split_low(dve, u0 + 1)
                    for j in range(KD // 2):
                        split_low(dve, u0 + j + AHEAD)
                        for c in range(2):
                            if j:
                                dve.wait_ge(m_ready, KD * l + 2 * j + c - 1)
                            for g in range(2):
                                dve.wait_ge(mg_done, 4 * (4 * l + j) + 2 * g + c + 1)
                                ins = nc.vector.scalar_tensor_tensor(out=mo_[:, c, T * g:T * g + T], in0=tanhs[:, (4 * j + 2 * g + c + KD) % (2 * KD), :],
                                                                     scalar=1.0, in1=ps[4 * (j % 2) + 2 * g + c][:, 0:T],
                                                                     op0=ALU.add, op1=ALU.mult)
                            ins.then_inc(mg_read, 1)
                            dve.wait_ge(mg_read, KD * l + 2 * j + c + 1)
                            nc.vector.tensor_tensor(mo_[:, c, 0:T], mo_[:, c, 0:T], mo_[:, c, T:2 * T], ALU.add
                                                    ).then_inc(m_full, 1)
                        for c in range(2):
                            m = 2 * j + c
                            dve.wait_ge(m_hi, KD * l + m + 1)
                            nc.vector.tensor_tensor(mTl[:, m, :], mo_[:, c, 0:T], mTh[:, m, :].bitcast(F32), ALU.subtract
                                                    ).then_inc(m_ready, 1)
                    for j in range(4):
                        if 4 + AHEAD + j < N_MERGE:
                            split_low(dve, u0 + 4 + AHEAD + j)
                        for i, (t0, n) in enumerate(TILES):
                            g = NT * j + i
                            dve.wait_ge(mo_done, 4 * NT * l + g + 1)
                            r = resid[0:n, i, 256 * j:256 * j + 256]
                            nc.vector.scalar_tensor_tensor(out=r, in0=ps[g % 8][0:n, 0:256], scalar=0.5, in1=r,
                                                           op0=ALU.mult, op1=ALU.add).then_inc(mo_added, 1)

        up_done, silu_done, g_full, g_high, gT_ready = (sem("up_done"), sem("silu_done"), sem("g_full"), sem("g_high"),
                                                       sem("gT_ready"))
        w2_done, y_even, y_odd, y_turned, y_added = (sem("w2_done"), sem("y_even"), sem("y_odd"), sem("y_turned"),
                                                     sem("y_added"))
        FCH, ECH = D_FF // P, D_FFE // P
        EPAIR = ECH // 2

        def dense_mlp():
            n0 = first["mlp", 0]
            inputs = [(hT[:, 0:4, :], hTh[:, 0:4, :], hTl[:, 0:4, :]), (hT[:, 4:8, :], hTh[:, 4:8, :], hTl[:, 4:8, :])]
            at = 2
            with nc.Block() as block:
                @block.sync
                def _(sp):
                    load_units(sp, n0 + N_FFN)

                @block.gpsimd
                def _(pool):
                    finish_stream(pool, 1)

                @block.tensor
                def _(pe):
                    pe.wait_ge(x_low, at + 2)
                    for u in range(FCH):
                        p, g = u // 2, u % 2
                        w = halves(n0 + u, (8, 256))
                        have_split(pe, n0 + u)
                        if p >= 2:
                            pe.wait_ge(g_full, 2 * (p - 1))
                        for c in range(2):
                            product(ps[4 * (p % 2) + 2 * g + c][:, 0:T],
                                    [([v[:, k, P * c:P * c + P] for v in w], (hTh[:, k, :], hTl[:, k, :])) for k in range(KD)]
                                    ).then_inc(up_done, 1)
                        rel.due = split_free
                    pe.wait_ge(g_full, FCH)
                    for j in range(FCH // 2):
                        n = n0 + FCH + j
                        w = halves(n, (2, D))
                        have_split(pe, n)
                        for q in range(2):
                            f = 2 * j + q
                            pe.wait_ge(gT_ready, f + 1)
                            for m in range(KD):
                                a, b = [v[:, q, P * m:P * m + P] for v in w]
                                for x, y, at_end in ((a, gTh, 0), (a, gTl, 0), (b, gTh, 1)):
                                    ins = rel.mm(ps[m][:, 0:T], x, y[:, f, :], start=(f == 0 and x is a and y is gTh),
                                                 stop=(f == FCH - 1 and at_end == 1))
                                if f == FCH - 1:
                                    ins.then_inc(w2_done, 1)
                        rel.due = split_free
                    pe.wait_ge(y_even, KD // 2)
                    pe.wait_ge(y_odd, KD // 2)
                    for i, (t0, n) in enumerate(TILES):
                        for c in range(2):
                            for m in range(4):
                                ins = rel.mm(ps[2 * i + c][0:n, P * m:P * m + P], yT[:, 4 * c + m, t0:t0 + n], ident[:],
                                             is_transpose=True, start=True, stop=True)
                            ins.then_inc(y_turned, 1)

                @block.scalar
                def _(act):
                    inputs_high(act, at, inputs)
                    for u in range(N_FFN):
                        p = u // 2
                        if u + AHEAD < N_FFN:
                            split_high(act, n0 + u + AHEAD)
                        if u >= FCH:
                            continue
                        for c in range(2):
                            m = 2 * p + c
                            if u % 2 == 0:
                                act.wait_ge(up_done, 4 * p + c + 1)
                                if p:
                                    act.wait_ge(g_full, m - 1)
                                nc.scalar.activation(slT[:, c, :], ps[4 * (p % 2) + c][:, 0:T], ACT.Silu).then_inc(silu_done, 1)
                            else:
                                act.wait_ge(g_full, m + 1)
                                nc.scalar.activation(gTh[:, m, :], gfull[:, c, :], ACT.Copy).then_inc(g_high, 1)
                    for m in range(0, KD, 2):
                        act.wait_ge(w2_done, m + 1)
                        nc.scalar.activation(yT[:, m, :], ps[m][:, 0:T], ACT.Copy).then_inc(y_even, 1)

                @block.vector
                def _(dve):
                    inputs_low(dve, at, inputs)
                    for u in range(N_FFN):
                        p = u // 2
                        if u + AHEAD < N_FFN:
                            split_low(dve, n0 + u + AHEAD)
                        if u >= FCH or u % 2 == 0:
                            continue
                        for c in range(2):
                            m = 2 * p + c
                            dve.wait_ge(up_done, 4 * p + c + 3)
                            dve.wait_ge(silu_done, m + 1)
                            if p:
                                dve.wait_ge(gT_ready, m - 1)
                            nc.vector.tensor_tensor(gfull[:, c, :], slT[:, c, :], ps[4 * (p % 2) + 2 + c][:, 0:T], ALU.mult
                                                    ).then_inc(g_full, 1)
                        for c in range(2):
                            m = 2 * p + c
                            dve.wait_ge(g_high, m + 1)
                            if m == 8:
                                dve.wait_ge(stream_done, 2)
                            nc.vector.tensor_tensor(gTl[:, m, :], gfull[:, c, :], gTh[:, m, :].bitcast(F32), ALU.subtract
                                                    ).then_inc(gT_ready, 1)
                    for m in range(1, KD, 2):
                        dve.wait_ge(w2_done, m + 1)
                        nc.vector.tensor_copy(yT[:, m, :], ps[m][:, 0:T]).then_inc(y_odd, 1)
                    for i, (t0, n) in enumerate(TILES):
                        for c in range(2):
                            dve.wait_ge(y_turned, 2 * i + c + 1)
                            r = resid[0:n, i, 512 * c:512 * c + 512]
                            nc.vector.tensor_tensor(r, r, ps[2 * i + c][0:n, :], ALU.add).then_inc(y_added, 1)

        lgt_in, rt_done, sel_ready, pos_done, flag_ready, pos_ready = (sem("lgt_in"), sem("rt_done"), sem("sel_ready"),
                                                                       sem("pos_done"), sem("flag_ready"), sem("pos_ready"))
        rt_exp, rt_top = sem("rt_exp"), sem("rt_top")
        oh_ready, ga_done, xg_ready, ohg_ready, ohT_done, ohT_ready = (sem("oh_ready"), sem("ga_done"), sem("xg_ready"),
                                                                       sem("ohg_ready"), sem("ohT_done"), sem("ohT_ready"))
        y_ready, sc_done, sc_added = sem("y_ready"), sem("sc_done"), sem("sc_added")
        gs_ready, yh_ready, tok_ready = sem("gs_ready"), sem("yh_ready"), sem("tok_ready")
        e_up, e_silu, e_gated, e_turned, e_high, e_ready, xg_high = [sem(x) for x in (
            "e_up", "e_silu", "e_gated", "e_turned", "e_high", "e_ready", "xg_high")]
        ea = Area(experts)
        router = ea(KD, NE)
        gt = ea(2, 256)
        slE = ea(2, 256)
        gslot = ea(1)
        ohg = ea(NT, CAP)
        rlog = ea(NT, NE)
        rtop = ea(NT, 8)
        rsel = ea(NT, 2 * NE)
        selm = ea(NT, NE)
        gate = ea(NT, NE)
        gate2 = ea(NT, NE)
        ridx = ea(NT, 8)
        rw = ea(NT, 4)
        posr = ea(NT, ROUNDS * NE + 1)
        cnt = ea(NE)
        cmx = ea(2)

        def moe():
            iu = itmp
            with nc.Block() as block:
                def up_unit(pe, i, u):
                    p, g = u // 2, u % 2
                    if u == 0:
                        pe.wait_ge(xg_ready, 2 * i + 2)
                    w = halves(moe0 + u, (8, 256))
                    have_split(pe, moe0 + u, i)
                    if p >= 2:
                        pe.wait_ge(e_gated, EPAIR * i + p - 1)
                    product(ps[2 * g + p % 2][0:CAP, 0:256],
                            [((xgh[:, k, :], xgl[:, k, :]), [v[:, k, :] for v in w]) for k in range(KD)]).then_inc(e_up, 1)
                    rel.due = split_free
                    if g and p:
                        turn_hidden(pe, i, p - 1)

                def expert_tensor(pe, r, e, early, on):
                    i = r * NE + e
                    for u in range(1 if early else 0, ECH):
                        up_unit(pe, i, u)
                    for j in range(EPAIR):
                        n = moe0 + ECH + j
                        w = halves(n, (2, D))
                        have_split(pe, n, i)
                        pe.wait_ge(e_ready, EPAIR * i + j + 1)
                        for q in range(2):
                            f = 2 * j + q
                            for a, b, last in ((gEh, w[0], False), (gEh, w[1], False), (gEl, w[0], True)):
                                for c in range(2):
                                    ins = rel.mm(ps[4 + c][0:CAP, :], a[:, f, :], b[:, q, 512 * c:512 * c + 512],
                                                 start=(f == 0 and a is gEh and b is w[0]), stop=(f == ECH - 1 and last))
                        if j == EPAIR - 1:
                            ins.then_inc(split_free, 1)
                        else:
                            rel.due = split_free
                        if j == 0:
                            turn_hidden(pe, i, EPAIR - 1)
                        if j == 1:
                            gather(pe, i + 1)
                            pe.wait_ge(ohg_ready, i + 1)
                            for t in range(NT):
                                m = TILES[t][1]
                                ins = rel.mm(ps[2][0:CAP, P * t:P * t + m], ohg[0:m, t, :], ident[0:m, 0:m],
                                             is_transpose=True, start=True, stop=True)
                            for t in range(NT):
                                m = TILES[t][1]
                                ins = rel.mm(ps[3][0:CAP, 0:1], ohg[0:m, t, :], ones[0:m, 0:1], start=(t == 0), stop=(t == NT - 1))
                            ins.then_inc(ohT_done, 1)
                    if on:
                        up_unit(pe, i + 1, 0)
                    pe.wait_ge(ohT_ready, i + 1)
                    pe.wait_ge(y_ready, i + 1)
                    for t in range(NT):
                        m = TILES[t][1]
                        if t == 2:
                            pe.wait_ge(sc_added, 3 * i + 2)
                        for c in range(2):
                            b = ps[(6, 4, 6)[t] + c][0:m, :]
                            for y in (yh, yl):
                                ins = rel.mm(b, ohT[0:CAP, t, 0:m], y[0:CAP, 512 * c:512 * c + 512], start=(y is yh), stop=(y is yl))
                        ins.then_inc(sc_done, 1)

                def turn_hidden(pe, i, p):
                    pe.wait_ge(e_gated, EPAIR * i + p + 1)
                    if p >= 2:
                        pe.wait_ge(e_ready, EPAIR * i + p - 1)
                    for c in range(2):
                        ins = rel.mm(ps[6 + p % 2][:, CAP * c:CAP * c + CAP], gt[0:CAP, p % 2, P * c:P * c + P],
                                     ident[0:CAP, 0:CAP], is_transpose=True, start=True, stop=True)
                    ins.then_inc(e_turned, 1)

                def first_unit(pe):
                    up_unit(pe, 0, 0)
                    rel.mm(ps[5][0:1, 0:1], ones[0:1, 0:1], ones[0:1, 0:1], start=True, stop=True)

                def gather(pe, i):
                    pe.wait_ge(oh_ready, i + 1)
                    for k in range(KD):
                        for t in range(NT):
                            n = TILES[t][1]
                            for h in (htokh, htokl):
                                ins = rel.mm(ps[k // 4][:, CAP * (k % 4):CAP * (k % 4) + CAP], h[0:n, t, P * k:P * k + P],
                                             oh[0:n, t, :], start=(t == 0 and h is htokh), stop=(t == NT - 1 and h is htokl))
                        if k % 4 == 3:
                            ins.then_inc(ga_done, 1)

                def expert_scalar(act, r, e, early, on):
                    i = r * NE + e
                    for u in range(0 if early else AHEAD):
                        split_high(act, moe0 + u, i)
                    for u in range(N_EXP):
                        p = u // 2
                        if u + AHEAD < N_EXP:
                            split_high(act, moe0 + u + AHEAD, i)
                        elif on:
                            split_high(act, moe0 + u + AHEAD - N_EXP, i + 1)
                        if u % 2 == 0 and 2 <= p <= EPAIR:
                            hidden_high(act, i, p - 2)
                        if u == ECH + 1:
                            hidden_high(act, i, EPAIR - 1)
                        if u % 2 == 0 and p < EPAIR:
                            act.wait_ge(e_up, ECH * i + u + 1)
                            if p >= 2:
                                act.wait_ge(e_gated, EPAIR * i + p - 1)
                            nc.scalar.activation(slE[0:CAP, p % 2, :], ps[p % 2][0:CAP, 0:256], ACT.Silu).then_inc(e_silu, 1)
                        if u == ECH + 2:
                            gathered_high(act, i + 1)
                            act.wait_ge(ohT_done, i + 1)
                            nc.scalar.activation(gslot[0:CAP], ps[3][0:CAP, 0:1], ACT.Copy).then_inc(gs_ready, 1)
                    act.wait_ge(split_free, split_index(moe0) + N_EXP * (i + 1))
                    act.wait_ge(gs_ready, i + 1)
                    for c in range(2):
                        nc.scalar.activation(yh[0:CAP, 512 * c:512 * c + 512], ps[4 + c][0:CAP, :], ACT.Copy,
                                             scale=gslot[0:CAP]).then_inc(yh_ready, 1)

                def turned_view(p):
                    return ps[6 + p % 2][:, 0:2 * CAP].rearrange("p (c t) -> p c t", c=2)

                def hidden_high(act, i, p):
                    act.wait_ge(e_turned, EPAIR * i + p + 1)
                    nc.scalar.activation(gEh[:, 2 * p:2 * p + 2, :], turned_view(p), ACT.Copy).then_inc(e_high, 1)

                def hidden_low(dve, i, p):
                    dve.wait_ge(e_high, EPAIR * i + p + 1)
                    nc.vector.tensor_tensor(gEl[:, 2 * p:2 * p + 2, :], turned_view(p), gEh[:, 2 * p:2 * p + 2, :].bitcast(F32),
                                            ALU.subtract).then_inc(e_ready, 1)

                def gathered_view(h):
                    return ps[h][:, 0:4 * CAP].rearrange("p (k t) -> p k t", k=4)

                def gathered_high(act, i):
                    for h in range(2):
                        act.wait_ge(ga_done, 2 * i + h + 1)
                        nc.scalar.activation(xgh[:, 4 * h:4 * h + 4, :], gathered_view(h), ACT.Copy).then_inc(xg_high, 1)

                def gathered_low(dve, i):
                    for h in range(2):
                        dve.wait_ge(xg_high, 2 * i + h + 1)
                        nc.vector.tensor_tensor(xgl[:, 4 * h:4 * h + 4, :], gathered_view(h),
                                                xgh[:, 4 * h:4 * h + 4, :].bitcast(F32), ALU.subtract).then_inc(xg_ready, 1)

                def onehot(i):
                    for t in range(NT):
                        n = TILES[t][1]
                        ins = nc.vector.tensor_scalar(oh[0:n, t, :], iota[0:n, :], posr[0:n, t, bass.ds(i, 1)], None, ALU.is_equal)
                    ins.then_inc(oh_ready, 1)

                def expert_vector(dve, r, e, early, on):
                    i = r * NE + e
                    for u in range(0 if early else AHEAD):
                        split_low(dve, moe0 + u, i)
                    onehot(i + 1)
                    for t in range(NT):
                        n = TILES[t][1]
                        ins = nc.vector.tensor_scalar(ohg[0:n, t, :], iota[0:n, :], posr[0:n, t, bass.ds(i, 1)],
                                                      gate[0:n, t, bass.ds(e, 1)], ALU.is_equal, ALU.mult)
                    ins.then_inc(ohg_ready, 1)
                    for u in range(N_EXP):
                        p = u // 2
                        if u + AHEAD < N_EXP:
                            split_low(dve, moe0 + u + AHEAD, i)
                        elif on:
                            split_low(dve, moe0 + u + AHEAD - N_EXP, i + 1)
                        if u % 2 == 0 and 2 <= p <= EPAIR:
                            hidden_low(dve, i, p - 2)
                        if u == ECH + 1:
                            hidden_low(dve, i, EPAIR - 1)
                        if u % 2 and p < EPAIR:
                            dve.wait_ge(e_up, ECH * i + u + 1)
                            dve.wait_ge(e_silu, EPAIR * i + p + 1)
                            if p >= 2:
                                dve.wait_ge(e_turned, EPAIR * i + p - 1)
                            nc.vector.tensor_tensor(gt[0:CAP, p % 2, :], slE[0:CAP, p % 2, :], ps[2 + p % 2][0:CAP, 0:256],
                                                    ALU.mult).then_inc(e_gated, 1)
                        if u == ECH + 2:
                            gathered_low(dve, i + 1)
                            dve.wait_ge(ohT_done, i + 1)
                            nc.vector.tensor_scalar(ohT[0:CAP, 0:2, :], ps[2][0:CAP, 0:256].rearrange("p (t c) -> p t c", t=2),
                                                    0.0, None, ALU.not_equal)
                            nc.vector.tensor_scalar(ohT[0:CAP, 2, 0:DEC], ps[2][0:CAP, 256:256 + DEC], 0.0, None, ALU.not_equal
                                                    ).then_inc(ohT_ready, 1)
                    for c in range(2):
                        dve.wait_ge(yh_ready, 2 * i + c + 1)
                        s_ = slice(512 * c, 512 * c + 512)
                        ins = nc.vector.scalar_tensor_tensor(out=yl[0:CAP, s_], in0=ps[4 + c][0:CAP, :], scalar=gslot[0:CAP],
                                                             in1=yh[0:CAP, s_].bitcast(F32), op0=ALU.mult, op1=ALU.subtract)
                    ins.then_inc(y_ready, 1)
                    for t in range(NT):
                        n = TILES[t][1]
                        dve.wait_ge(sc_done, 3 * i + t + 1)
                        for c in range(2):
                            q = resid[0:n, t, 512 * c:512 * c + 512]
                            ins = nc.vector.tensor_tensor(q, q, ps[(6, 4, 6)[t] + c][0:n, :], ALU.add)
                        ins.then_inc(sc_added, 1)

                def expert_loads(sp, r, e, lo):
                    i = r * NE + e
                    for j in range(lo, N_EXP):
                        sp.wait_ge(unit_used, moe0 + N_EXP * i + j - RING + 1)
                        w = [A[x][0, bass.ds(e, 1)].squeeze(0) if not isinstance(e, int) else A[x][0, e]
                             for x in ("moe_w1", "moe_w3", "moe_w2")]
                        dst, src = mlp_loads(moe0, j, *w, D_FFE)
                        sp.dma_start(dst, src).then_inc(slot_full[(moe0 + j) % RING], 16)

                def more_rounds(eng, body):
                    eng.wait_ge(flag_ready, 1)
                    more = eng.value_load(iu[0:1, 0:1], min_val=0, max_val=1)
                    with eng.If(more > 0):
                        with eng.Fori(1, ROUNDS) as r:
                            with eng.Fori(0, NE) as e:
                                body(r, e)

                def rounds(eng, body, prologue):
                    prologue()
                    with eng.Fori(0, NE - 1) as e:
                        body(eng, 0, e, True, True)
                    body(eng, 0, NE - 1, True, False)
                    more_rounds(eng, lambda r, e: body(eng, r, e, False, False))

                @block.sync
                def _(sp):
                    sp.dma_start(router, A["moe_router"][0].rearrange("(k p) e -> p k e", p=P)).then_inc(lgt_in, 16)
                    expert_loads(sp, 0, 0, RING)
                    with sp.Fori(1, NE) as e:
                        expert_loads(sp, 0, e, 0)
                    more_rounds(sp, lambda r, e: expert_loads(sp, r, e, 0))

                @block.tensor
                def _(pe):
                    pe.wait_ge(lgt_in, 16)
                    for i, (t0, n) in enumerate(TILES):
                        for k in range(KD):
                            ins = rel.mm(ps[0][0:n, NE * i:NE * i + NE], hT[:, k, t0:t0 + n], router[:, k, :],
                                         start=(k == 0), stop=(k == KD - 1))
                    ins.then_inc(rt_done, 1)
                    pe.wait_ge(sel_ready, 1)
                    for i, (t0, n) in enumerate(TILES):
                        for j in range(i):
                            nc.tensor.matmul(ps[1][0:n, NE * i:NE * i + NE], ones[:, 0:n], selm[:, j, :], start=(j == 0), stop=False)
                        ins = nc.tensor.matmul(ps[1][0:n, NE * i:NE * i + NE], before[0:n, 0:n], selm[0:n, i, :],
                                               start=(i == 0), stop=True)
                    for i, (t0, n) in enumerate(TILES):
                        ins = nc.tensor.matmul(ps[1][:, 32:32 + NE], ones[0:n, :], selm[0:n, i, :], start=(i == 0), stop=(i == NT - 1))
                    ins.then_inc(pos_done, 1)
                    pe.wait_ge(pos_ready, 1)
                    pe.wait_ge(tok_ready, 1)
                    gather(pe, 0)
                    rounds(pe, expert_tensor, lambda: first_unit(pe))

                @block.scalar
                def _(act):
                    for i, (t0, n) in enumerate(TILES):
                        nc.scalar.activation(resid[0:n, i, :], htok[0:n, i, :], ACT.Copy, scale=ALPHA)
                    for i, (t0, n) in enumerate(TILES):
                        nc.scalar.activation(htokh[0:n, i, :], htok[0:n, i, :], ACT.Copy).then_inc(stream_done, 1)
                    act.wait_ge(rt_top, 1)
                    nc.scalar.activation(rw[:, :, 1:2], rw[:, :, 0:1], ACT.Exp).then_inc(rt_exp, 1)
                    gathered_high(act, 0)
                    rounds(act, expert_scalar, lambda: None)

                @block.vector
                def _(dve):
                    c = chain(dve, "dve")
                    V = nc.vector
                    c.link(V.memset(rlog, 0.0))
                    dve.wait_ge(rt_done, 1)
                    for i, (t0, n) in enumerate(TILES):
                        ins = V.tensor_copy(rlog[0:n, i, :], ps[0][0:n, NE * i:NE * i + NE])
                    c.link(ins)
                    for i in range(NT):
                        c(V.max(rtop[:, i, :], rlog[:, i, :]))
                    c.sync()
                    for i in range(NT):
                        c(V.max_index(ridx[:, i, :].bitcast(U32), rtop[:, i, :], rlog[:, i, :]))
                    c.sync()
                    V.tensor_tensor(rw[:, :, 0:1], rtop[:, :, 1:2], rtop[:, :, 0:1], ALU.subtract).then_inc(rt_top, 1)
                    c.link(V.tensor_copy(rtop[:, :, 2:4], ridx[:, :, 0:2].bitcast(U32)))
                    dve.wait_ge(rt_exp, 1)
                    c.link(V.tensor_scalar(rw[:, :, 2:3], rw[:, :, 1:2], 1.0, None, ALU.add))
                    c.link(V.reciprocal(rw[:, :, 2:3], rw[:, :, 2:3]))
                    c.link(V.tensor_tensor(rw[:, :, 3:4], rw[:, :, 2:3], rw[:, :, 1:2], ALU.mult))
                    each = lambda x: x.to_broadcast([P, NT, NE])
                    for q in range(2):
                        c(V.tensor_tensor(rsel[:, :, NE * q:NE * q + NE], iota[:, 0:NE].unsqueeze(1).to_broadcast([P, NT, NE]),
                                          each(rtop[:, :, 2 + q:3 + q]), ALU.is_equal))
                    c.sync()
                    c(V.tensor_tensor(gate, rsel[:, :, 0:NE], each(rw[:, :, 2:3]), ALU.mult))
                    c(V.tensor_tensor(gate2, rsel[:, :, NE:2 * NE], each(rw[:, :, 3:4]), ALU.mult))
                    ins = V.tensor_tensor(selm, rsel[:, :, 0:NE], rsel[:, :, NE:2 * NE], ALU.add)
                    ins.then_inc(sel_ready, 1)
                    c.sync()
                    c(V.tensor_tensor(gate, gate, gate2, ALU.add))
                    c.link(V.memset(posr, -1.0))
                    dve.wait_ge(pos_done, 1)
                    c.link(V.tensor_reduce(cmx[:, 0:1], ps[1][:, 32:32 + NE], AX.X, ALU.max))
                    c.link(V.tensor_scalar(cmx[:, 1:2], cmx[:, 0:1], float(CAP), None, ALU.is_gt))
                    V.tensor_copy(iu[:, 0:1], cmx[:, 1:2]).then_inc(flag_ready, 1)
                    for i, (t0, n) in enumerate(TILES):
                        c(V.scalar_tensor_tensor(out=posr[0:n, i, 0:NE], in0=ps[1][0:n, NE * i:NE * i + NE], scalar=1.0,
                                                 in1=selm[0:n, i, :], op0=ALU.add, op1=ALU.mult))
                    c.sync()
                    c.link(V.tensor_scalar(posr[:, :, 0:NE], posr[:, :, 0:NE], -1.0, None, ALU.add))
                    for r in range(1, ROUNDS):
                        c(V.tensor_scalar(posr[:, :, NE * r:NE * r + NE], posr[:, :, 0:NE], -float(CAP * r), None, ALU.add))
                    c.sync()
                    V.memset(cmx[:, 0:1], 0.0).then_inc(sc_added, 1)
                    V.memset(cnt, 0.0).then_inc(pos_ready, 1)
                    onehot(0)
                    for i, (t0, n) in enumerate(TILES):
                        dve.wait_ge(stream_done, 2 * DEPTH - 1 + i + 1)
                        ins = V.tensor_tensor(htokl[0:n, i, :], htok[0:n, i, :], htokh[0:n, i, :].bitcast(F32), ALU.subtract)
                    ins.then_inc(tok_ready, 1)
                    gathered_low(dve, 0)
                    keep(c, "dve")
                    rounds(dve, expert_vector, lambda: None)

        norm(0, 0, A["ln_in_g"], A["ln_in_b"])
        calls = 1
        for l in range(DEPTH):
            if upto < 10 * l + 1:
                return
            project(l)
            attend(l)
            delta(l)
            if upto < 10 * l + 2:
                return
            merge(l)
            norm(calls, 1 + 2 * l, A["ln1_g"][l], A["ln1_b"][l], htok if l == 1 else None,
                 split_next=first["mlp", 0] if l == 0 else moe0)
            if upto < 10 * l + 3:
                return
            dense_mlp() if l == 0 else moe()
            norm(calls + 1, 2 + 2 * l, A["ln2_g"][l], A["ln2_b"][l], final=(l == DEPTH - 1))
            calls += 2


_SHAPES = {
    "y_prompt": (1, SEQ, D), "y_sample": (1, DEC, D),
    "new_k_p": (DEPTH, 1, SEQ, A_KV, HD), "new_v_p": (DEPTH, 1, SEQ, A_KV, HD), "new_idx_k_p": (DEPTH, 1, SEQ, HD),
    "new_conv_p": (DEPTH, 1, CW - 1, CCH), "new_gdn_p": (DEPTH, 1, B_HEADS, BD, BD),
    "new_k_s": (DEPTH, 1, DEC, A_KV, HD), "new_v_s": (DEPTH, 1, DEC, A_KV, HD), "new_idx_k_s": (DEPTH, 1, DEC, HD),
    "new_conv_s": (DEPTH, 1, CW - 1, CCH), "new_gdn_s": (DEPTH, 1, B_HEADS, BD, BD),
}


_INS = ["x_prompt", "x_sample", "cache_k", "cache_v", "cache_idx_k", "state_conv", "state_gdn", "ln_in_g", "ln_in_b",
        "w_in", "conv_w", "a_log", "dt_bias", "gnorm_g", "w_oa", "w_ob", "w_out", "ln1_g", "ln1_b", "ln2_g", "ln2_b",
        "ffn_w1", "ffn_w3", "ffn_w2", "moe_router", "moe_w1", "moe_w3", "moe_w2"]


def kernel(**inputs):
    import numpy as np
    import concourse.bacc as bacc
    from concourse.bass_utils import run_bass_kernel_spmd

    nc = bacc.Bacc("TRN2", target_bir_lowering=False, num_devices=1)
    arrays, A, OUT = {}, {}, {}
    for name in _INS:
        a = np.ascontiguousarray(inputs[name])
        arrays[f"in_{name}"] = a
        A[name] = nc.dram_tensor(f"in_{name}", a.shape, mybir.dt.from_np(a.dtype), kind="ExternalInput").ap()
    for name, shape in _SHAPES.items():
        OUT[name] = nc.dram_tensor(f"out_{name}", shape, F32, kind="ExternalOutput").ap()
    program(nc, A, OUT)
    r = run_bass_kernel_spmd(nc, [arrays], core_ids=[0])
    return tuple(r.results[0][f"out_{name}"] for name in _SHAPES)
```
